# Optimizing a Trainium2 kernel written in Bass

```python
import math
import jax, jax.numpy as jnp
from jax import lax
import numpy as np

D_MODEL = 1024
BATCH = 1
SEQ = 1024
DEPTH = 1
DEC_BATCH = 1
DEC_SEQ = 32
PAST_LEN = 1024

CHUNK = 64
HA = 8
DKA = 128
DVA = 128
CONV_W = 4
QK_A = HA * DKA
VA = HA * DVA
C_CONV = 2 * QK_A + VA
HB = 8
DHB = 64
WB = HB * DHB
BAND_CHUNKS = 8
BAND_PAST = BAND_CHUNKS * CHUNK
REL_MIN = -(CHUNK - 1)
REL_MAX = 128
N_REL = REL_MAX - REL_MIN + 1
O_Z = C_CONV
O_B = O_Z + VA
O_A = O_B + HA
O_QKV_B = O_A + HA
O_GATE = O_QKV_B + 3 * WB
N_IN = O_GATE + 2 * D_MODEL
N_GROUPS = 4
EXP_PER_GROUP = 4
N_EXPERTS = N_GROUPS * EXP_PER_GROUP
D_EXPERT = 256
TOP_K = 2
ALPHA = (2 * DEPTH) ** 0.25
BETA_INIT = (8 * DEPTH) ** -0.25
LN_EPS = 1e-5
RMS_EPS = 1e-6

kernel_name = 'hybrid_streaming_encoder_step'

def layer_norm(x, g, b):
    xf = x.astype(jnp.float32)
    mu = jnp.mean(xf, -1, keepdims=True)
    var = jnp.mean(jnp.square(xf - mu), -1, keepdims=True)
    return ((xf - mu) * lax.rsqrt(var + LN_EPS)).astype(x.dtype) * g + b

def l2norm(x):
    return x * lax.rsqrt(jnp.sum(x * x, -1, keepdims=True) + 1e-6)

def causal_conv(u, state, w):
    T = u.shape[1]
    full = jnp.concatenate([state.astype(u.dtype), u], axis=1)
    out = full[:, 0:T] * w[0]
    for i in range(1, CONV_W):
        out = out + full[:, i:i + T] * w[i]
    return out, full[:, T:]

def gated_delta_rule(q, k, v, g, beta, s0):
    Bn, T, H, DK = q.shape
    DV = v.shape[-1]
    L = CHUNK if T % CHUNK == 0 else T
    N = T // L

    def blk(a):
        a = a.reshape((Bn, N, L, H) + a.shape[3:])
        return jnp.moveaxis(a, (1, 3), (0, 2))

    qc, kc, vc, gc, bc = blk(q), blk(k), blk(v), blk(g), blk(beta)
    G = jnp.cumsum(gc, axis=-1)
    idx = jnp.arange(L)
    causal = idx[:, None] >= idx[None, :]
    strict = idx[:, None] > idx[None, :]
    decay_in = jnp.exp(jnp.where(causal, G[..., :, None] - G[..., None, :], -jnp.inf))
    kk = jnp.einsum('nbhid,nbhjd->nbhij', kc, kc)
    M = jnp.where(strict, bc[..., :, None] * kk * decay_in, 0.0)
    eye = jnp.eye(L, dtype=jnp.float32)
    rhs = jnp.concatenate([bc[..., None] * vc, (bc * jnp.exp(G))[..., None] * kc], axis=-1)
    sol = lax.linalg.triangular_solve(M + eye, rhs, left_side=True, lower=True)
    u_v, w_k = sol[..., :DV], sol[..., DV:]
    qk = jnp.einsum('nbhid,nbhjd->nbhij', qc, kc) * decay_in
    q_dec = qc * jnp.exp(G)[..., None]
    k_dec = kc * jnp.exp(G[..., -1:] - G)[..., None]
    g_last = jnp.exp(G[..., -1])

    def step(S, xs):
        u_v_n, w_k_n, qk_n, q_dec_n, k_dec_n, g_last_n = xs
        u = u_v_n - jnp.einsum('bhld,bhdv->bhlv', w_k_n, S)
        o = jnp.einsum('bhld,bhdv->bhlv', q_dec_n, S) + jnp.einsum('bhij,bhjv->bhiv', qk_n, u)
        S = S * g_last_n[..., None, None] + jnp.einsum('bhld,bhlv->bhdv', k_dec_n, u)
        return S, o

    s_fin, o = lax.scan(step, s0, (u_v, w_k, qk, q_dec, k_dec, g_last))
    o = jnp.moveaxis(o, (0, 2), (1, 3)).reshape(Bn, T, H, DV)
    return o, s_fin

def gdn_mixer(u, z, b_raw, a_raw, conv_state, s0, conv_w, a_log, dt_bias, norm_w):
    Bn, T, _ = u.shape
    c_out, new_conv = causal_conv(u, conv_state, conv_w)
    act = jax.nn.silu(c_out.astype(jnp.float32))
    q = l2norm(act[..., :QK_A].reshape(Bn, T, HA, DKA)) * (DKA ** -0.5)
    k = l2norm(act[..., QK_A:2 * QK_A].reshape(Bn, T, HA, DKA))
    v = act[..., 2 * QK_A:].reshape(Bn, T, HA, DVA)
    beta = jax.nn.sigmoid(b_raw.astype(jnp.float32))
    g = -jnp.exp(a_log.astype(jnp.float32)) * jax.nn.softplus(a_raw.astype(jnp.float32) + dt_bias.astype(jnp.float32))
    o, s_new = gated_delta_rule(q, k, v, g, beta, s0.astype(jnp.float32))
    o = o * lax.rsqrt(jnp.mean(o * o, -1, keepdims=True) + RMS_EPS) * norm_w.astype(jnp.float32)
    o = o * jax.nn.silu(z.astype(jnp.float32)).reshape(Bn, T, HA, DVA)
    return o.reshape(Bn, T, VA).astype(u.dtype), new_conv, s_new

def rel_bias_matrix(rel_bias, dist):
    idx = jnp.clip(dist, REL_MIN, REL_MAX) - REL_MIN
    return rel_bias[:, idx].astype(jnp.float32)

def band_attention_prompt(q, k, v, rel_bias):
    Bn, T, H, Dh = q.shape
    NC = T // CHUNK
    band = (BAND_CHUNKS + 1) * CHUNK
    qc = q.reshape(Bn, NC, CHUNK, H, Dh)
    pad = jnp.zeros((Bn, BAND_PAST, H, Dh), k.dtype)
    kp = jnp.concatenate([pad, k], 1).reshape(Bn, NC + BAND_CHUNKS, CHUNK, H, Dh)
    vp = jnp.concatenate([pad, v], 1).reshape(Bn, NC + BAND_CHUNKS, CHUNK, H, Dh)
    kb = jnp.concatenate([kp[:, s:s + NC] for s in range(BAND_CHUNKS + 1)], axis=2)
    vb = jnp.concatenate([vp[:, s:s + NC] for s in range(BAND_CHUNKS + 1)], axis=2)
    qi = jnp.arange(CHUNK)
    kj = jnp.arange(band)
    bias = rel_bias_matrix(rel_bias, BAND_PAST + qi[:, None] - kj[None, :])
    valid = (jnp.arange(NC)[:, None] * CHUNK - BAND_PAST + kj[None, :]) >= 0
    s = jnp.einsum('bnqhd,bnkhd->bnhqk', qc, kb).astype(jnp.float32) * (Dh ** -0.5) + bias[None, None]
    s = jnp.where(valid[None, :, None, None, :], s, -jnp.inf)
    p = jax.nn.softmax(s, axis=-1).astype(v.dtype)
    o = jnp.einsum('bnhqk,bnkhd->bnqhd', p, vb)
    return o.reshape(Bn, T, H * Dh)

def band_attention_sample(q, k, v, cache_k, cache_v, rel_bias):
    Bn, Tn, H, Dh = q.shape
    P = cache_k.shape[1]
    kf = jnp.concatenate([cache_k.astype(k.dtype), k], 1)
    vf = jnp.concatenate([cache_v.astype(v.dtype), v], 1)
    bias = rel_bias_matrix(rel_bias, P + jnp.arange(Tn)[:, None] - jnp.arange(P + Tn)[None, :])
    s = jnp.einsum('bqhd,bkhd->bhqk', q, kf).astype(jnp.float32) * (Dh ** -0.5) + bias[None]
    p = jax.nn.softmax(s, axis=-1).astype(v.dtype)
    o = jnp.einsum('bhqk,bkhd->bqhd', p, vf)
    return o.reshape(Bn, Tn, H * Dh)

def hier_moe(h, w_rg, b_rg, w_re, b_re, w_gate_e, w_up_e, w_down_e):
    shp = h.shape
    t = h.reshape(-1, shp[-1])
    pg = jax.nn.softmax((t @ w_rg + b_rg).astype(jnp.float32), axis=-1)
    p_grp, grp = lax.top_k(pg, 1)
    le = (t @ w_re + b_re).astype(jnp.float32).reshape(-1, N_GROUPS, EXP_PER_GROUP)
    le = jnp.einsum('ng,nge->ne', jax.nn.one_hot(grp[:, 0], N_GROUPS, dtype=jnp.float32), le)
    pe_top, e_loc = lax.top_k(jax.nn.softmax(le, axis=-1), TOP_K)
    w = p_grp * pe_top / jnp.sum(pe_top, -1, keepdims=True)
    e_glob = grp * EXP_PER_GROUP + e_loc
    gates = jnp.sum(jax.nn.one_hot(e_glob, N_EXPERTS, dtype=jnp.float32) * w[..., None], axis=1)
    hg = jnp.einsum('nd,edf->nef', t, w_gate_e)
    hu = jnp.einsum('nd,edf->nef', t, w_up_e)
    act = jax.nn.silu(hg) * hu * gates[..., None].astype(t.dtype)
    return jnp.einsum('nef,efd->nd', act, w_down_e).reshape(shp)

def trunk_layer(x, c, conv_state, gdn_state, cache_k, cache_v,
                w_mod, b_mod, w_in, conv_w, a_log, dt_bias, gdn_norm_w, rel_bias,
                w_up_a, w_up_b, w_out, ln1_g, ln1_b,
                w_rg, b_rg, w_re, b_re, w_gate_e, w_up_e, w_down_e, ln2_g, ln2_b):
    Bn, T, _ = x.shape
    mod = jax.nn.silu(c) @ w_mod + b_mod
    sh1, sc1, gt1, sh2, sc2, gt2 = [m[:, None, :] for m in jnp.split(mod, 6, axis=-1)]
    h = x * (1 + sc1) + sh1
    proj = h @ w_in
    u_a = proj[..., :C_CONV]
    z_a = proj[..., O_Z:O_B]
    b_a = proj[..., O_B:O_A]
    a_a = proj[..., O_A:O_QKV_B]
    qkv_b = proj[..., O_QKV_B:O_GATE]
    g_a = proj[..., O_GATE:O_GATE + D_MODEL]
    g_b = proj[..., O_GATE + D_MODEL:]
    y_a, new_conv, new_s = gdn_mixer(u_a, z_a, b_a, a_a, conv_state, gdn_state, conv_w, a_log, dt_bias, gdn_norm_w)
    qb, kb, vb = [t.reshape(Bn, T, HB, DHB) for t in jnp.split(qkv_b, 3, axis=-1)]
    if cache_k is None:
        y_b = band_attention_prompt(qb, kb, vb, rel_bias)
        keep = min(BAND_PAST, T)
        k_rows, v_rows = kb[:, T - keep:], vb[:, T - keep:]
    else:
        y_b = band_attention_sample(qb, kb, vb, cache_k, cache_v, rel_bias)
        k_rows, v_rows = kb, vb
    mix = jax.nn.sigmoid(g_a) * (y_a @ w_up_a) + jax.nn.sigmoid(g_b) * (y_b @ w_up_b)
    x = layer_norm(ALPHA * x + (1 + gt1) * (mix @ w_out), ln1_g, ln1_b)
    h2 = x * (1 + sc2) + sh2
    ffn = hier_moe(h2, w_rg, b_rg, w_re, b_re, w_gate_e, w_up_e, w_down_e)
    x = layer_norm(ALPHA * x + (1 + gt2) * ffn, ln2_g, ln2_b)
    return x, new_conv, new_s, k_rows, v_rows

def setup_inputs(seed: int = 0) -> dict:
    key = jax.random.key(seed)
    ks = list(jax.random.split(key, 40))
    f32 = jnp.float32

    def nrm(i, shape, scale):
        return jax.random.normal(ks[i], shape, f32) * scale

    P_B = min(BAND_PAST, PAST_LEN)
    D = D_MODEL
    dt = jnp.exp(jax.random.uniform(ks[14], (DEPTH, HA), f32) * (math.log(0.1) - math.log(0.001)) + math.log(0.001))
    return {
        'x_prompt': nrm(0, (BATCH, SEQ, D), 1.0),
        'x_sample': nrm(1, (DEC_BATCH, DEC_SEQ, D), 1.0),
        'c_prompt': nrm(2, (BATCH, D), 1.0),
        'c_sample': nrm(3, (DEC_BATCH, D), 1.0),
        'state_conv_a': nrm(4, (DEPTH, DEC_BATCH, CONV_W - 1, C_CONV), 1.0),
        'state_gdn': nrm(5, (DEPTH, DEC_BATCH, HA, DKA, DVA), DKA ** -0.5),
        'cache_k_b': nrm(6, (DEPTH, DEC_BATCH, P_B, HB, DHB), 1.0),
        'cache_v_b': nrm(7, (DEPTH, DEC_BATCH, P_B, HB, DHB), 1.0),
        'ln_in_g': 1.0 + nrm(8, (D,), 0.02),
        'ln_in_b': nrm(9, (D,), 0.02),
        'w_mod': nrm(10, (DEPTH, D, 6 * D), 0.1 * D ** -0.5),
        'b_mod': nrm(11, (DEPTH, 6 * D), 0.01),
        'w_in': nrm(12, (DEPTH, D, N_IN), D ** -0.5),
        'conv_w': nrm(13, (DEPTH, CONV_W, C_CONV), CONV_W ** -0.5),
        'a_log': jnp.log(jax.random.uniform(ks[15], (DEPTH, HA), f32, 1.0, 16.0)),
        'dt_bias': dt + jnp.log(-jnp.expm1(-dt)),
        'gdn_norm_w': 1.0 + nrm(16, (DEPTH, DVA), 0.02),
        'rel_bias': nrm(17, (DEPTH, HB, N_REL), 0.5),
        'w_up_a': nrm(18, (DEPTH, VA, D), VA ** -0.5),
        'w_up_b': nrm(19, (DEPTH, WB, D), WB ** -0.5),
        'w_out': nrm(20, (DEPTH, D, D), BETA_INIT * D ** -0.5),
        'ln1_g': 1.0 + nrm(21, (DEPTH, D), 0.02),
        'ln1_b': nrm(22, (DEPTH, D), 0.02),
        'w_rg': nrm(23, (DEPTH, D, N_GROUPS), D ** -0.5),
        'b_rg': nrm(24, (DEPTH, N_GROUPS), 0.01),
        'w_re': nrm(25, (DEPTH, D, N_EXPERTS), D ** -0.5),
        'b_re': nrm(26, (DEPTH, N_EXPERTS), 0.01),
        'w_gate_e': nrm(27, (DEPTH, N_EXPERTS, D, D_EXPERT), D ** -0.5),
        'w_up_e': nrm(28, (DEPTH, N_EXPERTS, D, D_EXPERT), D ** -0.5),
        'w_down_e': nrm(29, (DEPTH, N_EXPERTS, D_EXPERT, D), BETA_INIT * D_EXPERT ** -0.5),
        'ln2_g': 1.0 + nrm(30, (DEPTH, D), 0.02),
        'ln2_b': nrm(31, (DEPTH, D), 0.02),
    }

def reference(x_prompt, x_sample, c_prompt, c_sample, state_conv_a, state_gdn, cache_k_b, cache_v_b,
              ln_in_g, ln_in_b, w_mod, b_mod, w_in, conv_w, a_log, dt_bias, gdn_norm_w, rel_bias,
              w_up_a, w_up_b, w_out, ln1_g, ln1_b, w_rg, b_rg, w_re, b_re,
              w_gate_e, w_up_e, w_down_e, ln2_g, ln2_b):
    xp = layer_norm(x_prompt, ln_in_g, ln_in_b)
    xs = layer_norm(x_sample, ln_in_g, ln_in_b)
    conv_p, conv_s, gdn_p, gdn_s, kb_p, kb_s, vb_p, vb_s = [], [], [], [], [], [], [], []
    for l in range(DEPTH):
        lw = (w_mod[l], b_mod[l], w_in[l], conv_w[l], a_log[l], dt_bias[l], gdn_norm_w[l], rel_bias[l],
              w_up_a[l], w_up_b[l], w_out[l], ln1_g[l], ln1_b[l],
              w_rg[l], b_rg[l], w_re[l], b_re[l], w_gate_e[l], w_up_e[l], w_down_e[l], ln2_g[l], ln2_b[l])
        conv0 = jnp.zeros((xp.shape[0], CONV_W - 1, C_CONV), xp.dtype)
        s0 = jnp.zeros((xp.shape[0], HA, DKA, DVA), jnp.float32)
        xp, cp, sp, kp, vp = trunk_layer(xp, c_prompt, conv0, s0, None, None, *lw)
        xs, cs, ss, ksm, vsm = trunk_layer(xs, c_sample, state_conv_a[l], state_gdn[l], cache_k_b[l], cache_v_b[l], *lw)
        conv_p.append(cp)
        conv_s.append(cs)
        gdn_p.append(sp)
        gdn_s.append(ss)
        kb_p.append(kp)
        kb_s.append(ksm)
        vb_p.append(vp)
        vb_s.append(vsm)
    return (xp, xs, jnp.stack(conv_p), jnp.stack(conv_s), jnp.stack(gdn_p), jnp.stack(gdn_s),
            jnp.stack(kb_p), jnp.stack(kb_s), jnp.stack(vb_p), jnp.stack(vb_s))


_drawn_inputs = setup_inputs


def setup_inputs(seed=0):
    import zlib

    import numpy as np

    out = dict(_drawn_inputs(seed))
    spreads = {}
    factors = {'cache_k_b': 3.554,
     'gdn_norm_w': 21.717,
     'rel_bias': 4.023,
     'b_rg': 21.983,
     'b_re': 36.947,
     'ln2_g': 7.646,
     'ln2_b': 8.011}
    for name, (base, spread) in spreads.items():
        noise = np.random.default_rng([zlib.crc32(name.encode()), seed]).standard_normal(out[name].shape)
        drawn = base * np.exp(spread * noise) if base else spread * noise
        out[name] = __import__('jax').numpy.asarray(drawn.astype(out[name].dtype))
    for name, factor in factors.items():
        out[name] = (out[name] * factor).astype(out[name].dtype)
    return out
```

```python
from contextlib import ExitStack

import numpy as np

import concourse.bass as bass
from concourse import mybir

F32 = mybir.dt.float32
ALU = mybir.AluOpType
ACT = mybir.ActivationFunctionType
AX = mybir.AxisListType

P = 128
D = 1024
KD = D // P
PR = 1024
SR = 32
ROWS = PR + SR
TILES = PR // P + 1
PAD = TILES * P
NJ = 3
NW = ROWS // NJ
PIN = PR - 2 * NW
HA = 8
CH = 64
CW = 4
RAW = PR + SR + 2 * (CW - 1)
SOFF = PR + 2 * (CW - 1)
CONVW = RAW - (CW - 1)
SCONV = PR + CW - 1
HB = 8
DHB = 64
PAIRS = HB // 2
BAND = 512
KT = BAND // P + 1
NREL = 192
NE = 16
NG = 4
DE = 256
ALPHA = 2.0 ** 0.25
LN_EPS = 1e-5
RMS_EPS = 1e-6
L2_EPS = 1e-6

C_ID, C_CUM, C_ONE, C_NEG, C_M16, C_MOFF, C_CH0, C_CH1, C_BLK, C_VAL = range(10)
NCONST = 10

Q_G, Q_CUM, Q_NBETA, Q_BETA, Q_BEG, Q_KD, Q_GL0, Q_GL1 = range(8)
NQ = 8


def rows_of(t):
    return P if t < TILES - 1 else SR


class Chain:

    def __init__(self, eng, sem, base=0):
        self.eng, self.sem, self.base, self.n = eng, sem, base, 0

    def mark(self, ins):
        ins.then_inc(self.sem, 1)
        self.n += 1

    def wait(self, n=None):
        self.eng.wait_ge(self.sem, self.base + (self.n if n is None else n))

    def link(self, ins):
        self.mark(ins)
        self.wait()


def flat2(ap):
    return ap.rearrange("p a b -> p (a b)")


class Core:

    def __init__(self, nc, ctx, dram):
        self.nc, self.ctx, self.d = nc, ctx, dram

    def sem(self, name):
        return self.ctx.enter_context(self.nc.semaphore(name))


def sb(nc, ctx, name, shape):
    return ctx.enter_context(nc.sbuf_tensor(name, shape, F32))


def phase_modulation(nc, c):
    d = c.d
    HALF = 512
    NCHK = 6 * D // HALF
    with ExitStack() as ctx:
        wm = [sb(nc, ctx, f"wm{i}", [P, KD, HALF]) for i in range(2)]
        cT = sb(nc, ctx, "cT", [P, KD, 2])
        sc = sb(nc, ctx, "silu_c", [P, KD, 2])
        bm = sb(nc, ctx, "bm", [P, 6 * KD])
        al = sb(nc, ctx, "al", [P, 2, HA])
        gr = sb(nc, ctx, "gate_cols", [P, 2, 2, KD])
        grT = sb(nc, ctx, "gate_rows", [4 * KD, P])
        ps = ctx.enter_context(nc.psum_tensor("ps_mod", [P, 512], F32))
        psT = ctx.enter_context(nc.psum_tensor("ps_gate", [P, 512], F32))
        small_in, silu_done, w_in, w_used = c.sem("m_small"), c.sem("m_silu"), [c.sem("m_w0"), c.sem("m_w1")], c.sem("m_used")
        mod_dve, gates_cols, gates_T, gates_sb, gates_out = c.sem("m_dve"), c.sem("m_gc"), c.sem("m_gT"), c.sem("m_gsb"), c.sem("m_go")
        nega_done = c.sem("m_nega")
        with nc.Block() as block:
            @block.sync
            def _(sp):
                sp.dma_start(cT[:, :, :], d["cT"]).then_inc(small_in, 16)
                sp.dma_start(c.consts[:, :, :], d["consts"]).then_inc(small_in, 16)
                sp.dma_start(bm[:, :], d["b_mod"]).then_inc(small_in, 16)
                sp.dma_start(al[:, :, :], d["a_dt"].unsqueeze(0).to_broadcast([P, 2, HA])).then_inc(small_in, 16)
                for i in range(2):
                    sp.dma_start(wm[i][:, :, :], d["w_mod"][i]).then_inc(w_in[i], 16)
                with sp.Fori(1, NCHK // 2) as n:
                    for i in range(2):
                        sp.wait_ge(w_used, 2 * n + i - 1)
                        sp.dma_start(wm[i][:, :, :],
                                     d["w_mod"][bass.ds(2 * n + i, 1)].rearrange("a p k c -> p (a k) c")).then_inc(w_in[i], 16)
                sp.wait_ge(gates_sb, 1)
                sp.dma_start(d["gate_rows"], grT[:, :]).then_inc(gates_out, 16)
                sp.wait_ge(gates_out, 16)

            @block.scalar
            def _(act):
                act.wait_ge(small_in, 64)
                act.activation(sc[:, :, :], cT[:, :, :], ACT.Silu).then_inc(silu_done, 1)
                act.activation(c.adt[:, 0, :], al[:, 0, :], ACT.Exp).then_inc(nega_done, 1)

            @block.tensor
            def _(pe):
                pe.wait_ge(silu_done, 1)

                def chunk(n, i):
                    for m in range(HALF // P):
                        for k in range(KD):
                            mm = pe.matmul(ps[:, bass.ds((n * 2 + i) * 8 + 2 * m, 2)],
                                           wm[i][:, k, m * P:(m + 1) * P], sc[:, k, :],
                                           start=(k == 0), stop=(k == KD - 1))
                    mm.then_inc(w_used, 1)

                with pe.Fori(0, NCHK // 2) as n:
                    for i in range(2):
                        pe.wait_ge(w_in[i], 16 * n + 16)
                        chunk(n, i)
                pe.wait_ge(gates_cols, 2)
                pe.transpose(psT[0:4 * KD, 0:P], gr[:, :, :, :].rearrange("p a b k -> p (a b k)"),
                             c.consts[:, C_ID, :]).then_inc(gates_T, 1)

            @block.vector
            def _(dve):
                st = Chain(dve, mod_dve)
                st.mark(dve.memset(c.one[:, :], 1.0))
                dve.wait_ge(small_in, 64)
                dve.wait_ge(nega_done, 1)
                st.mark(dve.tensor_scalar(c.adt[:, 0, :], c.adt[:, 0, :], -1.0, None, ALU.mult))
                st.mark(dve.tensor_copy(c.adt[:, 1, :], al[:, 1, :]))
                dve.wait_ge(w_used, NCHK)
                st.link(dve.tensor_tensor(c.mod[:, :, :],
                                          ps[:, 0:12 * KD].rearrange("p (m s) -> p m s", s=2),
                                          bm[:, :].unsqueeze(2).to_broadcast([P, 6 * KD, 2]), ALU.add))
                for sec in (1, 2, 4, 5):
                    v = c.mod[:, sec * KD:(sec + 1) * KD, :]
                    st.mark(dve.tensor_scalar(v, v, 1.0, None, ALU.add))
                st.wait()
                for g, sec in enumerate((2, 5)):
                    dve.tensor_copy(gr[:, g, :, :],
                                    c.mod[:, sec * KD:(sec + 1) * KD, :].rearrange("p k s -> p s k")).then_inc(gates_cols, 1)
                dve.wait_ge(gates_T, 1)
                dve.tensor_copy(grT[:, :], psT[0:4 * KD, 0:P]).then_inc(gates_sb, 1)


def ln_stats(st, x, rows, stats, mv):
    half = D // 2
    for i in range(2):
        st.mark(st.eng.bn_stats(stats[0:rows, i * 6:i * 6 + 6], x[0:rows, i * half:(i + 1) * half]))
    st.wait()
    st.link(st.eng.bn_aggr(mv[0:rows, :], stats[0:rows, :]))


def phase_trunk_norm(nc, c):
    d = c.d
    NX = 3
    with ExitStack() as ctx:
        x = [sb(nc, ctx, f"x{i}", [P, D]) for i in range(NX)]
        lng = sb(nc, ctx, "lng", [P, D])
        lnb = sb(nc, ctx, "lnb", [P, D])
        wba = sb(nc, ctx, "wba", [P, KD, 2 * HA])
        stats = sb(nc, ctx, "stats", [P, 12])
        mv = sb(nc, ctx, "mv", [P, TILES, 2])
        std = sb(nc, ctx, "std", [P, TILES])
        rstd = sb(nc, ctx, "rstd", [P, TILES])
        ba = sb(nc, ctx, "ba", [P, TILES, 2 * HA])
        y = sb(nc, ctx, "y", [P, 4, TILES, HA])
        gv = sb(nc, ctx, "gv", [P, TILES, HA])
        eps = sb(nc, ctx, "eps", [P, 1])
        ps = [ctx.enter_context(nc.psum_tensor(f"psx{i}", [P, KD, P], F32)) for i in range(2)]
        psb = ctx.enter_context(nc.psum_tensor("psba", [P, 512], F32))
        psg = ctx.enter_context(nc.psum_tensor("psg", [P, 512], F32))
        x_in = [c.sem(f"n_xin{i}") for i in range(NX)]
        small, stat_done, std_done, x0_done, xT = (c.sem("n_" + n) for n in ("small", "stat", "std", "x0", "xT"))
        x0_out = [c.sem(f"n_x0out{i}") for i in range(NX)]
        hT_act, hT_dve, dchain, ba_mm, ba_sb = (c.sem("n_" + n) for n in ("hTa", "hTd", "chain", "bamm", "basb"))
        sig_in, sig, g_ready, cum_ready, e_in, e_done, acts = (c.sem("n_" + n) for n in
                                                               ("sigin", "sig", "g", "cum", "ein", "e", "acts"))
        with nc.Block() as block:
            @block.sync
            def _(sp):
                sp.dma_start(lng[:, :], d["ln_in_g"].partition_broadcast(P)).then_inc(small, 16)
                sp.dma_start(lnb[:, :], d["ln_in_b"].partition_broadcast(P)).then_inc(small, 16)
                sp.dma_start(wba[:, :, :], d["w_ba"]).then_inc(small, 16)
                for t in range(TILES + 1):
                    if t < TILES:
                        if t >= NX:
                            sp.wait_ge(x0_out[t % NX], 16 * (t // NX))
                            sp.wait_ge(xT, t - NX + 1)
                        sp.dma_start(x[t % NX][0:rows_of(t), :], d["x"][t * P:t * P + rows_of(t), :]).then_inc(x_in[t % NX], 16)
                    if t >= 1:
                        sp.wait_ge(x0_done, t)
                        sp.dma_start(d["x0"][(t - 1) * P:(t - 1) * P + rows_of(t - 1), :],
                                     x[(t - 1) % NX][0:rows_of(t - 1), :]).then_inc(x0_out[(t - 1) % NX], 16)
                for q in x0_out:
                    sp.wait_ge(q, 16 * TILES // NX)

            @block.scalar
            def _(act):
                for t in range(TILES + 1):
                    if t < TILES:
                        act.wait_ge(stat_done, t + 1)
                        act.activation(std[0:rows_of(t), t:t + 1], mv[0:rows_of(t), t, 1:2], ACT.Sqrt,
                                       bias=eps[0:rows_of(t), :]).then_inc(std_done, 1)
                    if t >= 1:
                        u = t - 1
                        s = 0 if u < TILES - 1 else 1
                        act.wait_ge(xT, u + 1)
                        for k in range(KD // 2):
                            a = act.activation(c.hT[:, k, u * P:u * P + rows_of(u)], ps[u % 2][:, k, 0:rows_of(u)],
                                               ACT.Identity, bias=c.mod[:, 0 * KD + k, s:s + 1],
                                               scale=c.mod[:, 1 * KD + k, s:s + 1])
                        a.then_inc(hT_act, 1)
                act.wait_ge(sig_in, 1)
                act.activation(y[:, 0, :, :], ba[:, :, 0:HA], ACT.Sigmoid).then_inc(sig, 1)
                act.activation(y[:, 2, :, :], y[:, 2, :, :], ACT.Exp, scale=-1.0).then_inc(acts, 1)
                act.wait_ge(acts, 1)
                act.activation(y[:, 2, :, :], y[:, 2, :, :], ACT.Ln, bias=c.one[:, :]).then_inc(sig, 1)
                act.wait_ge(e_in, 1)
                act.activation(y[:, 0, :, :], y[:, 0, :, :], ACT.Exp).then_inc(e_done, 1)
                act.activation(y[:, 1, :, :], y[:, 1, :, :], ACT.Exp).then_inc(e_done, 1)
                for r in range(2):
                    act.activation(y[:, 2 + r, :, :],
                                   psg[:, (2 + r) * TILES * HA:(3 + r) * TILES * HA].rearrange("p (t h) -> p t h", h=HA),
                                   ACT.Exp).then_inc(e_done, 1)

            @block.tensor
            def _(pe):
                for t in range(TILES):
                    rows = rows_of(t)
                    pe.wait_ge(x0_done, t + 1)
                    if t >= 2:
                        pe.wait_ge(hT_act, t - 1)
                        pe.wait_ge(hT_dve, t - 1)
                    for k in range(KD):
                        tr = pe.transpose(ps[t % 2][:, k, 0:rows], x[t % NX][0:rows, k * P:(k + 1) * P],
                                          c.consts[0:rows, C_ID, 0:rows])
                    tr.then_inc(xT, 1)
                pe.wait_ge(small, 48)
                pe.wait_ge(hT_act, TILES)
                pe.wait_ge(hT_dve, TILES)
                for t in range(TILES):
                    rows = rows_of(t)
                    for k in range(KD):
                        mm = pe.matmul(psb[0:rows, t * 2 * HA:(t + 1) * 2 * HA], c.hT[:, k, t * P:t * P + rows],
                                       wba[:, k, :], start=(k == 0), stop=(k == KD - 1))
                mm.then_inc(ba_mm, 1)
                pe.wait_ge(g_ready, 1)
                for i, m in enumerate((C_CUM, C_BLK, C_CH0, C_CH1)):
                    mm = pe.matmul(psg[:, i * TILES * HA:(i + 1) * TILES * HA], c.consts[:, m, :],
                                   gv[:, :, :].rearrange("p t h -> p (t h)"), start=True, stop=True)
                mm.then_inc(cum_ready, 1)

            @block.vector
            def _(dve):
                st = Chain(dve, dchain)
                st.mark(dve.memset(eps[:, :], LN_EPS))
                st.link(dve.memset(ba[:, :, :], 0.0))
                dve.wait_ge(small, 48)
                for t in range(TILES + 1):
                    if t < TILES:
                        dve.wait_ge(x_in[t % NX], 16 * (t // NX + 1))
                        ln_stats(st, x[t % NX], rows_of(t), stats, mv[:, t, :])
                        dve.tensor_copy(rstd[0:rows_of(t), t:t + 1], mv[0:rows_of(t), t, 0:1]).then_inc(stat_done, 1)
                        dve.wait_ge(std_done, t + 1)
                        dve.wait_ge(stat_done, t + 1)
                        r, xt = rows_of(t), x[t % NX]
                        st.link(dve.reciprocal(rstd[0:r, t:t + 1], std[0:r, t:t + 1]))
                        st.link(dve.tensor_scalar(xt[0:r, :], xt[0:r, :], mv[0:r, t, 0:1], rstd[0:r, t:t + 1],
                                                  ALU.subtract, ALU.mult))
                        st.link(dve.tensor_tensor(xt[0:r, :], xt[0:r, :], lng[0:r, :], ALU.mult))
                        dve.tensor_tensor(xt[0:r, :], xt[0:r, :], lnb[0:r, :], ALU.add).then_inc(x0_done, 1)
                    if t >= 1:
                        u = t - 1
                        s = 0 if u < TILES - 1 else 1
                        dve.wait_ge(xT, u + 1)
                        for k in range(KD // 2, KD):
                            a = dve.tensor_scalar(c.hT[:, k, u * P:u * P + rows_of(u)], ps[u % 2][:, k, 0:rows_of(u)],
                                                  c.mod[:, 1 * KD + k, s:s + 1], c.mod[:, 0 * KD + k, s:s + 1],
                                                  ALU.mult, ALU.add)
                        a.then_inc(hT_dve, 1)
                dve.wait_ge(ba_mm, 1)
                st.mark(dve.tensor_copy(ba[:, 0:TILES - 1, :],
                                        psb[:, 0:(TILES - 1) * 2 * HA].rearrange("p (t c) -> p t c", c=2 * HA)))
                st.link(dve.tensor_copy(ba[0:SR, TILES - 1, :], psb[0:SR, (TILES - 1) * 2 * HA:TILES * 2 * HA]))
                st.link(dve.tensor_tensor(y[:, 1, :, :], ba[:, :, HA:2 * HA],
                                          c.adt[:, 1, :].unsqueeze(1).to_broadcast([P, TILES, HA]), ALU.add))
                st.link(dve.tensor_scalar(y[:, 3, :, :], y[:, 1, :, :], 0.0, None, ALU.max))
                dve.scalar_tensor_tensor(out=flat2(y[:, 2, :, :]), in0=flat2(y[:, 3, :, :]), scalar=2.0,
                                         in1=flat2(y[:, 1, :, :]), op0=ALU.mult, op1=ALU.subtract).then_inc(sig_in, 1)
                dve.wait_ge(sig, 2)
                st.wait()
                valid = c.consts[:, C_VAL, 0:TILES].unsqueeze(2).to_broadcast([P, TILES, HA])
                tok = [c.tok[:, :, q, :].rearrange("p h t -> p t h") for q in range(NQ)]
                st.mark(dve.tensor_tensor(tok[Q_BETA], y[:, 0, :, :], valid, ALU.mult))
                st.link(dve.tensor_tensor(y[:, 1, :, :], y[:, 2, :, :], y[:, 3, :, :], ALU.add))
                st.link(dve.tensor_tensor(y[:, 1, :, :], y[:, 1, :, :],
                                          c.adt[:, 0, :].unsqueeze(1).to_broadcast([P, TILES, HA]), ALU.mult))
                dve.tensor_tensor(gv[:, :, :], y[:, 1, :, :], valid, ALU.mult).then_inc(g_ready, 1)
                st.mark(dve.tensor_scalar(tok[Q_NBETA], tok[Q_BETA], -1.0, None, ALU.mult))
                dve.wait_ge(cum_ready, 1)
                dve.wait_ge(g_ready, 1)
                st.mark(dve.tensor_copy(tok[Q_G], gv[:, :, :]))
                n = TILES * HA
                pg = [psg[:, i * n:(i + 1) * n].rearrange("p (t h) -> p t h", h=HA) for i in range(2)]
                st.mark(dve.tensor_copy(tok[Q_CUM], pg[0]))
                st.link(dve.tensor_copy(y[:, 0, :, :], pg[0]))
                dve.tensor_tensor(y[:, 1, :, :], pg[1], y[:, 0, :, :], ALU.subtract).then_inc(e_in, 1)
                dve.wait_ge(e_done, 4)
                st.mark(dve.tensor_tensor(tok[Q_BEG], tok[Q_BETA], y[:, 0, :, :], ALU.mult))
                st.mark(dve.tensor_copy(tok[Q_KD], y[:, 1, :, :]))
                st.mark(dve.tensor_copy(tok[Q_GL0], y[:, 2, :, :]))
                st.link(dve.tensor_copy(tok[Q_GL1], y[:, 3, :, :]))


def phase_deltanet(nc, c):
    d = c.d
    G3 = 3
    NGRP = TILES // G3
    W3 = G3 * P
    JOBS = 4 * NJ
    NCHUNK = 2 * (TILES - 1) + 1
    with ExitStack() as ctx:
        def buf(name, shape):
            return sb(nc, ctx, name, shape)
        w = [buf(f"w{i}", [P, KD, P]) for i in range(4)]
        cw = buf("cw", [P, HA, 3, CW])
        nw = buf("nw", [P, 1])
        cst = buf("cst", [P, HA, 3, CW - 1])
        raw = [buf(f"raw{i}", [P, RAW]) for i in range(3)]
        rawz = buf("rawz", [P, ROWS])
        cv = [buf(f"cv{i}", [P, CONVW]) for i in range(2)]
        f = [buf(f"f{i}", [P, PAD]) for i in range(3)]
        rinv = buf("rinv", [P, ROWS])
        sq = buf("sq", [P, ROWS])
        cwh = buf("cwh", [P, 3, CW])
        zs = buf("zs", [P, ROWS])
        yat = buf("yat", [P, ROWS])
        hq = buf("hq", [P, NQ, TILES])
        Dm, Eq, ET, A0, A0T, A1, A1T, Q, nN, kd = (buf(n, [P, PAD]) for n in
                                                  ("Dm", "Eq", "ET", "A0", "A0T", "A1", "A1T", "Q", "nN", "kd"))
        kb, bv, WKT, UV, PT = ET, nN, Q, A1, A1T
        obuf = buf("obuf", [P, TILES, P])
        S = [buf(f"S{i}", [P, P]) for i in range(2)]
        Ssam = buf("Ssam", [P, 2, P])
        u = buf("u", [P, 2, P])
        ssq = buf("ssq", [P, 3, TILES])
        eps = buf("epsl", [P, 4])
        bank = [ctx.enter_context(nc.psum_tensor(f"bk{i}", [P, 512], F32)) for i in range(8)]
        pj, stg, aux, obank = bank[0:2], bank[2:5], bank[5:8], (bank[7], bank[2])

        s = {n: c.sem("g_" + n) for n in (
            "w0", "w1", "w2", "w3", "st_in", "s_free", "yat_free", "init", "tail_out",
            "pj_ready", "pj_taken", "raw_used", "z_used", "hq", "gb", "conv", "actv", "sq", "ss", "lnr",
            "rn", "qn", "zn", "st_ready", "st_dve", "st_act", "st_pool", "qd",
            "chain", "wk_ready", "wk_taken", "ws", "u", "ds", "S", "o", "o_taken", "son", "ssq", "rms",
            "on")}

        def psv(b):
            return b[:, 0:W3].rearrange("p (t n) -> p t n", n=P)

        def grp(m, g):
            return m[:, g * W3:(g + 1) * W3]

        def grp3(m, g):
            return grp(m, g).rearrange("p (t n) -> p t n", n=P)

        (G_ROW, KK, T_ET, T_A, A2, A2T, T_K, Q1, A4, A4T, Q2, A8, RT, BT, B, T_V, R, B2, W, TT, QK,
         T_O) = range(22)
        STAGES = 22

        def st_base(h):
            return STAGES * NGRP * h + NGRP

        with nc.Block() as block:
            @block.sync
            def _(sp):
                for dst, src in ((cw, d["conv_w"]), (cst, d["conv_state"])):
                    sp.dma_start(dst[:, :, :, :], src).then_inc(s["s_free"], 16)
                sp.dma_start(nw[:, :], d["norm_w"]).then_inc(s["yat_free"], 16)

                def weights(h, b):
                    src = d["w_gdn"][h, b] if isinstance(h, int) else \
                        d["w_gdn"][bass.ds(h, 1), b].rearrange("a p k c -> p (a k) c")
                    sp.dma_start(w[b][:, :, :], src).then_inc(s[f"w{b}"], 16)

                def head(ap, h):
                    return ap[h] if isinstance(h, int) else ap[bass.ds(h, 1)].rearrange("a p c -> (a p) c")

                def state(h):
                    sp.dma_start(Ssam[:, 0, :], head(d["state"], h)).then_inc(s["st_in"], 16)

                def outputs(h):
                    sp.wait_ge(s["S"], (NCHUNK + 1) * h + NCHUNK)
                    sp.dma_start(head(d["gdn_p"], h), S[0][:, :]).then_inc(s["s_free"], 16)
                    sp.wait_ge(s["S"], (NCHUNK + 1) * h + NCHUNK + 1)
                    sp.dma_start(head(d["gdn_s"], h), Ssam[:, 1, :]).then_inc(s["s_free"], 16)

                def gated(h):
                    sp.wait_ge(s["st_dve"], st_base(h + 1))
                    sp.dma_start(head(d["ya"], h), yat[:, :]).then_inc(s["yat_free"], 16)

                for b in range(4):
                    weights(0, b)
                state(0)
                for b in range(4):
                    sp.wait_ge(s["pj_ready"], NJ * (b + 1))
                    weights(1, b)
                with sp.Fori(0, HA - 2) as h:
                    for b in range(4):
                        sp.wait_ge(s["pj_ready"], JOBS * (h + 1) + NJ * (b + 1))
                        weights(h + 2, b)
                    outputs(h)
                    state(h + 1)
                    gated(h)
                outputs(HA - 2)
                state(HA - 1)
                gated(HA - 2)
                outputs(HA - 1)
                gated(HA - 1)
                sp.wait_ge(s["raw_used"], 3 * HA)
                sp.dma_start(d["tail"], c.tail[:, :, :, :]).then_inc(s["tail_out"], 16)
                sp.wait_ge(s["s_free"], 32 * (HA + 1))
                sp.wait_ge(s["yat_free"], 16 * (HA + 1))
                sp.wait_ge(s["tail_out"], 16)

            @block.scalar
            def _(act):
                def take(hh, n):
                    b, j = n // NJ, n % NJ
                    act.wait_ge(s["pj_ready"], JOBS * hh + n + 1)
                    if j == 0 and not isinstance(hh, int) or j == 0 and hh > 0:
                        if b < 3:
                            act.wait_ge(s["raw_used"], 3 * (hh - 1) + b + 1)
                        else:
                            act.wait_ge(s["z_used"], hh)
                    src = pj[n % 2]
                    if b == 3:
                        a = act.activation(rawz[:, j * NW:(j + 1) * NW], src[:, 0:NW], ACT.Copy)
                    elif j < 2:
                        a = act.activation(raw[b][:, CW - 1 + j * NW:CW - 1 + (j + 1) * NW], src[:, 0:NW], ACT.Copy)
                    else:
                        act.activation(raw[b][:, SOFF:SOFF + SR], src[:, PIN:NW], ACT.Copy)
                        a = act.activation(raw[b][:, CW - 1 + 2 * NW:CW - 1 + PR], src[:, 0:PIN], ACT.Copy)
                    a.then_inc(s["pj_taken"], 1)

                def head(h, last):
                    act.wait_ge(s["pj_taken"], JOBS * (h + 1) + 2)
                    act.wait_ge(s["st_dve"], st_base(h))
                    act.activation(zs[:, :], rawz[:, :], ACT.Silu).then_inc(s["z_used"], 1)
                    for b in range(3):
                        act.wait_ge(s["conv"], 3 * h + b + 1)
                        act.activation(f[b][:, 0:PR], cv[b % 2][:, 0:PR], ACT.Silu)
                        act.activation(f[b][:, PR:ROWS], cv[b % 2][:, SCONV:SCONV + SR],
                                       ACT.Silu).then_inc(s["actv"], 1)
                        if not last:
                            take(h + 1, 2 * b)
                            take(h + 1, 2 * b + 1)
                    for b in range(2):
                        if b == 1:
                            act.wait_ge(s["qn"], 2 * h + 1)
                        for j in range(NJ):
                            act.wait_ge(s["ss"], 2 * NJ * h + b * NJ + j + 1)
                            act.activation(rinv[:, j * NW:(j + 1) * NW], aux[j][:, 0:NW], ACT.Ln,
                                           bias=eps[:, 0:1]).then_inc(s["lnr"], 1)
                        act.wait_ge(s["lnr"], 2 * NJ * h + (b + 1) * NJ)
                        act.activation(rinv[:, :], rinv[:, :], ACT.Exp, scale=-0.5,
                                       bias=eps[:, 1 + 2 * b:2 + 2 * b]).then_inc(s["rn"], 1)
                    for g in range(NGRP):
                        act.wait_ge(s["st_ready"], STAGES * NGRP * h + g + 1)
                        act.activation(grp(Eq, g), stg[g][:, 0:W3], ACT.Exp).then_inc(s["st_act"], 1)
                    for g in range(NGRP):
                        act.wait_ge(s["st_dve"], st_base(h) + g + 1)
                        act.activation(grp(Dm, g), grp(Dm, g), ACT.Exp).then_inc(s["st_act"], 1)
                    if not last:
                        for n in range(6, 9):
                            take(h + 1, n)
                    for i in range(2 * NGRP):
                        g = i // 2
                        act.wait_ge(s["wk_ready"], 2 * NGRP * h + i + 1)
                        act.activation(grp((WKT, UV)[i % 2], g), aux[i % 2][:, 0:W3],
                                       ACT.Copy).then_inc(s["wk_taken"], 1)
                    for t in range(TILES):
                        r = rows_of(t)
                        act.wait_ge(s["o"], TILES * h + t + 1)
                        act.activation(obuf[0:r, t, :], obank[t % 2][0:r, 0:P], ACT.Copy).then_inc(s["o_taken"], 1)
                        if not last and t in (2, 4, 6):
                            take(h + 1, 9 + (t - 2) // 2)
                    act.wait_ge(s["ssq"], h + 1)
                    act.activation(ssq[:, 1, :], ssq[:, 0, :], ACT.Ln, scale=1.0 / P,
                                   bias=eps[:, 2:3]).then_inc(s["son"], 1)
                    act.wait_ge(s["son"], h + 1)
                    act.activation(ssq[:, 2, :], ssq[:, 1, :], ACT.Exp, scale=-0.5).then_inc(s["rms"], 1)

                act.wait_ge(s["init"], 1)
                for n in range(JOBS):
                    take(0, n)
                act.wait_ge(s["init"], 2)
                with act.Fori(0, HA - 1) as h:
                    head(h, False)
                head(HA - 1, True)

            @block.gpsimd
            def _(pool):
                def head(h):
                    pool.wait_ge(s["hq"], h + 1)
                    pool.tensor_tensor(Q[:, :].rearrange("p (t n) -> p t n", n=P),
                                       c.consts[:, C_ONE, :].unsqueeze(1).to_broadcast([P, TILES, P]),
                                       hq[:, Q_G, :].unsqueeze(2).to_broadcast([P, TILES, P]),
                                       ALU.mult).then_inc(s["gb"], 1)
                    pool.wait_ge(s["z_used"], h + 1)
                    pool.tensor_tensor(zs[:, :], zs[:, :], nw[:, 0:1].to_broadcast([P, ROWS]), ALU.mult).then_inc(s["zn"], 1)
                    for b in range(2):
                        pool.wait_ge(s["actv"], 3 * h + b + 1)
                        if b == 1:
                            pool.wait_ge(s["ss"], 2 * NJ * h + NJ)
                        pool.tensor_tensor(sq[:, :], f[b][:, 0:ROWS], f[b][:, 0:ROWS], ALU.mult).then_inc(s["sq"], 1)
                    pool.wait_ge(s["qn"], 2 * h + 1)
                    for g in range(NGRP):
                        pool.wait_ge(s["st_act"], 2 * NGRP * h + g + 1)
                        pool.tensor_tensor(grp(Eq, g), grp(Eq, g), grp(f[0], g), ALU.mult).then_inc(s["qd"], 1)
                    eye = c.consts[:, C_ID, :].unsqueeze(1).to_broadcast([P, G3, P])
                    for dst, src, stage in ((Q, A0T, T_A), (A1T, A0T, BT)):
                        for g in range(NGRP):
                            pool.wait_ge(s["st_dve"], st_base(h) + NGRP * stage + g + 1)
                            pool.tensor_tensor(grp3(dst, g), grp3(src, g), eye, ALU.add).then_inc(s["st_pool"], 1)

                pool.wait_ge(s["yat_free"], 16)
                with pool.Fori(0, HA) as h:
                    head(h)

            @block.tensor
            def _(pe):
                def product(hh, n):
                    b, j = n // NJ, n % NJ
                    if j == 0:
                        pe.wait_ge(s[f"w{b}"], 16 * (hh + 1))
                    pe.wait_ge(s["pj_taken"], JOBS * hh + n + 1)
                    for k in range(KD):
                        mm = pe.matmul(pj[n % 2][:, 0:NW], w[b][:, k, :], c.hT[:, k, j * NW:(j + 1) * NW],
                                       start=(k == 0), stop=(k == KD - 1))
                        if k == KD - 1:
                            mm.then_inc(s["pj_ready"], 1)
                        yield

                def products(hh, jobs):
                    for n in jobs:
                        yield from product(hh, n)

                def head(h, last):
                    fill = products(h + 1, () if last else range(JOBS))

                    def step(n):
                        for _ in range(n):
                            next(fill, None)

                    def stage(n, mms):
                        for g in range(NGRP):
                            pe.wait_ge(s["st_dve"], st_base(h) + NGRP * (n - 1) + g + 1)
                            for t in range(G3 * g, G3 * g + G3):
                                mm = mms(t, stg[g][:, (t - G3 * g) * P:(t - G3 * g + 1) * P])
                            mm.then_inc(s["st_ready"], 1)

                    def tl(m, t):
                        return m[:, t * P:(t + 1) * P]

                    def mul(lhsT, rhs):
                        return lambda t, out: pe.matmul(out, tl(lhsT, t), tl(rhs, t), start=True, stop=True)

                    def turn(m):
                        return lambda t, out: pe.transpose(out, tl(m, t), c.consts[:, C_ID, :])

                    step(6 * KD)
                    for b in range(2):
                        pe.wait_ge(s["sq"], 2 * h + b + 1)
                        for j in range(NJ):
                            if b == 1:
                                pe.wait_ge(s["lnr"], 2 * NJ * h + j + 1)
                            pe.matmul(aux[j][:, 0:NW], c.consts[:, C_ONE, :], sq[:, j * NW:(j + 1) * NW],
                                      start=True, stop=True).then_inc(s["ss"], 1)
                        step(KD)
                    pe.wait_ge(s["gb"], h + 1)
                    stage(G_ROW, lambda t, out: pe.matmul(out, tl(Q, t), c.consts[:, C_CUM, :], start=True, stop=True))
                    pe.wait_ge(s["qn"], 2 * h + 2)
                    stage(KK, mul(f[1], f[1]))
                    stage(T_ET, turn(ET))
                    step(2)
                    stage(T_A, turn(A0))
                    step(2)
                    stage(A2, mul(A0T, A0))
                    stage(A2T, mul(A0, A0T))
                    stage(T_K, turn(f[1]))
                    step(2)
                    pe.wait_ge(s["st_pool"], 2 * NGRP * h + NGRP)
                    stage(Q1, mul(A1, Q))
                    stage(A4, mul(A1T, A1))
                    stage(A4T, mul(A1, A1T))
                    stage(Q2, mul(A0, Q))
                    stage(A8, mul(A0T, A0))
                    step(2)
                    stage(RT, mul(A1, Q))
                    step(2)
                    stage(BT, mul(nN, Q))
                    stage(B, mul(Q, nN))
                    pe.wait_ge(s["actv"], 3 * h + 3)
                    stage(T_V, turn(f[2]))
                    stage(R, turn(Q))
                    stage(B2, mul(A0T, A0))
                    step(2)
                    pe.wait_ge(s["st_pool"], 2 * NGRP * h + 2 * NGRP)
                    stage(W, mul(A0, A1T))
                    step(2)
                    stage(TT, mul(A1, A1T))
                    step(2)
                    for i in range(2 * NGRP):
                        g = i // 2
                        pe.wait_ge(s["st_dve"], st_base(h) + NGRP * TT + g + 1)
                        if i >= 2:
                            pe.wait_ge(s["wk_taken"], 2 * NGRP * h + i - 1)
                        for t in range(G3 * g, G3 * g + G3):
                            lhsT, rhs = ((kb, A0T), (A0T, bv))[i % 2]
                            mm = pe.matmul(aux[i % 2][:, (t - G3 * g) * P:(t - G3 * g + 1) * P],
                                           tl(lhsT, t), tl(rhs, t), start=True, stop=True)
                        mm.then_inc(s["wk_ready"], 1)
                    stage(QK, mul(f[1], f[0]))
                    pe.wait_ge(s["qd"], NGRP * h + NGRP)
                    pe.wait_ge(s["wk_taken"], 2 * NGRP * (h + 1))
                    pe.wait_ge(s["st_dve"], st_base(h) + NGRP * QK + NGRP)
                    for n in range(NCHUNK):
                        t, r = n // 2, n % 2
                        lo, hi = r * CH, r * CH + CH
                        if n < NCHUNK - 1:
                            Sn = S[n % 2][:, :]
                            pe.wait_ge(s["S"], (NCHUNK + 1) * h + n + 1)
                        else:
                            Sn = Ssam[:, 0, :]
                            pe.wait_ge(s["st_in"], 16 * (h + 1))
                            pe.wait_ge(s["u"], NCHUNK * h + n)
                        pe.matmul(aux[0][lo:hi, 0:P], WKT[:, t * P + lo:t * P + hi], Sn,
                                  start=True, stop=True).then_inc(s["ws"], 1)
                        if r == 0:
                            pe.wait_ge(s["o_taken"], TILES * h + t + 1)
                        pe.matmul(obank[t % 2][lo:hi, 0:P], Eq[:, t * P + lo:t * P + hi], Sn,
                                  start=True, stop=False)
                        if n < NCHUNK - 1:
                            step(1)
                        pe.wait_ge(s["u"], NCHUNK * h + n + 1)
                        if n == NCHUNK - 1:
                            pe.wait_ge(s["S"], (NCHUNK + 1) * h + n + 1)
                        pe.matmul(aux[1][:, 0:P], kd[lo:hi, t * P:(t + 1) * P], u[lo:hi, t % 2, :],
                                  start=True, stop=True).then_inc(s["ds"], 1)
                        mm = pe.matmul(obank[t % 2][lo:hi, 0:P], PT[lo:hi, t * P + lo:t * P + hi],
                                       u[lo:hi, t % 2, :], start=False, stop=True)
                        if r == 1 or n == NCHUNK - 1:
                            mm.then_inc(s["o"], 1)
                    step(JOBS * KD)
                    pe.wait_ge(s["on"], h + 1)
                    stage(T_O, lambda t, out: pe.transpose(out[:, 0:rows_of(t)], obuf[0:rows_of(t), t, :],
                                                           c.consts[0:rows_of(t), C_ID, 0:rows_of(t)]))

                pe.wait_ge(s["init"], 1)
                for _ in products(0, range(JOBS)):
                    pass
                with pe.Fori(0, HA - 1) as h:
                    head(h, False)
                head(HA - 1, True)

            @block.vector
            def _(dve):
                PER = 14

                def head(h):
                    st = Chain(dve, s["chain"], PER * h + 8)
                    st.mark(dve.tensor_copy(cwh[:, :, :], cw[:, bass.ds(h, 1), :, :].rearrange("p a b i -> p (a b) i")))
                    for b in range(3):
                        st.mark(dve.tensor_copy(raw[b][:, SOFF - CW + 1:SOFF], cst[:, bass.ds(h, 1), b, :].rearrange("p a i -> p (a i)")))
                    dve.tensor_copy(hq[:, :, :], c.tok[:, bass.ds(h, 1), :, :].rearrange("p a q t -> p (a q) t")).then_inc(s["hq"], 1)
                    st.wait()
                    for b in range(3):
                        dve.wait_ge(s["pj_taken"], JOBS * h + NJ * (b + 1) + 2)
                        if b == 2:
                            dve.wait_ge(s["actv"], 3 * h + 1)
                        cvb = cv[b % 2][:, :]
                        st.link(dve.tensor_scalar(cvb, raw[b][:, 0:CONVW], cwh[:, b, 0:1], None, ALU.mult))
                        for k in range(1, CW):
                            ins = dve.scalar_tensor_tensor(out=cvb, in0=raw[b][:, k:k + CONVW],
                                                           scalar=cwh[:, b, k:k + 1], in1=cvb,
                                                           op0=ALU.mult, op1=ALU.add)
                            if k < CW - 1:
                                st.link(ins)
                            else:
                                ins.then_inc(s["conv"], 1)
                        dve.tensor_copy(c.tail[:, bass.ds(h, 1), b, 0:3].rearrange("p a i -> p (a i)"), raw[b][:, PR:PR + 3])
                        dve.tensor_copy(c.tail[:, bass.ds(h, 1), b, 3:6].rearrange("p a i -> p (a i)"),
                                        raw[b][:, RAW - 3:RAW]).then_inc(s["raw_used"], 1)
                    for b in range(2):
                        dve.wait_ge(s["rn"], 2 * h + b + 1)
                        dve.tensor_tensor(f[b][:, 0:ROWS], f[b][:, 0:ROWS], rinv[:, :], ALU.mult).then_inc(s["qn"], 1)

                    def ready(n, g):
                        dve.wait_ge(s["st_ready"], STAGES * NGRP * h + NGRP * n + g + 1)

                    def take(n, op):
                        for g in range(NGRP):
                            ready(n, g)
                            op(g).then_inc(s["st_dve"], 1)

                    def copy(m):
                        return lambda g: dve.tensor_copy(grp(m, g), stg[g][:, 0:W3])

                    def add(m):
                        return lambda g: dve.tensor_tensor(grp(m, g), stg[g][:, 0:W3], grp(m, g), ALU.add)

                    def tiles(g):
                        return [(t, stg[g][:, (t - G3 * g) * P:(t - G3 * g + 1) * P]) for t in range(G3 * g, G3 * g + G3)]

                    def scaled(m, q):
                        return lambda g: dve.tensor_tensor(
                            grp3(m, g), psv(stg[g]), hq[:, q, G3 * g:G3 * g + G3].unsqueeze(2).to_broadcast([P, G3, P]),
                            ALU.mult)

                    def decay(g):
                        dve.wait_ge(s["st_act"], 2 * NGRP * h + g + 1)
                        for t, ps in tiles(g):
                            ins = dve.scalar_tensor_tensor(out=Dm[:, t * P:(t + 1) * P], in0=ps,
                                                           scalar=hq[:, Q_CUM, t:t + 1], in1=c.consts[:, C_NEG, :],
                                                           op0=ALU.subtract, op1=ALU.min)
                        return ins

                    def kk(g):
                        dve.wait_ge(s["st_act"], 2 * NGRP * h + NGRP + g + 1)
                        return dve.tensor_tensor(grp(ET, g), stg[g][:, 0:W3], grp(Dm, g), ALU.mult)

                    def split(g):
                        for t, ps in tiles(g):
                            for m, mask in ((A0, C_M16), (nN, C_MOFF)):
                                ins = dve.scalar_tensor_tensor(out=m[:, t * P:(t + 1) * P], in0=ps,
                                                               scalar=hq[:, Q_NBETA, t:t + 1], in1=c.consts[:, mask, :],
                                                               op0=ALU.mult, op1=ALU.mult)
                        return ins

                    def keys(g):
                        scaled(kb, Q_BEG)(g)
                        return scaled(kd, Q_KD)(g)

                    take(G_ROW, decay)
                    take(KK, kk)
                    take(T_ET, split)
                    take(T_A, copy(A0T))
                    take(A2, copy(A1))
                    take(A2T, copy(A1T))
                    take(T_K, keys)
                    take(Q1, add(Q))
                    take(A4, copy(A0))
                    take(A4T, copy(A0T))
                    take(Q2, add(Q))
                    take(A8, copy(A1))
                    take(RT, add(Q))
                    take(BT, copy(A0T))
                    take(B, copy(A0))
                    take(T_V, scaled(bv, Q_BETA))
                    take(R, copy(A1))
                    take(B2, copy(A0))
                    take(W, add(A1T))
                    take(TT, copy(A0T))
                    take(QK, lambda g: dve.tensor_tensor(grp(PT, g), stg[g][:, 0:W3], grp(Dm, g), ALU.mult))
                    dve.wait_ge(s["s_free"], 32 * (h + 1))
                    dve.memset(S[0][:, :], 0.0).then_inc(s["S"], 1)
                    dve.wait_ge(s["wk_taken"], 2 * NGRP * (h + 1))
                    for n in range(NCHUNK):
                        t, r = n // 2, n % 2
                        lo, hi = r * CH, r * CH + CH
                        dve.wait_ge(s["ws"], NCHUNK * h + n + 1)
                        dve.tensor_tensor(u[lo:hi, t % 2, :], UV[lo:hi, t * P:(t + 1) * P], aux[0][lo:hi, 0:P],
                                          ALU.subtract).then_inc(s["u"], 1)
                        dve.wait_ge(s["ds"], NCHUNK * h + n + 1)
                        old, new = (S[n % 2][:, :], S[(n + 1) % 2][:, :]) if n < NCHUNK - 1 else (Ssam[:, 0, :], Ssam[:, 1, :])
                        dve.scalar_tensor_tensor(out=new, in0=old, scalar=hq[:, Q_GL0 + r, t:t + 1], in1=aux[1][:, 0:P],
                                                 op0=ALU.mult, op1=ALU.add).then_inc(s["S"], 1)
                    dve.wait_ge(s["o_taken"], TILES * (h + 1) + 2)
                    osq = Dm[:, :].rearrange("p (t n) -> p t n", n=P)
                    st.link(dve.tensor_tensor(osq, obuf[:, :, :], obuf[:, :, :], ALU.mult))
                    dve.tensor_reduce(ssq[:, 0, :], osq, AX.X, ALU.add).then_inc(s["ssq"], 1)
                    dve.wait_ge(s["rms"], h + 1)
                    dve.tensor_tensor(obuf[:, :, :], obuf[:, :, :],
                                      ssq[:, 2, :].unsqueeze(2).to_broadcast([P, TILES, P]), ALU.mult).then_inc(s["on"], 1)
                    dve.wait_ge(s["zn"], h + 1)
                    dve.wait_ge(s["yat_free"], 16 * (h + 1))
                    for g in range(NGRP):
                        ready(T_O, g)
                        lo, hi = g * W3, min((g + 1) * W3, ROWS)
                        dve.tensor_tensor(yat[:, lo:hi], stg[g][:, 0:hi - lo], zs[:, lo:hi],
                                          ALU.mult).then_inc(s["st_dve"], 1)
                    assert st.n == PER, st.n

                st = Chain(dve, s["chain"])
                for b in range(3):
                    st.mark(dve.memset(raw[b][:, 0:CW - 1], 0.0))
                    st.mark(dve.memset(f[b][:, ROWS:PAD], 0.0))
                st.mark(dve.memset(obuf[:, :, :], 0.0))
                st.link(dve.memset(eps[:, 3:4], 0.0))
                dve.memset(eps[:, 0:1], L2_EPS)
                dve.memset(eps[:, 1:2], float(-0.5 * np.log(P))).then_inc(s["init"], 1)
                dve.memset(eps[:, 2:3], RMS_EPS).then_inc(s["init"], 1)
                for i, (sem, n) in enumerate(((s["pj_taken"], 2), (s["st_dve"], NGRP), (s["o_taken"], 2))):
                    dve.memset(ssq[:, 0, i:i + 1], 0.0).then_inc(sem, n)
                dve.wait_ge(s["s_free"], 32)
                with dve.Fori(0, HA) as h:
                    head(h)


def phase_attention(nc, c):
    d = c.d
    W = KT * P
    UNITS = 2 * TILES
    JOBS = 3 * NJ
    TAB = c.d["table"].shape[1]
    FIRST = P - CH
    NKS = BAND + SR
    SCALE = float(DHB) ** -0.5
    with ExitStack() as ctx:
        def buf(name, shape):
            return sb(nc, ctx, name, shape)
        w = [buf(f"wa{i}", [P, KD, P]) for i in range(3)]
        qT, kT = buf("qT", [P, PAD]), buf("kT", [P, ROWS])
        v = buf("v", [P, TILES, P])
        kc, vc = buf("kc", [P, BAND]), buf("vc", [P, BAND // P, P])
        bias, brev = buf("bias", [P, 2, W]), buf("brev", [P, 2, W])
        x = [buf(f"sx{i}", [P, W]) for i in range(2)]
        pr = [buf(f"pr{i}", [P, W]) for i in range(2)]
        pt = [buf(f"pt{i}", [P, W]) for i in range(2)]
        osb = [buf(f"osb{i}", [P, P]) for i in range(2)]
        yb = buf("yb", [P, ROWS])
        tab, tab8 = buf("tab", [HB, NREL]), buf("tab8", [HB, TAB])
        waits = buf("waits", [P, 1])
        num = buf("num", [P, 4, 4])
        sc = [ctx.enter_context(nc.psum_tensor(f"sc{i}", [P, 1024], F32)) for i in range(2)]
        pst = ctx.enter_context(nc.psum_tensor("pst", [P, 1024], F32))
        pso = ctx.enter_context(nc.psum_tensor("pso", [P, 512], F32))
        psy = ctx.enter_context(nc.psum_tensor("psy", [P, 512], F32))
        s = {n: c.sem("a_" + n) for n in (
            "w0", "w1", "w2", "tab", "tab8", "tab_out", "toep", "bias", "masked", "cache", "yb_free", "kv_out",
            "pj_ready", "pj_taken", "sc_ready", "x_ready", "p_ready", "pt_ready", "pt_taken", "pv_ready",
            "o_taken", "oT_ready", "y_taken", "chain", "init")}

        def keys(t):
            if t == TILES - 1:
                return 0, KT, NKS
            first = max(0, t - KT + 1)
            return first, t - first + 1, (t - first + 1) * P

        def bcol(t):
            return 0 if t == TILES - 1 else (KT - keys(t)[1]) * P

        with nc.Block() as block:
            @block.sync
            def _(sp):
                sp.dma_start(tab[:, :], d["rel_bias"]).then_inc(s["tab"], 16)
                for b in range(3):
                    sp.dma_start(w[b][:, :, :], d["w_att"][0, b]).then_inc(s[f"w{b}"], 16)
                sp.dma_start(yb[:, 0:KD], d["x"][0:P, 0:KD]).then_inc(s["yb_free"], 16)
                sp.dma_start(kT[:, 0:KD], d["x"][0:P, 0:KD]).then_inc(s["kv_out"], 16)
                sp.wait_ge(s["tab8"], 4)
                sp.dma_start(d["table"], tab8[:, :]).then_inc(s["tab_out"], 16)
                sp.wait_ge(s["tab_out"], 16)
                for h in range(HB):
                    row = d["table"][h, 0:W]
                    src = bass.AP(row.tensor, row.offset, [[1, P], [1, W]])
                    sp.dma_start(d["toeplitz"][h], src).then_inc(s["toep"], 16)
                sp.wait_ge(s["toep"], 16 * HB)

                def load(p):
                    i = bass.ds(p, 1)
                    for e in range(2):
                        sp.dma_start(brev[:, e, :], d["toeplitz"][bass.ds(2 * p + e, 1)].rearrange("a p c -> (a p) c")).then_inc(s["bias"], 16)
                    sp.dma_start(kc[:, :], d["k_cache"][i].rearrange("a p c -> (a p) c")).then_inc(s["cache"], 16)
                    sp.dma_start(vc[:, :, :], d["v_cache"][i].rearrange("a p t c -> p (a t) c")).then_inc(s["cache"], 16)

                def weights(p):
                    for b in range(3):
                        sp.wait_ge(s["pj_ready"], JOBS * p + NJ * (b + 1))
                        sp.dma_start(w[b][:, :, :], d["w_att"][bass.ds(p + 1, 1), b].rearrange("a p k c -> p (a k) c")).then_inc(s[f"w{b}"], 16)

                def outputs(p):
                    i = bass.ds(p, 1)
                    sp.wait_ge(s["pj_taken"], JOBS * (p + 1) + 2)
                    sp.dma_start(d["kb_p"][i].rearrange("a p c -> (a p) c"), kT[:, PR - BAND:PR]).then_inc(s["kv_out"], 16)
                    sp.dma_start(d["kb_s"][i].rearrange("a p c -> (a p) c"), kT[:, PR:ROWS]).then_inc(s["kv_out"], 16)
                    nt = (PR - BAND) // P
                    sp.dma_start(d["vb_p"][i].rearrange("a p t c -> p (a t) c"), v[:, nt:TILES - 1, :]).then_inc(s["kv_out"], 16)
                    sp.dma_start(d["vb_s"][i].rearrange("a p c -> (a p) c"), v[0:SR, TILES - 1, :]).then_inc(s["kv_out"], 16)
                    sp.wait_ge(s["y_taken"], TILES * (p + 1) + 1)
                    sp.dma_start(d["yb"][i].rearrange("a p c -> (a p) c"), yb[:, :]).then_inc(s["yb_free"], 16)

                with sp.Fori(0, PAIRS - 1) as p:
                    load(p)
                    weights(p)
                    outputs(p)
                load(PAIRS - 1)
                outputs(PAIRS - 1)
                sp.wait_ge(s["kv_out"], 64 * PAIRS + 16)
                sp.wait_ge(s["yb_free"], 16 * (PAIRS + 1))

            @block.scalar
            def _(act):
                def pair(p):
                    act.wait_ge(s["y_taken"], TILES * p + 1)
                    act.wait_ge(s["kv_out"], 64 * p + 16)
                    for n in range(JOBS):
                        b, j = n // NJ, n % NJ
                        act.wait_ge(s["pj_ready"], JOBS * p + n + 1)
                        src = sc[n % 2]
                        if b < 2:
                            a = act.activation((qT, kT)[b][:, j * NW:(j + 1) * NW], src[:, 0:NW], ACT.Copy)
                        elif j < NJ - 1:
                            a = act.activation(v[:, NJ * j:NJ * j + NJ, :],
                                               src[:, 0:NJ * P].rearrange("p (t n) -> p t n", n=P), ACT.Copy)
                        else:
                            act.activation(v[0:SR, TILES - 1, :], src[0:SR, 2 * P:3 * P], ACT.Copy)
                            a = act.activation(v[:, NJ * j:NJ * j + 2, :],
                                               src[:, 0:2 * P].rearrange("p (t n) -> p t n", n=P), ACT.Copy)
                        a.then_inc(s["pj_taken"], 1)
                    for i in range(UNITS + 1):
                        if i < UNITS:
                            nk = keys(i // 2)[2]
                            act.wait_ge(s["x_ready"], UNITS * p + i + 3)
                            act.activation(pr[i % 2][:, 0:nk], x[i % 2][:, 0:nk], ACT.Exp, scale=SCALE,
                                           bias=num[:, i % 4, 1:2],
                                           accum_out=num[:, i % 4, 2:3]).then_inc(s["p_ready"], 1)
                        if i >= 1:
                            t = (i - 1) // 2
                            n = keys(t)[1]
                            act.wait_ge(s["pt_ready"], UNITS * p + i)
                            act.wait_ge(s["pv_ready"], UNITS * p + i)
                            dst, src = pt[(i - 1) % 2], pst
                            if t < TILES - 1:
                                a = act.activation(dst[:, 0:n * P], src[:, 0:n * P], ACT.Copy)
                            else:
                                act.activation(dst[0:SR, BAND:W], src[0:SR, BAND:W], ACT.Copy)
                                a = act.activation(dst[:, 0:BAND], src[:, 0:BAND], ACT.Copy)
                            a.then_inc(s["pt_taken"], 1)

                act.wait_ge(s["init"], 1)
                with act.Fori(0, PAIRS) as p:
                    pair(p)

            @block.tensor
            def _(pe):
                def pair(p):
                    for n in range(JOBS):
                        b, j = n // NJ, n % NJ
                        if j == 0:
                            pe.wait_ge(s[f"w{b}"], 16 * p + 16)
                        pe.wait_ge(s["pj_taken"], JOBS * p + n + 1)
                        if n < 2:
                            pe.wait_ge(s["x_ready"], UNITS * p + 2)
                        if b < 2:
                            for k in range(KD):
                                mm = pe.matmul(sc[n % 2][:, 0:NW], w[b][:, k, :], c.hT[:, k, j * NW:(j + 1) * NW],
                                               start=(k == 0), stop=(k == KD - 1))
                        else:
                            for t in range(NJ * j, NJ * j + NJ):
                                r = rows_of(t)
                                for k in range(KD):
                                    mm = pe.matmul(sc[n % 2][0:r, (t - NJ * j) * P:(t - NJ * j + 1) * P],
                                                   c.hT[:, k, t * P:t * P + r], w[b][:, k, :],
                                                   start=(k == 0), stop=(k == KD - 1))
                        mm.then_inc(s["pj_ready"], 1)
                    pe.wait_ge(s["pj_taken"], JOBS * (p + 1) + 2)
                    pe.wait_ge(s["cache"], 32 * p + 32)

                    def scores(i):
                        t, e = i // 2, i % 2
                        lo, hi = e * DHB, e * DHB + DHB
                        first, n, nk = keys(t)
                        pe.wait_ge(s["x_ready"], UNITS * p + i + 1)
                        lhsT = qT[lo:hi, t * P:(t + 1) * P]
                        if t < TILES - 1:
                            pieces = [(0, min(nk, 512), kT[lo:hi, first * P:first * P + min(nk, 512)])]
                            if nk > 512:
                                pieces.append((512, nk, kT[lo:hi, first * P + 512:first * P + nk]))
                        else:
                            pieces = [(0, BAND, kc[lo:hi, :]), (BAND, NKS, kT[lo:hi, PR:ROWS])]
                        for a, b, rhs in pieces:
                            mm = pe.matmul(sc[i % 2][:, a:b], lhsT, rhs, start=True, stop=True)
                        mm.then_inc(s["sc_ready"], 1)

                    def turn(i):
                        t = i // 2
                        n = keys(t)[1]
                        pe.wait_ge(s["p_ready"], UNITS * p + i + 3)
                        pe.wait_ge(s["pt_taken"], UNITS * p + i + 1)
                        for k in range(n):
                            m = SR if t == TILES - 1 and k == n - 1 else P
                            tr = pe.transpose(pst[0:m, k * P:(k + 1) * P], pr[i % 2][:, k * P:k * P + m],
                                              c.consts[:, C_ID, :])
                        tr.then_inc(s["pt_ready"], 1)

                    def values(i):
                        t, e = i // 2, i % 2
                        first, n, _ = keys(t)
                        pe.wait_ge(s["pt_taken"], UNITS * p + i + 2)
                        if e == 0:
                            pe.wait_ge(s["o_taken"], TILES * p + t + 1)
                        cols = slice(e * DHB, e * DHB + DHB)
                        for k in range(n):
                            m = SR if t == TILES - 1 and k == n - 1 else P
                            if t < TILES - 1:
                                rhs = v[:, first + k, cols]
                            else:
                                rhs = vc[:, k, cols] if k < n - 1 else v[0:SR, TILES - 1, cols]
                            mm = pe.matmul(pso[:, cols], pt[i % 2][0:m, k * P:(k + 1) * P], rhs,
                                           start=(k == 0), stop=(k == n - 1))
                        mm.then_inc(s["pv_ready"], 1)

                    def turn_out(t):
                        pe.wait_ge(s["o_taken"], TILES * p + t + 2)
                        pe.wait_ge(s["y_taken"], TILES * p + t + 1)
                        pe.transpose(psy[:, 0:P], osb[t % 2][:, :], c.consts[:, C_ID, :]).then_inc(s["oT_ready"], 1)

                    for i in range(UNITS + 4):
                        if i < UNITS:
                            scores(i)
                        if 1 <= i <= UNITS:
                            turn(i - 1)
                        if 2 <= i < UNITS + 2:
                            values(i - 2)
                        if i >= 4 and i % 2 == 0:
                            turn_out((i - 4) // 2)

                pe.wait_ge(s["init"], 1)
                with pe.Fori(0, PAIRS) as p:
                    pair(p)

            @block.vector
            def _(dve):
                PER = 6 + 5 * TILES
                dve.wait_ge(s["tab"], 16)
                inv = 1.0 / SCALE
                end = FIRST + NREL
                for lo, hi, src in ((0, FIRST, tab[:, 0:1].to_broadcast([HB, FIRST])), (FIRST, end, tab[:, :]),
                                    (end, TAB, tab[:, NREL - 1:NREL].to_broadcast([HB, TAB - end]))):
                    dve.tensor_scalar(tab8[:, lo:hi], src, inv, None, ALU.mult).then_inc(s["tab8"], 1)
                dve.memset(qT[:, ROWS:PAD], 0.0).then_inc(s["tab8"], 1)
                for i, (n, k) in enumerate((("pj_taken", 2), ("x_ready", 2), ("p_ready", 2), ("pt_taken", 1),
                                            ("pv_ready", 2), ("o_taken", 1), ("y_taken", 1), ("init", 1))):
                    dve.memset(num[:, 1 + i // 4, i % 4:i % 4 + 1], 0.0).then_inc(s[n], k)

                def pair(p):
                    st = Chain(dve, s["chain"], PER * p)
                    dve.wait_ge(s["bias"], 32 * p + 32)
                    for e in range(2):
                        st.link(dve.tensor_copy(bias[:, e, :], brev[:, e, ::-1]))
                        st.mark(dve.memset(bias[CH:P, e, 0:CH], -1e30))
                        st.mark(dve.memset(bias[0:CH, e, W - CH:W], -1e30))
                    st.wait()

                    def softmax_in(i):
                        t, e = i // 2, i % 2
                        nk, b0 = keys(t)[2], bcol(t)
                        dve.wait_ge(s["p_ready"], UNITS * p + i + 1)
                        dve.wait_ge(s["sc_ready"], UNITS * p + i + 1)
                        st.mark(dve.memset(waits[:, :], 0.0))
                        st.link(dve.tensor_tensor_reduce(x[i % 2][:, 0:nk], sc[i % 2][:, 0:nk],
                                                         bias[:, e, b0:b0 + nk], 1.0, -3.0e38, ALU.add, ALU.max,
                                                         num[:, i % 4, 0:1]))
                        dve.tensor_scalar(num[:, i % 4, 1:2], num[:, i % 4, 0:1], -SCALE, None,
                                          ALU.mult).then_inc(s["x_ready"], 1)

                    def scale_out(t):
                        k = 2 * (t % 2)
                        dve.wait_ge(s["pv_ready"], UNITS * p + 2 * t + 4)
                        st.link(dve.reciprocal(num[:, k:k + 2, 3], num[:, k:k + 2, 2]))
                        dve.tensor_tensor(osb[t % 2][:, :].rearrange("p (e n) -> p e n", e=2),
                                          pso[:, 0:P].rearrange("p (e n) -> p e n", e=2),
                                          num[:, k:k + 2, 3].unsqueeze(2).to_broadcast([P, 2, DHB]),
                                          ALU.mult).then_inc(s["o_taken"], 1)

                    dve.wait_ge(s["yb_free"], 16 * p + 16)
                    for i in range(UNITS + 5):
                        if 4 <= i < UNITS + 4 and i % 2 == 0:
                            scale_out((i - 4) // 2)
                        if i < UNITS:
                            softmax_in(i)
                        if i >= 5 and i % 2 == 1:
                            t = (i - 5) // 2
                            r = rows_of(t)
                            dve.wait_ge(s["oT_ready"], TILES * p + t + 1)
                            dve.tensor_copy(yb[:, t * P:t * P + r], psy[:, 0:r]).then_inc(s["y_taken"], 1)
                    assert st.n == PER, st.n

                with dve.Fori(0, PAIRS) as p:
                    pair(p)


def phase_merge(nc, c):
    d = c.d
    NWB = 2 * KD + HA + PAIRS
    with ExitStack() as ctx:
        w = [sb(nc, ctx, f"wmix{i}", [P, NWB, P]) for i in range(2)]
        yaT = sb(nc, ctx, "yaT", [P, HA, ROWS])
        ybT = sb(nc, ctx, "ybT", [P, PAIRS, ROWS])
        sg = [sb(nc, ctx, f"sg{i}", [P, 2, NW]) for i in range(2)]
        m = [sb(nc, ctx, f"m{i}", [P, NW]) for i in range(2)]
        ps = [[ctx.enter_context(nc.psum_tensor(f"pm{i}{q}", [P, 512], F32)) for q in range(4)] for i in range(2)]
        w_in = [c.sem(f"x_w{i}") for i in range(2)]
        y_in, g_ready, u_ready, sg_done, taken, chain, init, out = (c.sem("x_" + n) for n in (
            "y", "g", "u", "sg", "taken", "chain", "init", "out"))
        with nc.Block() as block:
            @block.sync
            def _(sp):
                for i in range(2):
                    sp.dma_start(w[i][:, :, :], d["w_mix"][i]).then_inc(w_in[i], 16)
                    if i == 0:
                        sp.dma_start(yaT[:, :, :], d["ya"].rearrange("h p r -> p h r")).then_inc(y_in, 16)
                        sp.dma_start(ybT[:, :, :], d["yb"].rearrange("h p r -> p h r")).then_inc(y_in, 16)
                with sp.Fori(1, KD // 2) as n:
                    for i in range(2):
                        sp.wait_ge(u_ready, NJ * (2 * n + i - 1))
                        sp.dma_start(w[i][:, :, :], d["w_mix"][bass.ds(2 * n + i, 1)].rearrange("a p k c -> p (a k) c")).then_inc(w_in[i], 16)

            @block.tensor
            def _(pe):
                pe.wait_ge(init, 1)
                with pe.Fori(0, KD // 2) as n:
                    for i in range(2):
                        pe.wait_ge(w_in[i], 16 * n + 16)
                        for j in range(NJ):
                            job = NJ * i + j
                            cols = slice(j * NW, (j + 1) * NW)
                            b = ps[job % 2]
                            pe.wait_ge(taken, 2 * NJ * n + job + 1)
                            for q in range(2):
                                for k in range(KD):
                                    mm = pe.matmul(b[q][:, 0:NW], w[i][:, q * KD + k, :], c.hT[:, k, cols],
                                                   start=(k == 0), stop=(k == KD - 1))
                            mm.then_inc(g_ready, 1)
                            pe.wait_ge(y_in, 32)
                            for q, (src, off, nk) in enumerate(((yaT, 2 * KD, HA), (ybT, 2 * KD + HA, PAIRS))):
                                for k in range(nk):
                                    mm = pe.matmul(b[2 + q][:, 0:NW], w[i][:, off + k, :], src[:, k, cols],
                                                   start=(k == 0), stop=(k == nk - 1))
                            mm.then_inc(u_ready, 1)

            @block.scalar
            def _(act):
                act.wait_ge(init, 1)
                with act.Fori(0, KD // 2) as n:
                    for job in range(2 * NJ):
                        act.wait_ge(g_ready, 2 * NJ * n + job + 1)
                        act.wait_ge(taken, 2 * NJ * n + job + 1)
                        act.activation(sg[job % 2][:, 0, :], ps[job % 2][0][:, 0:NW], ACT.Sigmoid)
                        act.activation(sg[job % 2][:, 1, :], ps[job % 2][1][:, 0:NW], ACT.Sigmoid).then_inc(sg_done, 1)

            @block.vector
            def _(dve):
                PER = 4 * NJ
                dve.memset(m[0][:, 0:1], 0.0).then_inc(taken, 2)
                dve.memset(m[1][:, 0:1], 0.0).then_inc(init, 1)
                with dve.Fori(0, KD // 2) as n:
                    st = Chain(dve, chain, PER * n)
                    for i in range(2):
                        for j in range(NJ):
                            job = NJ * i + j
                            b, g = ps[job % 2], sg[job % 2]
                            dve.wait_ge(u_ready, 2 * NJ * n + job + 1)
                            dve.wait_ge(sg_done, 2 * NJ * n + job + 1)
                            dve.wait_ge(taken, 2 * NJ * n + job + 2)
                            st.mark(dve.tensor_tensor(m[0][:, :], b[2][:, 0:NW], g[:, 0, :], ALU.mult))
                            st.link(dve.tensor_tensor(m[1][:, :], b[3][:, 0:NW], g[:, 1, :], ALU.mult))
                            dve.tensor_tensor(c.mixT[:, bass.ds(2 * n + i, 1), j * NW:(j + 1) * NW].rearrange("p a r -> p (a r)"),
                                              m[0][:, :], m[1][:, :], ALU.add).then_inc(taken, 1)
                    assert st.n == PER, st.n


def phase_residual(nc, c):
    d = c.d
    NR = NG + NE
    with ExitStack() as ctx:
        def buf(name, shape):
            return sb(nc, ctx, name, shape)
        wo = buf("wo", [P, KD, D])
        wr = buf("wr", [P, KD, NR])
        br = buf("br", [P, NR])
        gt = buf("gt", [P, 2, D])
        lng, lnb = buf("l1g", [P, D]), buf("l1b", [P, D])
        x0 = [buf(f"xr{i}", [P, D]) for i in range(2)]
        x1 = [buf(f"x1{i}", [P, D]) for i in range(2)]
        stats, mv = buf("stats1", [P, 12]), buf("mv1", [P, TILES, 2])
        std, rstd = buf("std1", [P, TILES]), buf("rstd1", [P, TILES])
        eps = buf("eps1", [P, 1])
        lg = buf("lg", [P, TILES, NR])
        z = [buf(f"z{i}", [P, TILES, 4]) for i in range(8)]
        z1 = [buf(f"zz{i}", [P, TILES]) for i in range(8)]
        psy = [ctx.enter_context(nc.psum_tensor(f"py{i}", [P, 1024], F32)) for i in range(2)]
        pst = ctx.enter_context(nc.psum_tensor("pt_x1", [P, KD, P], F32))
        psr = ctx.enter_context(nc.psum_tensor("p_rt", [P, 512], F32))
        x_in = [c.sem(f"r_xin{i}") for i in range(2)]
        x_out = [c.sem(f"r_xout{i}") for i in range(2)]
        small, y_ready, var_ready, std_ready, x1_ready, xT, ha, hd, chain, rt, e_in, e_out, res, init = (
            c.sem("r_" + n) for n in ("small", "y", "var", "std", "x1", "xT", "ha", "hd", "chain", "rt", "ein",
                                      "eout", "res", "init"))
        with nc.Block() as block:
            @block.sync
            def _(sp):
                sp.dma_start(wo[:, :, :], d["w_out"]).then_inc(small, 16)
                rows = d["gate_rows"].rearrange("(g s k) c -> g s (k c)", g=2, s=2)
                for st in range(2):
                    sp.dma_start(gt[:, st, :], rows[0, st].partition_broadcast(P)).then_inc(small, 16)
                sp.dma_start(lng[:, :], d["ln1_g"].partition_broadcast(P)).then_inc(small, 16)
                sp.dma_start(lnb[:, :], d["ln1_b"].partition_broadcast(P)).then_inc(small, 16)
                sp.dma_start(wr[:, :, :], d["w_r"]).then_inc(small, 16)
                sp.dma_start(br[:, :], d["b_r"].partition_broadcast(P)).then_inc(small, 16)
                for t in range(TILES + 1):
                    if t < TILES:
                        if t >= 2:
                            sp.wait_ge(res, t - 1)
                        sp.dma_start(x0[t % 2][0:rows_of(t), :], d["x0"][t * P:t * P + rows_of(t), :]).then_inc(x_in[t % 2], 16)
                    if t >= 1:
                        sp.wait_ge(x1_ready, t)
                        sp.dma_start(d["x1"][(t - 1) * P:(t - 1) * P + rows_of(t - 1), :],
                                     x1[(t - 1) % 2][0:rows_of(t - 1), :]).then_inc(x_out[(t - 1) % 2], 16)
                sp.wait_ge(x_out[0], 16 * 5)
                sp.wait_ge(x_out[1], 16 * 4)

            @block.tensor
            def _(pe):
                pe.wait_ge(small, 16 * 7)

                def turn(t):
                    r = rows_of(t)
                    pe.wait_ge(x1_ready, t + 1)
                    if t >= 1:
                        pe.wait_ge(ha, t)
                        pe.wait_ge(hd, t)
                    for k in range(KD):
                        tr = pe.transpose(pst[:, k, 0:r], x1[t % 2][0:r, k * P:(k + 1) * P], c.consts[0:r, C_ID, 0:r])
                    tr.then_inc(xT, 1)

                for t in range(TILES):
                    r = rows_of(t)
                    if t >= 2:
                        pe.wait_ge(res, t - 1)
                    for h in range(2):
                        for k in range(KD):
                            mm = pe.matmul(psy[t % 2][0:r, h * 512:(h + 1) * 512], c.mixT[:, k, t * P:t * P + r],
                                           wo[:, k, h * 512:(h + 1) * 512], start=(k == 0), stop=(k == KD - 1))
                    mm.then_inc(y_ready, 1)
                    if t >= 1:
                        turn(t - 1)
                turn(TILES - 1)
                pe.wait_ge(ha, TILES)
                pe.wait_ge(hd, TILES)
                for t in range(TILES):
                    r = rows_of(t)
                    for k in range(KD):
                        mm = pe.matmul(psr[0:r, t * NR:(t + 1) * NR], c.h2T[:, k, t * P:t * P + r], wr[:, k, :],
                                       start=(k == 0), stop=(k == KD - 1))
                mm.then_inc(rt, 1)

            @block.scalar
            def _(act):
                act.wait_ge(init, 1)
                for t in range(TILES + 1):
                    if t < TILES:
                        r = rows_of(t)
                        act.wait_ge(var_ready, t + 1)
                        act.activation(std[0:r, t:t + 1], mv[0:r, t, 1:2], ACT.Sqrt, bias=eps[0:r, :]).then_inc(std_ready, 1)
                    if t >= 1:
                        u = t - 1
                        r, s = rows_of(u), 0 if u < TILES - 1 else 1
                        act.wait_ge(xT, u + 1)
                        for k in range(KD // 2):
                            a = act.activation(c.h2T[:, k, u * P:u * P + r], pst[:, k, 0:r], ACT.Identity,
                                               bias=c.mod[:, 3 * KD + k, s:s + 1], scale=c.mod[:, 4 * KD + k, s:s + 1])
                        a.then_inc(ha, 1)
                act.wait_ge(e_in, 1)
                act.activation(z[1][:, :, :], z[0][:, :, :], ACT.Exp).then_inc(e_out, 1)
                act.wait_ge(e_in, 2)
                act.activation(z1[3][:, :], z1[2][:, :], ACT.Exp).then_inc(e_out, 1)

            @block.vector
            def _(dve):
                st = Chain(dve, chain)
                dve.memset(eps[:, :], LN_EPS).then_inc(init, 1)
                st.link(dve.memset(lg[:, TILES - 1, :], 0.0))
                dve.wait_ge(small, 16 * 7)
                for t in range(TILES + 1):
                    if t < TILES:
                        r, s = rows_of(t), 0 if t < TILES - 1 else 1
                        xn = x1[t % 2]
                        dve.wait_ge(y_ready, t + 1)
                        if t >= 2:
                            dve.wait_ge(x_out[t % 2], 16 * (t // 2))
                            dve.wait_ge(xT, t - 1)
                        st.link(dve.tensor_tensor(xn[0:r, :], psy[t % 2][0:r, :], gt[0:r, s, :], ALU.mult))
                        dve.wait_ge(x_in[t % 2], 16 * (t // 2 + 1))
                        dve.scalar_tensor_tensor(out=xn[0:r, :], in0=x0[t % 2][0:r, :], scalar=ALPHA, in1=xn[0:r, :],
                                                 op0=ALU.mult, op1=ALU.add).then_inc(res, 1)
                        dve.wait_ge(res, t + 1)
                        for i in range(2):
                            st.mark(dve.bn_stats(stats[0:r, i * 6:i * 6 + 6], xn[0:r, i * 512:(i + 1) * 512]))
                        st.wait()
                        dve.bn_aggr(mv[0:r, t, :], stats[0:r, :]).then_inc(var_ready, 1)
                    if t >= 1:
                        u = t - 1
                        ru, su = rows_of(u), 0 if u < TILES - 1 else 1
                        dve.wait_ge(xT, u + 1)
                        for k in range(KD // 2, KD):
                            a = dve.tensor_scalar(c.h2T[:, k, u * P:u * P + ru], pst[:, k, 0:ru],
                                                  c.mod[:, 4 * KD + k, su:su + 1], c.mod[:, 3 * KD + k, su:su + 1],
                                                  ALU.mult, ALU.add)
                        a.then_inc(hd, 1)
                    if t < TILES:
                        dve.wait_ge(std_ready, t + 1)
                        st.link(dve.reciprocal(rstd[0:r, t:t + 1], std[0:r, t:t + 1]))
                        dve.wait_ge(var_ready, t + 1)
                        st.link(dve.tensor_scalar(xn[0:r, :], xn[0:r, :], mv[0:r, t, 0:1], rstd[0:r, t:t + 1],
                                                  ALU.subtract, ALU.mult))
                        st.link(dve.tensor_tensor(xn[0:r, :], xn[0:r, :], lng[0:r, :], ALU.mult))
                        dve.tensor_tensor(xn[0:r, :], xn[0:r, :], lnb[0:r, :], ALU.add).then_inc(x1_ready, 1)
                dve.wait_ge(rt, 1)
                full = TILES - 1
                st.mark(dve.tensor_tensor(lg[:, 0:full, :], psr[:, 0:full * NR].rearrange("p (t n) -> p t n", n=NR),
                                          br[:, :].unsqueeze(1).to_broadcast([P, full, NR]), ALU.add))
                st.link(dve.tensor_tensor(lg[0:SR, full, :], psr[0:SR, full * NR:TILES * NR], br[0:SR, :], ALU.add))

                def each(col):
                    return col[:, :].unsqueeze(2).to_broadcast([P, TILES, 4])

                def first_max(src, top, sel, seen):
                    st.link(dve.tensor_reduce(top[:, :], src, AX.X, ALU.max))
                    st.link(dve.tensor_tensor(sel[:, :, :], src, each(top), ALU.is_equal))
                    st.link(dve.tensor_copy(seen[:, :], sel[:, :, 0]))
                    for i in range(1, 4):
                        st.link(dve.tensor_tensor(sel[:, :, i], sel[:, :, i], seen[:, :], ALU.is_gt))
                        st.link(dve.tensor_tensor(seen[:, :], seen[:, :], sel[:, :, i], ALU.max))

                grp = lg[:, :, 0:NG]
                first_max(grp, z1[0], z[2], z1[1])
                dve.tensor_tensor(z[0][:, :, :], grp, each(z1[0]), ALU.subtract).then_inc(e_in, 1)
                z2 = z[2]
                le = [lg[:, :, NG + 4 * g:NG + 4 * g + 4] for g in range(NG)]
                pick = [z2[:, :, g].unsqueeze(2).to_broadcast([P, TILES, 4]) for g in range(NG)]
                st.link(dve.tensor_tensor(z[3][:, :, :], le[0], pick[0], ALU.mult))
                for g in range(1, NG):
                    st.link(dve.tensor_tensor(z[4][:, :, :], le[g], pick[g], ALU.mult))
                    st.link(dve.tensor_tensor(z[3][:, :, :], z[3][:, :, :], z[4][:, :, :], ALU.add))
                first_max(z[3][:, :, :], z1[4], z[5], z1[1])
                st.link(dve.scalar_tensor_tensor(out=flat2(z[4][:, :, :]), in0=flat2(z[5][:, :, :]), scalar=-1e30,
                                                 in1=flat2(z[3][:, :, :]), op0=ALU.mult, op1=ALU.add))
                first_max(z[4][:, :, :], z1[5], z[6], z1[1])
                dve.tensor_tensor(z1[2][:, :], z1[5][:, :], z1[4][:, :], ALU.subtract).then_inc(e_in, 1)
                dve.wait_ge(e_out, 2)
                st.link(dve.tensor_reduce(z1[6][:, :], z[1][:, :, :], AX.X, ALU.add))
                st.link(dve.tensor_scalar(z1[7][:, :], z1[3][:, :], 1.0, None, ALU.add))
                st.link(dve.tensor_tensor(z1[6][:, :], z1[6][:, :], z1[7][:, :], ALU.mult))
                st.link(dve.reciprocal(z1[6][:, :], z1[6][:, :]))
                st.link(dve.tensor_tensor(z1[7][:, :], z1[6][:, :], z1[3][:, :], ALU.mult))
                st.link(dve.tensor_tensor(z[5][:, :, :], z[5][:, :, :], each(z1[6]), ALU.mult))
                st.link(dve.tensor_tensor(z[6][:, :, :], z[6][:, :, :], each(z1[7]), ALU.mult))
                st.link(dve.tensor_tensor(z[5][:, :, :], z[5][:, :, :], z[6][:, :, :], ALU.add))
                for g in range(NG):
                    st.link(dve.tensor_tensor(c.gates[:, :, 4 * g:4 * g + 4], z[5][:, :, :], pick[g], ALU.mult))


def phase_experts(nc, c):
    d = c.d
    NF = DE // P
    JOBS = NJ * NF
    with ExitStack() as ctx:
        wgu = [sb(nc, ctx, f"wgu{i}", [P, KD, 2 * DE]) for i in range(2)]
        wd = [sb(nc, ctx, f"wd{i}", [P, NF, D]) for i in range(2)]
        aT = [sb(nc, ctx, f"aT{i}", [P, NF, ROWS]) for i in range(2)]
        sg = [sb(nc, ctx, f"sge{i}", [P, NW]) for i in range(2)]
        up = [[ctx.enter_context(nc.psum_tensor(f"pe{i}{q}", [P, 512], F32)) for q in range(2)] for i in range(2)]
        dn = [ctx.enter_context(nc.psum_tensor(f"pd{i}", [P, 512], F32)) for i in range(4)]
        gu_in, wd_in = [c.sem(f"e_gu{i}") for i in range(2)], [c.sem(f"e_wd{i}") for i in range(2)]
        up_ready, sg_done, a_done, dn_ready, dn_taken, init = (c.sem("e_" + n) for n in (
            "up", "sg", "a", "dn", "dnt", "init"))
        DN = 2 * TILES
        with nc.Block() as block:
            @block.sync
            def _(sp):
                for i in range(2):
                    sp.dma_start(wgu[i][:, :, :], d["w_gu"][i]).then_inc(gu_in[i], 16)
                    sp.dma_start(wd[i][:, :, :], d["w_dn"][i]).then_inc(wd_in[i], 16)
                with sp.Fori(1, NE // 2) as n:
                    for i in range(2):
                        e = bass.ds(2 * n + i, 1)
                        sp.wait_ge(up_ready, JOBS * (2 * n + i - 1))
                        sp.dma_start(wgu[i][:, :, :], d["w_gu"][e].rearrange("a p k c -> p (a k) c")).then_inc(gu_in[i], 16)
                        sp.wait_ge(dn_ready, DN * (2 * n + i - 1))
                        sp.dma_start(wd[i][:, :, :], d["w_dn"][e].rearrange("a p k c -> p (a k) c")).then_inc(wd_in[i], 16)

            @block.tensor
            def _(pe):
                pe.wait_ge(init, 1)
                with pe.Fori(0, NE // 2) as n:
                    for i in range(2):
                        pe.wait_ge(gu_in[i], 16 * n + 16)
                        for job in range(JOBS):
                            j, f = job // NF, job % NF
                            pe.wait_ge(a_done, JOBS * (2 * n + i) + job + 1)
                            for q in range(2):
                                for k in range(KD):
                                    mm = pe.matmul(up[job % 2][q][:, 0:NW], wgu[i][:, k, q * DE + f * P:q * DE + (f + 1) * P],
                                                   c.h2T[:, k, j * NW:(j + 1) * NW], start=(k == 0), stop=(k == KD - 1))
                            mm.then_inc(up_ready, 1)
                        pe.wait_ge(wd_in[i], 16 * n + 16)
                        for job in range(DN):
                            t, h = job // 2, job % 2
                            r = rows_of(t)
                            need = min(NJ, ((t + 1) * P - 1) // NW + 1) * NF
                            pe.wait_ge(a_done, JOBS * (2 * n + i) + need + 2)
                            pe.wait_ge(dn_taken, DN * (2 * n + i) + job + 1)
                            for f in range(NF):
                                mm = pe.matmul(dn[job % 4][0:r, :], aT[i][:, f, t * P:t * P + r],
                                               wd[i][:, f, h * 512:(h + 1) * 512], start=(f == 0), stop=(f == NF - 1))
                            mm.then_inc(dn_ready, 1)

            @block.scalar
            def _(act):
                act.wait_ge(init, 1)
                with act.Fori(0, NE // 2) as n:
                    for i in range(2):
                        for job in range(JOBS):
                            act.wait_ge(up_ready, JOBS * (2 * n + i) + job + 1)
                            act.wait_ge(a_done, JOBS * (2 * n + i) + job + 1)
                            act.activation(sg[job % 2][:, :], up[job % 2][0][:, 0:NW], ACT.Silu).then_inc(sg_done, 1)

            @block.vector
            def _(dve):
                dve.memset(sg[0][:, 0:1], 0.0).then_inc(a_done, 2)
                dve.memset(sg[1][:, 0:1], 0.0).then_inc(dn_taken, 4)
                dve.memset(c.acc[:, :, :], 0.0).then_inc(init, 1)
                dve.wait_ge(init, 1)
                with dve.Fori(0, NE // 2) as n:
                    for i in range(2):
                        for job in range(JOBS):
                            j, f = job // NF, job % NF
                            dve.wait_ge(sg_done, JOBS * (2 * n + i) + job + 1)
                            dve.tensor_tensor(aT[i][:, f, j * NW:(j + 1) * NW], up[job % 2][1][:, 0:NW], sg[job % 2][:, :],
                                              ALU.mult).then_inc(a_done, 1)
                        for job in range(DN):
                            t, h = job // 2, job % 2
                            r = rows_of(t)
                            a = c.acc[0:r, t, h * 512:(h + 1) * 512]
                            dve.wait_ge(dn_ready, DN * (2 * n + i) + job + 1)
                            dve.scalar_tensor_tensor(out=a, in0=dn[job % 4][0:r, :],
                                                     scalar=c.gates[0:r, t, bass.ds(2 * n + i, 1)], in1=a,
                                                     op0=ALU.mult, op1=ALU.add).then_inc(dn_taken, 1)


def phase_final(nc, c):
    d = c.d
    NX = 3
    with ExitStack() as ctx:
        def buf(name, shape):
            return sb(nc, ctx, name, shape)
        gt = buf("gt2", [P, 2, D])
        lng, lnb = buf("l2g", [P, D]), buf("l2b", [P, D])
        x1 = [buf(f"xf{i}", [P, D]) for i in range(NX)]
        stats, mv = buf("stats2", [P, 12]), buf("mv2", [P, TILES, 2])
        std, rstd, eps = buf("std2", [P, TILES]), buf("rstd2", [P, TILES]), buf("eps2", [P, 1])
        x_in = [c.sem(f"f_xin{i}") for i in range(NX)]
        y_out = [c.sem(f"f_yo{i}") for i in range(NX)]
        small, var_ready, std_ready, y_ready, chain, init = (c.sem("f_" + n) for n in (
            "small", "var", "std", "y", "chain", "init"))
        with nc.Block() as block:
            @block.sync
            def _(sp):
                rows = d["gate_rows"].rearrange("(g s k) c -> g s (k c)", g=2, s=2)
                for st in range(2):
                    sp.dma_start(gt[:, st, :], rows[1, st].partition_broadcast(P)).then_inc(small, 16)
                sp.dma_start(lng[:, :], d["ln2_g"].partition_broadcast(P)).then_inc(small, 16)
                sp.dma_start(lnb[:, :], d["ln2_b"].partition_broadcast(P)).then_inc(small, 16)
                for t in range(TILES + 1):
                    if t < TILES:
                        if t >= NX:
                            sp.wait_ge(y_out[t % NX], 16 * (t // NX))
                        sp.dma_start(x1[t % NX][0:rows_of(t), :], d["x1"][t * P:t * P + rows_of(t), :]).then_inc(x_in[t % NX], 16)
                    if t >= 1:
                        u = t - 1
                        sp.wait_ge(y_ready, t)
                        sp.dma_start(d["y"][u * P:u * P + rows_of(u), :], x1[u % NX][0:rows_of(u), :]).then_inc(y_out[u % NX], 16)
                for q in y_out:
                    sp.wait_ge(q, 16 * TILES // NX)

            @block.scalar
            def _(act):
                act.wait_ge(init, 1)
                for t in range(TILES):
                    r = rows_of(t)
                    act.wait_ge(var_ready, t + 1)
                    act.activation(std[0:r, t:t + 1], mv[0:r, t, 1:2], ACT.Sqrt, bias=eps[0:r, :]).then_inc(std_ready, 1)

            @block.vector
            def _(dve):
                st = Chain(dve, chain)
                dve.memset(eps[:, :], LN_EPS).then_inc(init, 1)
                dve.wait_ge(small, 64)
                for t in range(TILES + 1):
                    if t < TILES:
                        r, s, xn, a = rows_of(t), 0 if t < TILES - 1 else 1, x1[t % NX], c.acc
                        st.link(dve.tensor_tensor(a[0:r, t, :], a[0:r, t, :], gt[0:r, s, :], ALU.mult))
                        dve.wait_ge(x_in[t % NX], 16 * (t // NX + 1))
                        st.link(dve.scalar_tensor_tensor(out=xn[0:r, :], in0=xn[0:r, :], scalar=ALPHA, in1=a[0:r, t, :],
                                                         op0=ALU.mult, op1=ALU.add))
                        for i in range(2):
                            st.mark(dve.bn_stats(stats[0:r, i * 6:i * 6 + 6], xn[0:r, i * 512:(i + 1) * 512]))
                        st.wait()
                        dve.bn_aggr(mv[0:r, t, :], stats[0:r, :]).then_inc(var_ready, 1)
                    if t >= 1:
                        u = t - 1
                        r, xn = rows_of(u), x1[u % NX]
                        dve.wait_ge(std_ready, u + 1)
                        dve.wait_ge(var_ready, u + 1)
                        st.link(dve.reciprocal(rstd[0:r, u:u + 1], std[0:r, u:u + 1]))
                        st.link(dve.tensor_scalar(xn[0:r, :], xn[0:r, :], mv[0:r, u, 0:1], rstd[0:r, u:u + 1],
                                                  ALU.subtract, ALU.mult))
                        st.link(dve.tensor_tensor(xn[0:r, :], xn[0:r, :], lng[0:r, :], ALU.mult))
                        dve.tensor_tensor(xn[0:r, :], xn[0:r, :], lnb[0:r, :], ALU.add).then_inc(y_ready, 1)


def constants():
    r, col = np.arange(P)[:, None], np.arange(P)[None, :]
    same, blk = r // CH == col // CH, r // 16 == col // 16
    k = np.zeros((P, NCONST, P), np.float32)
    k[:, C_ID] = r == col
    k[:, C_CUM] = same & (r <= col)
    k[:, C_ONE] = 1.0
    k[:, C_NEG] = np.where(same & (r <= col), 0.0, -30000.0)
    k[:, C_M16] = blk & (col < r)
    k[:, C_MOFF] = same & ~blk & (col < r)
    k[:, C_CH0] = (r < CH) & (col >= 0)
    k[:, C_CH1] = (r >= CH) & (col >= 0)
    k[:, C_BLK] = same
    k[:, C_VAL, 0:TILES] = 1.0
    k[SR:, C_VAL, TILES - 1] = 0.0
    return k


def layout(i):
    a = {k: np.asarray(v) for k, v in i.items()}
    feat = lambda m: np.ascontiguousarray(m)
    w_in = a["w_in"][0]
    kpc = lambda m, *shape: m.reshape((KD, P) + shape)
    o = {}
    o["x"] = np.concatenate([a["x_prompt"][0], a["x_sample"][0]], 0)
    o["cT"] = np.stack([a["c_prompt"][0].reshape(KD, P), a["c_sample"][0].reshape(KD, P)], 2).transpose(1, 0, 2)
    o["consts"] = constants()
    o["w_mod"] = kpc(a["w_mod"][0], 12, 512).transpose(2, 1, 0, 3)
    o["b_mod"] = a["b_mod"][0].reshape(6 * KD, P).T
    o["a_dt"] = np.stack([a["a_log"][0], a["dt_bias"][0]])
    o["ln_in_g"], o["ln_in_b"] = a["ln_in_g"], a["ln_in_b"]
    o["w_ba"] = kpc(w_in[:, 4096:4112], 16).transpose(1, 0, 2)
    o["w_gdn"] = kpc(w_in[:, :4096], 4, HA, P).transpose(3, 2, 1, 0, 4)
    o["conv_w"] = a["conv_w"][0].reshape(CW, 3, HA, P).transpose(3, 2, 1, 0)
    o["conv_state"] = a["state_conv_a"][0, 0].reshape(CW - 1, 3, HA, P).transpose(3, 2, 1, 0)
    o["norm_w"] = a["gdn_norm_w"][0].reshape(P, 1)
    o["state"] = a["state_gdn"][0, 0]
    o["rel_bias"] = a["rel_bias"][0]
    o["w_att"] = kpc(w_in[:, 4112:5648], 3, PAIRS, P).transpose(3, 2, 1, 0, 4)
    o["k_cache"] = a["cache_k_b"][0, 0].reshape(BAND, PAIRS, P).transpose(1, 2, 0)
    o["v_cache"] = a["cache_v_b"][0, 0].reshape(BAND // P, P, PAIRS, P).transpose(2, 1, 0, 3)
    gates = kpc(w_in[:, 5648:], 2, KD, P).transpose(3, 1, 2, 0, 4).reshape(KD, P, 2 * KD, P)
    ups = [m.reshape(-1, P, KD, P).transpose(2, 1, 0, 3) for m in (a["w_up_a"][0], a["w_up_b"][0])]
    o["w_mix"] = np.concatenate([gates] + ups, 2)
    o["w_out"] = kpc(a["w_out"][0], D).transpose(1, 0, 2)
    for n in ("ln1_g", "ln1_b", "ln2_g", "ln2_b"):
        o[n] = a[n][0]
    o["w_r"] = kpc(np.concatenate([a["w_rg"][0], a["w_re"][0]], 1), NG + NE).transpose(1, 0, 2)
    o["b_r"] = np.concatenate([a["b_rg"][0], a["b_re"][0]])
    gu = np.concatenate([a["w_gate_e"][0], a["w_up_e"][0]], 2)
    o["w_gu"] = gu.reshape(NE, KD, P, 2 * DE).transpose(0, 2, 1, 3)
    o["w_dn"] = a["w_down_e"][0].reshape(NE, DE // P, P, D).transpose(0, 2, 1, 3)
    return {k: np.ascontiguousarray(v) for k, v in o.items()}


SCRATCH = {"gate_rows": (4 * KD, P), "x0": (ROWS, D), "ya": (HA, P, ROWS), "yb": (PAIRS, P, ROWS),
           "table": (HB, 768), "toeplitz": (HB, P, KT * P), "x1": (ROWS, D)}
OUTPUTS = {"gdn_p": (HA, P, P), "gdn_s": (HA, P, P), "tail": (P, HA, 3, 6), "kb_p": (PAIRS, P, BAND),
           "kb_s": (PAIRS, P, SR), "vb_p": (PAIRS, P, BAND // P, P), "vb_s": (PAIRS, SR, P), "y": (ROWS, D)}



def build(nc, d):
    with ExitStack() as ctx:
        c = Core(nc, ctx, d)
        c.consts = sb(nc, ctx, "consts", [P, NCONST, P])
        c.mod = sb(nc, ctx, "mod", [P, 6 * KD, 2])
        c.adt = sb(nc, ctx, "adt", [P, 2, HA])
        c.one = sb(nc, ctx, "one", [P, 1])
        c.gates = sb(nc, ctx, "gates", [P, TILES, NE])
        c.hT = c.h2T = sb(nc, ctx, "hT", [P, KD, ROWS])
        with ExitStack() as part:
            c.tok = sb(nc, part, "tok", [P, HA, NQ, TILES])
            c.tail = sb(nc, part, "tail", [P, HA, 3, 6])
            phase_modulation(nc, c)
            phase_trunk_norm(nc, c)
            phase_deltanet(nc, c)
            phase_attention(nc, c)
        with ExitStack() as part:
            c.mixT = sb(nc, part, "mixT", [P, KD, ROWS])
            phase_merge(nc, c)
            phase_residual(nc, c)
        with ExitStack() as part:
            c.acc = sb(nc, part, "acc", [P, TILES, D])
            phase_experts(nc, c)
            phase_final(nc, c)


def kernel(**inputs):
    import concourse.bacc as bacc
    from concourse.bass_utils import run_bass_kernel_spmd

    arrays = layout(inputs)
    nc = bacc.Bacc("TRN2", target_bir_lowering=False, num_devices=1)
    d = {n: nc.dram_tensor("in_" + n, a.shape, F32, kind="ExternalInput").ap() for n, a in arrays.items()}
    for n, shape in SCRATCH.items():
        d[n] = nc.dram_tensor("tmp_" + n, shape, F32, kind=SCRATCH_KIND).ap()
    for n, shape in OUTPUTS.items():
        d[n] = nc.dram_tensor("out_" + n, shape, F32, kind="ExternalOutput").ap()
    build(nc, d)
    r = run_bass_kernel_spmd(nc, [{"in_" + n: a for n, a in arrays.items()}], core_ids=[0]).results[0]
    y = r["out_y"]
    tail = r["out_tail"].transpose(3, 2, 1, 0).reshape(2, CW - 1, 3 * HA * P)
    kp = r["out_kb_p"].transpose(2, 0, 1).reshape(1, 1, BAND, HB, DHB)
    ks = r["out_kb_s"].transpose(2, 0, 1).reshape(1, 1, SR, HB, DHB)
    vp = r["out_vb_p"].transpose(2, 1, 0, 3).reshape(1, 1, BAND, HB, DHB)
    vs = r["out_vb_s"].transpose(1, 0, 2).reshape(1, 1, SR, HB, DHB)
    return (y[None, :PR], y[None, PR:], tail[None, None, 0], tail[None, None, 1],
            r["out_gdn_p"][None, None], r["out_gdn_s"][None, None], kp, ks, vp, vs)


SCRATCH_KIND = "Internal"
```

```python
from contextlib import ExitStack

import numpy as np

import concourse.bass as bass
from concourse import mybir

F32 = mybir.dt.float32
F32R = mybir.dt.float32r
ALU = mybir.AluOpType
ACT = mybir.ActivationFunctionType
AX = mybir.AxisListType

P = 128
D = 1024
KD = D // P
PR = 1024
SR = 32
ROWS = PR + SR
TILES = PR // P + 1
PAD = TILES * P
NJ = 3
NW = ROWS // NJ
PIN = PR - 2 * NW
HA = 8
CH = 64
CW = 4
RAW = PR + SR + 2 * (CW - 1)
SOFF = PR + 2 * (CW - 1)
CONVW = RAW - (CW - 1)
SCONV = PR + CW - 1
HB = 8
DHB = 64
PAIRS = HB // 2
BAND = 512
KT = BAND // P + 1
NREL = 192
NE = 16
NG = 4
DE = 256
ROW_SECTIONS = (2, 4, 3, 5)
MAXCH = 32
TCH = MAXCH + 4
RING = 4
TAB_E, TAB_S, TAB_END, TAB_N = 0, TCH, 2 * TCH, 2 * TCH + NE
NTAB = TAB_N + 1
ALPHA = 2.0 ** 0.25
LN_EPS = 1e-5
RMS_EPS = 1e-6
L2_EPS = 1e-6

C_ID, C_CUM, C_ONE, C_NEG, C_M16, C_MOFF, C_CH0, C_CH1, C_BLK, C_VAL, C_SUM, C_IOTA = range(12)
NCONST = 12

Q_G, Q_CUM, Q_NBETA, Q_BETA, Q_BEG, Q_KD, Q_GL0, Q_GL1 = range(8)
NQ = 8


def rows_of(t):
    return P if t < TILES - 1 else SR


class Chain:

    def __init__(self, eng, sem, base=0):
        self.eng, self.sem, self.base, self.n = eng, sem, base, 0

    def mark(self, ins):
        ins.then_inc(self.sem, 1)
        self.n += 1

    def wait(self, n=None):
        self.eng.wait_ge(self.sem, self.base + (self.n if n is None else n))

    def link(self, ins):
        self.mark(ins)
        self.wait()


def flat2(ap):
    return ap.rearrange("p a b -> p (a b)")


class Core:

    def __init__(self, nc, ctx, dram):
        self.nc, self.ctx, self.d = nc, ctx, dram
        self.used = []

    def h(self, k, lo, hi):
        return [m[:, k, lo:hi] for m in self.hT]

    def ones(self):
        return self.consts[:, C_ONE, :].unsqueeze(1).to_broadcast([P, KD, P])

    def sem(self, name):
        s = self.nc.alloc_semaphore(name=name)
        self.used.append(s)
        return s

    def run(self, phase):
        self.used = []
        phase(self.nc, self)
        used = self.used
        with self.nc.Block() as block:
            @block.gpsimd
            def _(pool):
                for s in used:
                    pool.sem_clear(s)
        for s in used:
            self.nc.release_semaphore(s)


def sb(nc, ctx, name, shape, dtype=F32):
    return ctx.enter_context(nc.sbuf_tensor(name, shape, dtype))


def plain(ap):
    return ap.bitcast(F32)


def split_matmul(pe, out, lhsT, rhs, start, stop):
    (lh, ll), (rh, rl) = lhsT, rhs
    pe.matmul(out, lh, rh, start=start, stop=False)
    pe.matmul(out, lh, rl, start=False, stop=False)
    return pe.matmul(out, ll, rh, start=False, stop=stop)


def ln_stats(st, x, rows, stats, mv):
    half = D // 2
    for i in range(2):
        st.mark(st.eng.bn_stats(stats[0:rows, i * 6:i * 6 + 6], x[0:rows, i * half:(i + 1) * half]))
    st.wait()
    st.link(st.eng.bn_aggr(mv[0:rows, :], stats[0:rows, :]))


def phase_entry(nc, c):
    d = c.d
    NX = NWM = 4
    HALF = 512
    NCHK = 6 * D // HALF
    LEAD = 2 * D // HALF
    BA = 2 * HA
    jobs = [("mod", n) for n in range(LEAD)]
    for t in range(TILES):
        jobs += [("turn", t)]
        if LEAD + t < NCHK:
            jobs += [("mod", LEAD + t)]
        jobs += [("ba", j) for j in range(NJ) if t == min(-(-NW * (j + 1) // P), TILES - 1) and t < TILES - 1]
    jobs += [("ba", NJ - 1)]
    taken = [j for j in jobs if j[0] != "turn"]
    with ExitStack() as ctx:
        wm = [sb(nc, ctx, f"wm{i}", [P, KD, HALF]) for i in range(NWM)]
        cT = sb(nc, ctx, "cT", [P, KD, 2])
        sc = sb(nc, ctx, "silu_c", [P, KD, 2])
        mod = sb(nc, ctx, "mod", [2, 6 * D])
        hx = [sb(nc, ctx, f"hx{i}", [P, KD, P]) for i in range(2)]
        modc = sb(nc, ctx, "mod_cols", [P, 2 * KD, 2])
        al = sb(nc, ctx, "al", [P, 2, HA])
        x = [sb(nc, ctx, f"x{i}", [P, D]) for i in range(NX)]
        lng = sb(nc, ctx, "lng", [P, D])
        lnb = sb(nc, ctx, "lnb", [P, D])
        wba = sb(nc, ctx, "wba", [P, KD, BA])
        wba2 = [sb(nc, ctx, f"wba_{n}", [P, KD, BA], F32R) for n in ("high", "low")]
        baT = sb(nc, ctx, "baT", [BA, ROWS])
        stats = sb(nc, ctx, "stats", [P, 12])
        mv = sb(nc, ctx, "mv", [P, TILES, 2])
        std = sb(nc, ctx, "std", [P, TILES])
        rstd = sb(nc, ctx, "rstd", [P, TILES])
        ba = sb(nc, ctx, "ba", [P, TILES, BA])
        y = sb(nc, ctx, "y", [P, 4, TILES, HA])
        gv = sb(nc, ctx, "gv", [P, TILES, HA])
        eps = sb(nc, ctx, "eps", [P, 1])
        psm = [ctx.enter_context(nc.psum_tensor(f"psm{i}", [P, 512], F32)) for i in range(2)]
        ps = [ctx.enter_context(nc.psum_tensor(f"psx{i}", [P, KD, P], F32)) for i in range(2)]
        psb = ctx.enter_context(nc.psum_tensor("psba", [P, 512], F32))
        psg = ctx.enter_context(nc.psum_tensor("psg", [P, 512], F32))
        x_in = [c.sem(f"n_xin{i}") for i in range(NX)]
        x0_out = [c.sem(f"n_x0out{i}") for i in range(NX)]
        w_in = [c.sem(f"m_w{i}") for i in range(NWM)]
        c_in, small, silu_done, nega_done, m_ready, m_taken = (
            c.sem("n_" + n) for n in ("cin", "small", "silu", "nega", "mready", "mtaken"))
        colsT, cols, rows_out, stat_done, std_done, xn, xg, x0_done, xT, hx_done, hT_done, wba_split = (
            c.sem("n_" + n) for n in ("colsT", "cols", "rowsout", "stat", "std", "xn", "xg", "x0", "xT", "hx", "hT", "wba"))
        dchain, eps_set, ba_T, sig_in, sig, g_ready, cum_ready, e_in, e_done, acts = (
            c.sem("n_" + n) for n in ("chain", "eps", "baT", "sigin", "sig", "g", "cum", "ein", "e", "acts"))
        with nc.Block() as block:
            @block.sync
            def _(sp):
                def w_mod(n):
                    sp.dma_start(wm[n % NWM][:, :, :], d["w_mod"][n]).then_inc(w_in[n % NWM], 16)

                def x_tile(t):
                    sp.dma_start(x[t % NX][0:rows_of(t), :], d["x"][t * P:t * P + rows_of(t), :]).then_inc(x_in[t % NX], 16)

                sp.dma_start(cT[:, :, :], d["cT"]).then_inc(c_in, 16)
                w_mod(0)
                x_tile(0)
                sp.dma_start(mod[:, :], d["b_mod"].partition_broadcast(2)).then_inc(small, 16)
                sp.dma_start(al[:, :, :], d["a_dt"].unsqueeze(0).to_broadcast([P, 2, HA])).then_inc(small, 16)
                sp.dma_start(lng[:, :], d["ln_in_g"].partition_broadcast(P)).then_inc(small, 16)
                sp.dma_start(lnb[:, :], d["ln_in_b"].partition_broadcast(P)).then_inc(small, 16)
                w_mod(1)
                sp.dma_start(c.consts[:, :, :], d["consts"]).then_inc(small, 16)
                sp.dma_start(wba[:, :, :], d["w_ba"]).then_inc(small, 16)
                x_tile(1)
                w_mod(2)
                x_tile(2)
                w_mod(3)
                x_tile(3)
                for t in range(TILES):
                    if t + NWM < NCHK:
                        sp.wait_ge(m_ready, taken.index(("mod", t)) + 1)
                        w_mod(t + NWM)
                    sp.wait_ge(x0_done, t + 1)
                    sp.dma_start(d["x0"][t * P:t * P + rows_of(t), :],
                                 x[t % NX][0:rows_of(t), :]).then_inc(x0_out[t % NX], 16)
                    if 1 <= t and t - 1 + NX < TILES:
                        sp.wait_ge(x0_out[(t - 1) % NX], 16 * ((t - 1) // NX + 1))
                        sp.wait_ge(xT, t)
                        x_tile(t - 1 + NX)
                sp.wait_ge(m_taken, taken.index(("mod", NCHK - 1)) + 1)
                out = d["gate_rows"].rearrange("(g s k) c -> g s (k c)", g=4, s=2)
                for g, sec in enumerate(ROW_SECTIONS):
                    sp.dma_start(out[g], mod[:, sec * D:(sec + 1) * D]).then_inc(rows_out, 16)
                sp.wait_ge(rows_out, 64)
                for i, q in enumerate(x0_out):
                    sp.wait_ge(q, 16 * len(range(i, TILES, NX)))

            @block.scalar
            def _(act):
                act.wait_ge(c_in, 16)
                act.activation(sc[:, :, :], cT[:, :, :], ACT.Silu).then_inc(silu_done, 1)
                act.wait_ge(small, 96)
                act.activation(c.adt[:, 0, :], al[:, 0, :], ACT.Exp).then_inc(nega_done, 1)
                act.wait_ge(eps_set, 1)
                for t in range(TILES + NX):
                    if t < TILES:
                        act.wait_ge(stat_done, t + 1)
                        act.activation(std[0:rows_of(t), t:t + 1], mv[0:rows_of(t), t, 1:2], ACT.Sqrt,
                                       bias=eps[0:rows_of(t), :]).then_inc(std_done, 1)
                    u = t - NX + 1
                    if 0 <= u < TILES:
                        s = 0 if u < TILES - 1 else 1
                        act.wait_ge(cols, 1)
                        act.wait_ge(xT, u + 1)
                        if u >= 2:
                            act.wait_ge(hT_done, u - 1)
                        for k in range(KD):
                            a = act.activation(hx[u % 2][:, k, 0:rows_of(u)], ps[u % 2][:, k, 0:rows_of(u)],
                                               ACT.Identity, bias=modc[:, 0 * KD + k, s:s + 1],
                                               scale=modc[:, 1 * KD + k, s:s + 1])
                        a.then_inc(hx_done, 1)
                act.wait_ge(sig_in, 1)
                act.activation(y[:, 0, :, :], ba[:, :, 0:HA], ACT.Sigmoid).then_inc(sig, 1)
                act.activation(y[:, 2, :, :], y[:, 2, :, :], ACT.Exp, scale=-1.0).then_inc(acts, 1)
                act.wait_ge(acts, 1)
                act.activation(y[:, 2, :, :], y[:, 2, :, :], ACT.Ln, bias=c.one[:, :]).then_inc(sig, 1)
                act.wait_ge(e_in, 1)
                act.activation(y[:, 0, :, :], y[:, 0, :, :], ACT.Exp).then_inc(e_done, 1)
                act.activation(y[:, 1, :, :], y[:, 1, :, :], ACT.Exp).then_inc(e_done, 1)
                for r in range(2):
                    act.activation(y[:, 2 + r, :, :],
                                   psg[:, (2 + r) * TILES * HA:(3 + r) * TILES * HA].rearrange("p (t h) -> p t h", h=HA),
                                   ACT.Exp).then_inc(e_done, 1)

            @block.gpsimd
            def _(pool):
                pool.wait_ge(small, 96)
                for t in range(TILES):
                    r, xt = rows_of(t), x[t % NX]
                    pool.wait_ge(xn, t + 1)
                    pool.tensor_tensor(xt[0:r, :], xt[0:r, :], lng[0:r, :], ALU.mult).then_inc(xg, 1)
                    pool.wait_ge(xg, t + 1)
                    pool.tensor_tensor(xt[0:r, :], xt[0:r, :], lnb[0:r, :], ALU.add).then_inc(x0_done, 1)

            @block.tensor
            def _(pe):
                pe.wait_ge(silu_done, 1)
                done = 0
                for kind, n in jobs:
                    if kind == "turn":
                        if n == 0:
                            pe.wait_ge(small, 96)
                            pe.wait_ge(m_taken, LEAD)
                            for i in range(2 * KD):
                                tr = pe.transpose(psb[:, 2 * i:2 * i + 2], mod[0:2, i * P:(i + 1) * P],
                                                  c.consts[0:2, C_ID, 0:2])
                            tr.then_inc(colsT, 1)
                        rows = rows_of(n)
                        pe.wait_ge(x0_done, n + 1)
                        if n >= 2:
                            pe.wait_ge(hx_done, n - 1)
                        for k in range(KD):
                            tr = pe.transpose(ps[n % 2][:, k, 0:rows], x[n % NX][0:rows, k * P:(k + 1) * P],
                                              c.consts[0:rows, C_ID, 0:rows])
                        tr.then_inc(xT, 1)
                        continue
                    out = psm[done % 2]
                    if done >= 2:
                        pe.wait_ge(m_taken, done - 1)
                    if kind == "mod":
                        pe.wait_ge(w_in[n % NWM], 16 * (n // NWM + 1))
                        for k in range(KD):
                            mm = pe.matmul(out[0:2, :], sc[:, k, :], wm[n % NWM][:, k, :],
                                           start=(k == 0), stop=(k == KD - 1))
                        mm.then_inc(m_ready, 1)
                    else:
                        pe.wait_ge(hT_done, min(-(-NW * (n + 1) // P), TILES))
                        pe.wait_ge(wba_split, 2)
                        for k in range(KD):
                            mm = split_matmul(pe, out[0:BA, 0:NW], [m[:, k, :] for m in wba2],
                                              c.h(k, n * NW, (n + 1) * NW), start=(k == 0), stop=(k == KD - 1))
                        mm.then_inc(m_ready, 1)
                    done += 1
                pe.wait_ge(m_taken, done)
                for t in range(TILES):
                    rows = rows_of(t)
                    tr = pe.transpose(psb[0:rows, t * BA:(t + 1) * BA], baT[0:BA, t * P:t * P + rows],
                                      c.consts[0:BA, C_ID, 0:BA])
                tr.then_inc(ba_T, 1)
                pe.wait_ge(g_ready, 1)
                for i, m in enumerate((C_CUM, C_BLK, C_CH0, C_CH1)):
                    mm = pe.matmul(psg[:, i * TILES * HA:(i + 1) * TILES * HA], c.consts[:, m, :],
                                   gv[:, :, :].rearrange("p t h -> p (t h)"), start=True, stop=True)
                mm.then_inc(cum_ready, 1)

            @block.vector
            def _(dve):
                st = Chain(dve, dchain)
                st.mark(dve.memset(c.one[:, :], 1.0))
                st.mark(dve.memset(ba[:, :, :], 0.0))
                dve.memset(eps[:, :], LN_EPS).then_inc(eps_set, 1)

                def norm(t):
                    r, xt = rows_of(t), x[t % NX]
                    dve.wait_ge(x_in[t % NX], 16 * (t // NX + 1))
                    ln_stats(st, xt, r, stats, mv[:, t, :])
                    dve.tensor_copy(rstd[0:r, t:t + 1], mv[0:r, t, 0:1]).then_inc(stat_done, 1)
                    dve.wait_ge(std_done, t + 1)
                    dve.wait_ge(stat_done, t + 1)
                    st.link(dve.reciprocal(rstd[0:r, t:t + 1], std[0:r, t:t + 1]))
                    dve.tensor_scalar(xt[0:r, :], xt[0:r, :], mv[0:r, t, 0:1], rstd[0:r, t:t + 1],
                                      ALU.subtract, ALU.mult).then_inc(xn, 1)

                def take(m, kind, n):
                    dve.wait_ge(m_ready, m + 1)
                    src = psm[m % 2]
                    if kind == "mod":
                        lo, one = n * HALF, 1.0 if n * HALF // D in (1, 2, 4, 5) else 0.0
                        ins = dve.scalar_tensor_tensor(out=mod[0:2, lo:lo + HALF], in0=src[0:2, :], scalar=one,
                                                       in1=mod[0:2, lo:lo + HALF], op0=ALU.add, op1=ALU.add)
                        ins.then_inc(m_taken, 1)
                        if n == LEAD - 1:
                            dve.wait_ge(colsT, 1)
                            dve.tensor_copy(modc[:, :, :], psb[:, 0:4 * KD].rearrange("p (i s) -> p i s", s=2)).then_inc(cols, 1)
                    else:
                        dve.tensor_copy(baT[0:BA, n * NW:(n + 1) * NW], src[0:BA, 0:NW]).then_inc(m_taken, 1)

                def split(t):
                    r = rows_of(t)
                    dve.wait_ge(hx_done, t + 1)
                    hi, lo = (m[:, :, t * P:t * P + r] for m in c.hT)
                    st.link(dve.tensor_copy(hi, hx[t % 2][:, :, 0:r]))
                    dve.tensor_tensor(lo, hx[t % 2][:, :, 0:r], plain(hi), ALU.subtract).then_inc(hT_done, 1)

                for i, (kind, n) in enumerate(taken):
                    if kind == "mod" and n < TILES:
                        norm(n)
                    if i == 0:
                        dve.wait_ge(small, 96)
                        dve.tensor_copy(wba2[0][:, :, :], wba[:, :, :]).then_inc(wba_split, 1)
                        dve.wait_ge(wba_split, 1)
                        dve.tensor_tensor(wba2[1][:, :, :], wba[:, :, :], plain(wba2[0][:, :, :]),
                                          ALU.subtract).then_inc(wba_split, 1)
                    if kind == "ba" and n == NJ - 1:
                        split(TILES - 1)
                    take(i, kind, n)
                    if kind == "mod" and n >= LEAD:
                        split(n - LEAD)
                dve.wait_ge(nega_done, 1)
                st.mark(dve.tensor_scalar(c.adt[:, 0, :], c.adt[:, 0, :], -1.0, None, ALU.mult))
                st.mark(dve.tensor_copy(c.adt[:, 1, :], al[:, 1, :]))
                dve.wait_ge(ba_T, 1)
                st.mark(dve.tensor_copy(ba[:, 0:TILES - 1, :],
                                        psb[:, 0:(TILES - 1) * BA].rearrange("p (t c) -> p t c", c=BA)))
                st.link(dve.tensor_copy(ba[0:SR, TILES - 1, :], psb[0:SR, (TILES - 1) * BA:TILES * BA]))
                st.link(dve.tensor_tensor(y[:, 1, :, :], ba[:, :, HA:2 * HA],
                                          c.adt[:, 1, :].unsqueeze(1).to_broadcast([P, TILES, HA]), ALU.add))
                st.link(dve.tensor_scalar(y[:, 3, :, :], y[:, 1, :, :], 0.0, None, ALU.max))
                dve.scalar_tensor_tensor(out=flat2(y[:, 2, :, :]), in0=flat2(y[:, 3, :, :]), scalar=2.0,
                                         in1=flat2(y[:, 1, :, :]), op0=ALU.mult, op1=ALU.subtract).then_inc(sig_in, 1)
                dve.wait_ge(sig, 2)
                st.wait()
                valid = c.consts[:, C_VAL, 0:TILES].unsqueeze(2).to_broadcast([P, TILES, HA])
                tok = [c.tok[:, :, q, :].rearrange("p h t -> p t h") for q in range(NQ)]
                st.mark(dve.tensor_tensor(tok[Q_BETA], y[:, 0, :, :], valid, ALU.mult))
                st.link(dve.tensor_tensor(y[:, 1, :, :], y[:, 2, :, :], y[:, 3, :, :], ALU.add))
                st.link(dve.tensor_tensor(y[:, 1, :, :], y[:, 1, :, :],
                                          c.adt[:, 0, :].unsqueeze(1).to_broadcast([P, TILES, HA]), ALU.mult))
                dve.tensor_tensor(gv[:, :, :], y[:, 1, :, :], valid, ALU.mult).then_inc(g_ready, 1)
                st.mark(dve.tensor_scalar(tok[Q_NBETA], tok[Q_BETA], -1.0, None, ALU.mult))
                dve.wait_ge(cum_ready, 1)
                dve.wait_ge(g_ready, 1)
                st.mark(dve.tensor_copy(tok[Q_G], gv[:, :, :]))
                n = TILES * HA
                pg = [psg[:, i * n:(i + 1) * n].rearrange("p (t h) -> p t h", h=HA) for i in range(2)]
                st.mark(dve.tensor_copy(tok[Q_CUM], pg[0]))
                st.link(dve.tensor_copy(y[:, 0, :, :], pg[0]))
                dve.tensor_tensor(y[:, 1, :, :], pg[1], y[:, 0, :, :], ALU.subtract).then_inc(e_in, 1)
                dve.wait_ge(e_done, 4)
                st.mark(dve.tensor_tensor(tok[Q_BEG], tok[Q_BETA], y[:, 0, :, :], ALU.mult))
                st.mark(dve.tensor_copy(tok[Q_KD], y[:, 1, :, :]))
                st.mark(dve.tensor_copy(tok[Q_GL0], y[:, 2, :, :]))
                st.link(dve.tensor_copy(tok[Q_GL1], y[:, 3, :, :]))


def phase_deltanet(nc, c):
    d = c.d
    G3 = 3
    NGRP = TILES // G3
    W3 = G3 * P
    JOBS = 4 * NJ
    NCHUNK = 2 * (TILES - 1) + 1
    with ExitStack() as ctx:
        def buf(name, shape):
            return sb(nc, ctx, name, shape)
        wraw = buf("wraw", [P, KD, P])
        w2 = [[sb(nc, ctx, f"w{i}_{n}", [P, KD, P], F32R) for n in ("high", "low")] for i in range(4)]
        cw = buf("cw", [P, HA, 3, CW])
        nw = buf("nw", [P, 1])
        cst = buf("cst", [P, HA, 3, CW - 1])
        raw = [buf(f"raw{i}", [P, RAW]) for i in range(3)]
        rawz = buf("rawz", [P, ROWS])
        f = [buf(f"f{i}", [P, PAD]) for i in range(3)]
        cwh = buf("cwh", [P, 3, CW])
        zs = buf("zs", [P, ROWS])
        yat = buf("yat", [P, ROWS])
        hq = buf("hq", [P, NQ, TILES])
        Dm, Eq, ET, A0, A0T, A1, A1T, Q, nN, kd = (buf(n, [P, PAD]) for n in
                                                  ("Dm", "Eq", "ET", "A0", "A0T", "A1", "A1T", "Q", "nN", "kd"))
        kb, bv, WKT, UV, PT = ET, nN, Q, A1, A1T
        cv, rinv, sq = (A0, A0T), Dm, Eq
        obuf = buf("obuf", [P, TILES, P])
        S = [buf(f"S{i}", [P, P]) for i in range(2)]
        Ssam = buf("Ssam", [P, 2, P])
        u = buf("u", [P, 2, P])
        ssq = buf("ssq", [P, 3, TILES])
        eps = buf("epsl", [P, 4])
        bank = [ctx.enter_context(nc.psum_tensor(f"bk{i}", [P, 512], F32)) for i in range(8)]
        pj, stg, aux, obank = bank[0:2], bank[2:5], bank[5:8], (bank[7], bank[2])

        s = {n: c.sem("g_" + n) for n in (
            "w_raw", "w_high", "w_split", "st_in", "s_free", "yat_free", "init", "tail_out",
            "pj_ready", "pj_taken", "raw_used", "z_used", "hq", "gb", "conv", "actv", "sq", "ss", "lnr",
            "rn", "qn", "zn", "st_ready", "st_dve", "st_act", "st_pool", "qd",
            "chain", "wk_ready", "wk_taken", "ws", "u", "ds", "S", "o", "o_taken", "son", "ssq", "rms",
            "on")}

        def psv(b):
            return b[:, 0:W3].rearrange("p (t n) -> p t n", n=P)

        def grp(m, g):
            return m[:, g * W3:(g + 1) * W3]

        def grp3(m, g):
            return grp(m, g).rearrange("p (t n) -> p t n", n=P)

        (G_ROW, KK, T_ET, T_A, A2, A2T, T_K, Q1, A4, A4T, Q2, A8, RT, BT, B, T_V, R, B2, W, TT, QK,
         T_O) = range(22)
        STAGES = 22

        def st_base(h):
            return STAGES * NGRP * h + NGRP

        with nc.Block() as block:
            @block.sync
            def _(sp):
                for dst, src in ((cw, d["conv_w"]), (cst, d["conv_state"])):
                    sp.dma_start(dst[:, :, :, :], src).then_inc(s["s_free"], 16)
                sp.dma_start(nw[:, :], d["norm_w"]).then_inc(s["yat_free"], 16)

                def weights(h, b):
                    src = d["w_gdn"][h, b] if isinstance(h, int) else \
                        d["w_gdn"][bass.ds(h, 1), b].rearrange("a p k c -> p (a k) c")
                    if not isinstance(h, int) or 4 * h + b > 0:
                        sp.wait_ge(s["w_split"], 4 * h + b)
                    sp.dma_start(wraw[:, :, :], src).then_inc(s["w_raw"], 16)

                def head(ap, h):
                    return ap[h] if isinstance(h, int) else ap[bass.ds(h, 1)].rearrange("a p c -> (a p) c")

                def state(h):
                    sp.dma_start(Ssam[:, 0, :], head(d["state"], h)).then_inc(s["st_in"], 16)

                def outputs(h):
                    sp.wait_ge(s["S"], (NCHUNK + 1) * h + NCHUNK)
                    sp.dma_start(head(d["gdn_p"], h), S[0][:, :]).then_inc(s["s_free"], 16)
                    sp.wait_ge(s["S"], (NCHUNK + 1) * h + NCHUNK + 1)
                    sp.dma_start(head(d["gdn_s"], h), Ssam[:, 1, :]).then_inc(s["s_free"], 16)

                def gated(h):
                    sp.wait_ge(s["st_dve"], st_base(h + 1))
                    sp.dma_start(head(d["ya"], h), yat[:, :]).then_inc(s["yat_free"], 16)

                state(0)
                for b in range(4):
                    weights(0, b)
                for b in range(2):
                    weights(1, b)
                with sp.Fori(0, HA - 2) as h:
                    for b in range(4):
                        weights(h + 1 + (b + 2) // 4, (b + 2) % 4)
                    outputs(h)
                    state(h + 1)
                    gated(h)
                for b in (2, 3):
                    weights(HA - 1, b)
                outputs(HA - 2)
                state(HA - 1)
                gated(HA - 2)
                outputs(HA - 1)
                gated(HA - 1)
                sp.wait_ge(s["raw_used"], 3 * HA)
                sp.dma_start(d["tail"], c.tail[:, :, :, :]).then_inc(s["tail_out"], 16)
                sp.wait_ge(s["s_free"], 32 * (HA + 1))
                sp.wait_ge(s["yat_free"], 16 * (HA + 1))
                sp.wait_ge(s["tail_out"], 16)

            @block.scalar
            def _(act):
                def take(hh, n):
                    b, j = n // NJ, n % NJ
                    act.wait_ge(s["pj_ready"], JOBS * hh + n + 1)
                    if j == 0 and not isinstance(hh, int) or j == 0 and hh > 0:
                        if b < 3:
                            act.wait_ge(s["raw_used"], 3 * (hh - 1) + b + 1)
                        else:
                            act.wait_ge(s["z_used"], hh)
                    src = pj[n % 2]
                    if b == 3:
                        a = act.activation(rawz[:, j * NW:(j + 1) * NW], src[:, 0:NW], ACT.Copy)
                    elif j < 2:
                        a = act.activation(raw[b][:, CW - 1 + j * NW:CW - 1 + (j + 1) * NW], src[:, 0:NW], ACT.Copy)
                    else:
                        act.activation(raw[b][:, SOFF:SOFF + SR], src[:, PIN:NW], ACT.Copy)
                        a = act.activation(raw[b][:, CW - 1 + 2 * NW:CW - 1 + PR], src[:, 0:PIN], ACT.Copy)
                    a.then_inc(s["pj_taken"], 1)

                def head(h, last):
                    act.wait_ge(s["pj_taken"], JOBS * (h + 1) + 2)
                    act.wait_ge(s["st_dve"], st_base(h))
                    act.activation(zs[:, :], rawz[:, :], ACT.Silu).then_inc(s["z_used"], 1)
                    for b in range(3):
                        act.wait_ge(s["conv"], 3 * h + b + 1)
                        act.activation(f[b][:, 0:PR], cv[b % 2][:, 0:PR], ACT.Silu)
                        act.activation(f[b][:, PR:ROWS], cv[b % 2][:, SCONV:SCONV + SR],
                                       ACT.Silu).then_inc(s["actv"], 1)
                        if not last:
                            take(h + 1, 2 * b)
                            take(h + 1, 2 * b + 1)
                    for b in range(2):
                        if b == 1:
                            act.wait_ge(s["qn"], 2 * h + 1)
                        for j in range(NJ):
                            act.wait_ge(s["ss"], 2 * NJ * h + b * NJ + j + 1)
                            act.activation(rinv[:, j * NW:(j + 1) * NW], aux[j][:, 0:NW], ACT.Ln,
                                           bias=eps[:, 0:1]).then_inc(s["lnr"], 1)
                        act.wait_ge(s["lnr"], 2 * NJ * h + (b + 1) * NJ)
                        act.activation(rinv[:, 0:ROWS], rinv[:, 0:ROWS], ACT.Exp, scale=-0.5,
                                       bias=eps[:, 1 + 2 * b:2 + 2 * b]).then_inc(s["rn"], 1)
                    for g in range(NGRP):
                        act.wait_ge(s["st_ready"], STAGES * NGRP * h + g + 1)
                        act.activation(grp(Eq, g), stg[g][:, 0:W3], ACT.Exp).then_inc(s["st_act"], 1)
                    for g in range(NGRP):
                        act.wait_ge(s["st_dve"], st_base(h) + g + 1)
                        act.activation(grp(Dm, g), grp(Dm, g), ACT.Exp).then_inc(s["st_act"], 1)
                    if not last:
                        for n in range(6, 9):
                            take(h + 1, n)
                    for i in range(2 * NGRP):
                        g = i // 2
                        act.wait_ge(s["wk_ready"], 2 * NGRP * h + i + 1)
                        act.activation(grp((WKT, UV)[i % 2], g), aux[i % 2][:, 0:W3],
                                       ACT.Copy).then_inc(s["wk_taken"], 1)
                    for t in range(TILES):
                        r = rows_of(t)
                        act.wait_ge(s["o"], TILES * h + t + 1)
                        act.activation(obuf[0:r, t, :], obank[t % 2][0:r, 0:P], ACT.Copy).then_inc(s["o_taken"], 1)
                        if not last and t in (4, 7):
                            take(h + 1, 9 if t == 4 else 10)
                    act.wait_ge(s["ssq"], h + 1)
                    act.activation(ssq[:, 1, :], ssq[:, 0, :], ACT.Ln, scale=1.0 / P,
                                   bias=eps[:, 2:3]).then_inc(s["son"], 1)
                    act.wait_ge(s["son"], h + 1)
                    act.activation(ssq[:, 2, :], ssq[:, 1, :], ACT.Exp, scale=-0.5).then_inc(s["rms"], 1)
                    if not last:
                        take(h + 1, 11)

                act.wait_ge(s["init"], 1)
                for n in range(JOBS):
                    take(0, n)
                act.wait_ge(s["init"], 2)
                with act.Fori(0, HA - 1) as h:
                    head(h, False)
                head(HA - 1, True)

            @block.gpsimd
            def _(pool):
                def split(h, b):
                    pool.wait_ge(s["w_raw"], 16 * (4 * h + b) + 16)
                    if not isinstance(h, int) or h > 0:
                        pool.wait_ge(s["pj_ready"], JOBS * (h - 1) + NJ * (b + 1))
                    hi, lo = (m[:, :, :] for m in w2[b])
                    raw_w = wraw[:, :, :]
                    pool.tensor_tensor(hi, raw_w, c.ones(), ALU.mult).then_inc(s["w_high"], 1)
                    pool.wait_ge(s["w_high"], 4 * h + b + 1)
                    pool.tensor_tensor(lo, raw_w, plain(hi), ALU.subtract).then_inc(s["w_split"], 1)

                def head(h, splits):
                    for b in (2, 3):
                        if splits >= 2:
                            split(h + 1, b)
                    pool.wait_ge(s["hq"], h + 1)
                    pool.tensor_tensor(Q[:, :].rearrange("p (t n) -> p t n", n=P),
                                       c.consts[:, C_ONE, :].unsqueeze(1).to_broadcast([P, TILES, P]),
                                       hq[:, Q_G, :].unsqueeze(2).to_broadcast([P, TILES, P]),
                                       ALU.mult).then_inc(s["gb"], 1)
                    pool.wait_ge(s["z_used"], h + 1)
                    pool.tensor_tensor(zs[:, :], zs[:, :], nw[:, 0:1].to_broadcast([P, ROWS]), ALU.mult).then_inc(s["zn"], 1)
                    for b in range(2):
                        pool.wait_ge(s["actv"], 3 * h + b + 1)
                        if b == 1:
                            pool.wait_ge(s["ss"], 2 * NJ * h + NJ)
                        pool.tensor_tensor(sq[:, 0:ROWS], f[b][:, 0:ROWS], f[b][:, 0:ROWS], ALU.mult).then_inc(s["sq"], 1)
                    pool.wait_ge(s["qn"], 2 * h + 1)
                    for g in range(NGRP):
                        pool.wait_ge(s["st_act"], 2 * NGRP * h + g + 1)
                        pool.tensor_tensor(grp(Eq, g), grp(Eq, g), grp(f[0], g), ALU.mult).then_inc(s["qd"], 1)
                    for b in (0, 1):
                        if splits == 4:
                            split(h + 2, b)
                    eye = c.consts[:, C_ID, :].unsqueeze(1).to_broadcast([P, G3, P])
                    for dst, src, stage in ((Q, A0T, T_A), (A1T, A0T, BT)):
                        for g in range(NGRP):
                            pool.wait_ge(s["st_dve"], st_base(h) + NGRP * stage + g + 1)
                            pool.tensor_tensor(grp3(dst, g), grp3(src, g), eye, ALU.add).then_inc(s["st_pool"], 1)

                for i in range(6):
                    split(i // 4, i % 4)
                pool.wait_ge(s["yat_free"], 16)
                with pool.Fori(0, HA - 2) as h:
                    head(h, 4)
                head(HA - 2, 2)
                head(HA - 1, 0)

            @block.tensor
            def _(pe):
                def product(hh, n):
                    b, j = n // NJ, n % NJ
                    if j == 0:
                        pe.wait_ge(s["w_split"], 4 * hh + b + 1)
                    pe.wait_ge(s["pj_taken"], JOBS * hh + n + 1)
                    for k in range(KD):
                        mm = split_matmul(pe, pj[n % 2][:, 0:NW], [m[:, k, :] for m in w2[b]],
                                          c.h(k, j * NW, (j + 1) * NW), start=(k == 0), stop=(k == KD - 1))
                        if k == KD - 1:
                            mm.then_inc(s["pj_ready"], 1)
                        yield

                def products(hh, jobs):
                    for n in jobs:
                        yield from product(hh, n)

                def head(h, last):
                    fill = products(h + 1, () if last else range(JOBS))

                    def step(n):
                        for _ in range(n):
                            next(fill, None)

                    def stage(n, mms):
                        for g in range(NGRP):
                            pe.wait_ge(s["st_dve"], st_base(h) + NGRP * (n - 1) + g + 1)
                            for t in range(G3 * g, G3 * g + G3):
                                mm = mms(t, stg[g][:, (t - G3 * g) * P:(t - G3 * g + 1) * P])
                            mm.then_inc(s["st_ready"], 1)

                    def tl(m, t):
                        return m[:, t * P:(t + 1) * P]

                    def mul(lhsT, rhs):
                        return lambda t, out: pe.matmul(out, tl(lhsT, t), tl(rhs, t), start=True, stop=True)

                    def turn(m):
                        return lambda t, out: pe.transpose(out, tl(m, t), c.consts[:, C_ID, :])

                    step(6 * KD)
                    for b in range(2):
                        pe.wait_ge(s["sq"], 2 * h + b + 1)
                        for j in range(NJ):
                            if b == 1:
                                pe.wait_ge(s["lnr"], 2 * NJ * h + j + 1)
                            pe.matmul(aux[j][:, 0:NW], c.consts[:, C_ONE, :], sq[:, j * NW:(j + 1) * NW],
                                      start=True, stop=True).then_inc(s["ss"], 1)
                        step(KD)
                    pe.wait_ge(s["gb"], h + 1)
                    stage(G_ROW, lambda t, out: pe.matmul(out, tl(Q, t), c.consts[:, C_CUM, :], start=True, stop=True))
                    pe.wait_ge(s["qn"], 2 * h + 2)
                    stage(KK, mul(f[1], f[1]))
                    stage(T_ET, turn(ET))
                    step(2)
                    stage(T_A, turn(A0))
                    step(2)
                    stage(A2, mul(A0T, A0))
                    stage(A2T, mul(A0, A0T))
                    stage(T_K, turn(f[1]))
                    step(2)
                    pe.wait_ge(s["st_pool"], 2 * NGRP * h + NGRP)
                    stage(Q1, mul(A1, Q))
                    stage(A4, mul(A1T, A1))
                    stage(A4T, mul(A1, A1T))
                    stage(Q2, mul(A0, Q))
                    stage(A8, mul(A0T, A0))
                    stage(RT, mul(A1, Q))
                    stage(BT, mul(nN, Q))
                    stage(B, mul(Q, nN))
                    pe.wait_ge(s["actv"], 3 * h + 3)
                    stage(T_V, turn(f[2]))
                    stage(R, turn(Q))
                    stage(B2, mul(A0T, A0))
                    pe.wait_ge(s["st_pool"], 2 * NGRP * h + 2 * NGRP)
                    stage(W, mul(A0, A1T))
                    step(2)
                    stage(TT, mul(A1, A1T))
                    for i in range(2 * NGRP):
                        g = i // 2
                        pe.wait_ge(s["st_dve"], st_base(h) + NGRP * TT + g + 1)
                        if i >= 2:
                            pe.wait_ge(s["wk_taken"], 2 * NGRP * h + i - 1)
                        for t in range(G3 * g, G3 * g + G3):
                            lhsT, rhs = ((kb, A0T), (A0T, bv))[i % 2]
                            mm = pe.matmul(aux[i % 2][:, (t - G3 * g) * P:(t - G3 * g + 1) * P],
                                           tl(lhsT, t), tl(rhs, t), start=True, stop=True)
                        mm.then_inc(s["wk_ready"], 1)
                    stage(QK, mul(f[1], f[0]))
                    pe.wait_ge(s["qd"], NGRP * h + NGRP)
                    pe.wait_ge(s["wk_taken"], 2 * NGRP * (h + 1))
                    pe.wait_ge(s["st_dve"], st_base(h) + NGRP * QK + NGRP)
                    for n in range(NCHUNK):
                        t, r = n // 2, n % 2
                        lo, hi = r * CH, r * CH + CH
                        if n < NCHUNK - 1:
                            Sn = S[n % 2][:, :]
                            pe.wait_ge(s["S"], (NCHUNK + 1) * h + n + 1)
                        else:
                            Sn = Ssam[:, 0, :]
                            pe.wait_ge(s["st_in"], 16 * (h + 1))
                            pe.wait_ge(s["u"], NCHUNK * h + n)
                        pe.matmul(aux[0][lo:hi, 0:P], WKT[:, t * P + lo:t * P + hi], Sn,
                                  start=True, stop=True).then_inc(s["ws"], 1)
                        if r == 0:
                            pe.wait_ge(s["o_taken"], TILES * h + t + 1)
                        pe.matmul(obank[t % 2][lo:hi, 0:P], Eq[:, t * P + lo:t * P + hi], Sn,
                                  start=True, stop=False)
                        if n < NCHUNK - 1:
                            step(1)
                        pe.wait_ge(s["u"], NCHUNK * h + n + 1)
                        if n == NCHUNK - 1:
                            pe.wait_ge(s["S"], (NCHUNK + 1) * h + n + 1)
                        pe.matmul(aux[1][:, 0:P], kd[lo:hi, t * P:(t + 1) * P], u[lo:hi, t % 2, :],
                                  start=True, stop=True).then_inc(s["ds"], 1)
                        mm = pe.matmul(obank[t % 2][lo:hi, 0:P], PT[lo:hi, t * P + lo:t * P + hi],
                                       u[lo:hi, t % 2, :], start=False, stop=True)
                        if r == 1 or n == NCHUNK - 1:
                            mm.then_inc(s["o"], 1)
                    step(JOBS * KD)
                    pe.wait_ge(s["on"], h + 1)
                    stage(T_O, lambda t, out: pe.transpose(out[:, 0:rows_of(t)], obuf[0:rows_of(t), t, :],
                                                           c.consts[0:rows_of(t), C_ID, 0:rows_of(t)]))

                pe.wait_ge(s["init"], 1)
                for _ in products(0, range(JOBS)):
                    pass
                with pe.Fori(0, HA - 1) as h:
                    head(h, False)
                head(HA - 1, True)

            @block.vector
            def _(dve):
                PER = 14

                def head(h):
                    st = Chain(dve, s["chain"], PER * h + 8)
                    st.mark(dve.tensor_copy(cwh[:, :, :], cw[:, bass.ds(h, 1), :, :].rearrange("p a b i -> p (a b) i")))
                    for b in range(3):
                        st.mark(dve.tensor_copy(raw[b][:, SOFF - CW + 1:SOFF], cst[:, bass.ds(h, 1), b, :].rearrange("p a i -> p (a i)")))
                    dve.tensor_copy(hq[:, :, :], c.tok[:, bass.ds(h, 1), :, :].rearrange("p a q t -> p (a q) t")).then_inc(s["hq"], 1)
                    st.wait()
                    for b in range(3):
                        dve.wait_ge(s["pj_taken"], JOBS * h + NJ * (b + 1) + 2)
                        if b == 2:
                            dve.wait_ge(s["actv"], 3 * h + 1)
                        cvb = cv[b % 2][:, 0:CONVW]
                        st.link(dve.tensor_scalar(cvb, raw[b][:, 0:CONVW], cwh[:, b, 0:1], None, ALU.mult))
                        for k in range(1, CW):
                            ins = dve.scalar_tensor_tensor(out=cvb, in0=raw[b][:, k:k + CONVW],
                                                           scalar=cwh[:, b, k:k + 1], in1=cvb,
                                                           op0=ALU.mult, op1=ALU.add)
                            if k < CW - 1:
                                st.link(ins)
                            else:
                                ins.then_inc(s["conv"], 1)
                        dve.tensor_copy(c.tail[:, bass.ds(h, 1), b, 0:3].rearrange("p a i -> p (a i)"), raw[b][:, PR:PR + 3])
                        dve.tensor_copy(c.tail[:, bass.ds(h, 1), b, 3:6].rearrange("p a i -> p (a i)"),
                                        raw[b][:, RAW - 3:RAW]).then_inc(s["raw_used"], 1)
                    for b in range(2):
                        dve.wait_ge(s["rn"], 2 * h + b + 1)
                        dve.tensor_tensor(f[b][:, 0:ROWS], f[b][:, 0:ROWS], rinv[:, 0:ROWS], ALU.mult).then_inc(s["qn"], 1)
                    dve.wait_ge(s["qn"], 2 * h + 2)

                    def ready(n, g):
                        dve.wait_ge(s["st_ready"], STAGES * NGRP * h + NGRP * n + g + 1)

                    def take(n, op):
                        for g in range(NGRP):
                            ready(n, g)
                            op(g).then_inc(s["st_dve"], 1)

                    def copy(m):
                        return lambda g: dve.tensor_copy(grp(m, g), stg[g][:, 0:W3])

                    def add(m):
                        return lambda g: dve.tensor_tensor(grp(m, g), stg[g][:, 0:W3], grp(m, g), ALU.add)

                    def tiles(g):
                        return [(t, stg[g][:, (t - G3 * g) * P:(t - G3 * g + 1) * P]) for t in range(G3 * g, G3 * g + G3)]

                    def scaled(m, q):
                        return lambda g: dve.tensor_tensor(
                            grp3(m, g), psv(stg[g]), hq[:, q, G3 * g:G3 * g + G3].unsqueeze(2).to_broadcast([P, G3, P]),
                            ALU.mult)

                    def decay(g):
                        dve.wait_ge(s["st_act"], 2 * NGRP * h + g + 1)
                        for t, ps in tiles(g):
                            ins = dve.scalar_tensor_tensor(out=Dm[:, t * P:(t + 1) * P], in0=ps,
                                                           scalar=hq[:, Q_CUM, t:t + 1], in1=c.consts[:, C_NEG, :],
                                                           op0=ALU.subtract, op1=ALU.min)
                        return ins

                    def kk(g):
                        dve.wait_ge(s["st_act"], 2 * NGRP * h + NGRP + g + 1)
                        return dve.tensor_tensor(grp(ET, g), stg[g][:, 0:W3], grp(Dm, g), ALU.mult)

                    def split(g):
                        for t, ps in tiles(g):
                            for m, mask in ((A0, C_M16), (nN, C_MOFF)):
                                ins = dve.scalar_tensor_tensor(out=m[:, t * P:(t + 1) * P], in0=ps,
                                                               scalar=hq[:, Q_NBETA, t:t + 1], in1=c.consts[:, mask, :],
                                                               op0=ALU.mult, op1=ALU.mult)
                        return ins

                    def keys(g):
                        scaled(kb, Q_BEG)(g)
                        return scaled(kd, Q_KD)(g)

                    take(G_ROW, decay)
                    take(KK, kk)
                    take(T_ET, split)
                    take(T_A, copy(A0T))
                    take(A2, copy(A1))
                    take(A2T, copy(A1T))
                    take(T_K, keys)
                    take(Q1, add(Q))
                    take(A4, copy(A0))
                    take(A4T, copy(A0T))
                    take(Q2, add(Q))
                    take(A8, copy(A1))
                    take(RT, add(Q))
                    take(BT, copy(A0T))
                    take(B, copy(A0))
                    take(T_V, scaled(bv, Q_BETA))
                    take(R, copy(A1))
                    take(B2, copy(A0))
                    take(W, add(A1T))
                    take(TT, copy(A0T))
                    take(QK, lambda g: dve.tensor_tensor(grp(PT, g), stg[g][:, 0:W3], grp(Dm, g), ALU.mult))
                    dve.wait_ge(s["s_free"], 32 * (h + 1))
                    dve.memset(S[0][:, :], 0.0).then_inc(s["S"], 1)
                    dve.wait_ge(s["wk_taken"], 2 * NGRP * (h + 1))
                    for n in range(NCHUNK):
                        t, r = n // 2, n % 2
                        lo, hi = r * CH, r * CH + CH
                        dve.wait_ge(s["ws"], NCHUNK * h + n + 1)
                        dve.tensor_tensor(u[lo:hi, t % 2, :], UV[lo:hi, t * P:(t + 1) * P], aux[0][lo:hi, 0:P],
                                          ALU.subtract).then_inc(s["u"], 1)
                        dve.wait_ge(s["ds"], NCHUNK * h + n + 1)
                        old, new = (S[n % 2][:, :], S[(n + 1) % 2][:, :]) if n < NCHUNK - 1 else (Ssam[:, 0, :], Ssam[:, 1, :])
                        dve.scalar_tensor_tensor(out=new, in0=old, scalar=hq[:, Q_GL0 + r, t:t + 1], in1=aux[1][:, 0:P],
                                                 op0=ALU.mult, op1=ALU.add).then_inc(s["S"], 1)
                    dve.wait_ge(s["o_taken"], TILES * (h + 1) + 2)
                    osq = Dm[:, :].rearrange("p (t n) -> p t n", n=P)
                    st.link(dve.tensor_tensor(osq, obuf[:, :, :], obuf[:, :, :], ALU.mult))
                    dve.tensor_reduce(ssq[:, 0, :], osq, AX.X, ALU.add).then_inc(s["ssq"], 1)
                    dve.wait_ge(s["rms"], h + 1)
                    dve.tensor_tensor(obuf[:, :, :], obuf[:, :, :],
                                      ssq[:, 2, :].unsqueeze(2).to_broadcast([P, TILES, P]), ALU.mult).then_inc(s["on"], 1)
                    dve.wait_ge(s["zn"], h + 1)
                    dve.wait_ge(s["yat_free"], 16 * (h + 1))
                    for g in range(NGRP):
                        ready(T_O, g)
                        lo, hi = g * W3, min((g + 1) * W3, ROWS)
                        dve.tensor_tensor(yat[:, lo:hi], stg[g][:, 0:hi - lo], zs[:, lo:hi],
                                          ALU.mult).then_inc(s["st_dve"], 1)
                    assert st.n == PER, st.n

                st = Chain(dve, s["chain"])
                for b in range(3):
                    st.mark(dve.memset(raw[b][:, 0:CW - 1], 0.0))
                    st.mark(dve.memset(f[b][:, ROWS:PAD], 0.0))
                st.mark(dve.memset(obuf[:, :, :], 0.0))
                st.link(dve.memset(eps[:, 3:4], 0.0))
                dve.memset(eps[:, 0:1], L2_EPS)
                dve.memset(eps[:, 1:2], float(-0.5 * np.log(P))).then_inc(s["init"], 1)
                dve.memset(eps[:, 2:3], RMS_EPS).then_inc(s["init"], 1)
                for i, (sem, n) in enumerate(((s["pj_taken"], 2), (s["st_dve"], NGRP), (s["o_taken"], 2))):
                    dve.memset(ssq[:, 0, i:i + 1], 0.0).then_inc(sem, n)
                dve.wait_ge(s["s_free"], 32)
                with dve.Fori(0, HA) as h:
                    head(h)


def phase_attention(nc, c):
    d = c.d
    W = KT * P
    UNITS = 2 * TILES
    JOBS = 4 * NJ
    TAB = c.d["table"].shape[1]
    FIRST = P - CH
    NKS = BAND + SR
    SCALE = float(DHB) ** -0.5
    with ExitStack() as ctx:
        def buf(name, shape):
            return sb(nc, ctx, name, shape)
        w = [buf(f"wa{i}", [P, KD, P]) for i in range(3)]
        w2 = [[sb(nc, ctx, f"wa{i}_{n}", [P, KD, P], F32R) for n in ("high", "low")] for i in range(3)]
        qT, kT = buf("qT", [P, PAD]), buf("kT", [P, ROWS])
        vT = buf("vT", [P, PAD])
        v = buf("v", [P, TILES, P])
        kc, vc = buf("kc", [P, BAND]), buf("vc", [P, BAND // P, P])
        bias, brev = buf("bias", [P, 2, W]), buf("brev", [P, 2, W])
        x = [buf(f"sx{i}", [P, W]) for i in range(2)]
        pr = [buf(f"pr{i}", [P, W]) for i in range(2)]
        pt = [buf(f"pt{i}", [P, W]) for i in range(2)]
        osb = [buf(f"osb{i}", [P, P]) for i in range(2)]
        yb = buf("yb", [P, ROWS])
        tab, tab8 = buf("tab", [HB, NREL]), buf("tab8", [HB, TAB])
        waits = buf("waits", [P, 1])
        zero = buf("zero_row", [P, D])
        num = buf("num", [P, 4, 4])
        sc = [ctx.enter_context(nc.psum_tensor(f"sc{i}", [P, 1024], F32)) for i in range(2)]
        pst = ctx.enter_context(nc.psum_tensor("pst", [P, 1024], F32))
        pso = ctx.enter_context(nc.psum_tensor("pso", [P, 512], F32))
        psy = ctx.enter_context(nc.psum_tensor("psy", [P, 512], F32))
        s = {n: c.sem("a_" + n) for n in (
            "w0", "w1", "w2", "w_high", "w_split", "tab", "tab8", "tab_out", "toep", "bias", "masked", "cache", "yb_free", "kv_out",
            "pj_ready", "pj_taken", "sc_ready", "x_ready", "p_ready", "pt_ready", "pt_taken", "pv_ready",
            "o_taken", "oT_ready", "y_taken", "chain", "init", "zero", "cleared")}

        def keys(t):
            if t == TILES - 1:
                return 0, KT, NKS
            first = max(0, t - KT + 1)
            return first, t - first + 1, (t - first + 1) * P

        def bcol(t):
            return 0 if t == TILES - 1 else (KT - keys(t)[1]) * P

        with nc.Block() as block:
            @block.sync
            def _(sp):
                sp.dma_start(tab[:, :], d["rel_bias"]).then_inc(s["tab"], 16)
                for b in range(3):
                    sp.dma_start(w[b][:, :, :], d["w_att"][0, b]).then_inc(s[f"w{b}"], 16)
                sp.dma_start(yb[:, 0:KD], d["x"][0:P, 0:KD]).then_inc(s["yb_free"], 16)
                sp.dma_start(kT[:, 0:KD], d["x"][0:P, 0:KD]).then_inc(s["kv_out"], 16)
                sp.wait_ge(s["tab8"], 4)
                sp.wait_ge(s["zero"], 1)
                sp.dma_start(d["table"], tab8[:, :]).then_inc(s["tab_out"], 16)
                sp.wait_ge(s["tab_out"], 16)
                for h in range(HB):
                    row = d["table"][h, 0:W]
                    src = bass.AP(row.tensor, row.offset, [[1, P], [1, W]])
                    sp.dma_start(d["toeplitz"][h], src).then_inc(s["toep"], 16)
                sp.wait_ge(s["toep"], 16 * HB)

                def load(p):
                    i = bass.ds(p, 1)
                    for e in range(2):
                        sp.dma_start(brev[:, e, :], d["toeplitz"][bass.ds(2 * p + e, 1)].rearrange("a p c -> (a p) c")).then_inc(s["bias"], 16)
                    sp.dma_start(kc[:, :], d["k_cache"][i].rearrange("a p c -> (a p) c")).then_inc(s["cache"], 16)
                    sp.dma_start(vc[:, :, :], d["v_cache"][i].rearrange("a p t c -> p (a t) c")).then_inc(s["cache"], 16)

                def clear(p):
                    n = TCH // PAIRS
                    dst = d["expert_out"].rearrange("(c p) n -> p c n", p=P)[:, bass.ds(n * p, n), :]
                    sp.dma_start(dst, zero[:, :].unsqueeze(1).to_broadcast([P, n, D])).then_inc(s["cleared"], 16)

                def weights(p):
                    for b in range(3):
                        sp.wait_ge(s["w_split"], 3 * p + b + 1)
                        sp.dma_start(w[b][:, :, :], d["w_att"][bass.ds(p + 1, 1), b].rearrange("a p k c -> p (a k) c")).then_inc(s[f"w{b}"], 16)

                def outputs(p):
                    i = bass.ds(p, 1)
                    sp.wait_ge(s["pj_taken"], JOBS * (p + 1) + 2)
                    sp.dma_start(d["kb_p"][i].rearrange("a p c -> (a p) c"), kT[:, PR - BAND:PR]).then_inc(s["kv_out"], 16)
                    sp.dma_start(d["kb_s"][i].rearrange("a p c -> (a p) c"), kT[:, PR:ROWS]).then_inc(s["kv_out"], 16)
                    nt = (PR - BAND) // P
                    sp.dma_start(d["vb_p"][i].rearrange("a p t c -> p (a t) c"), v[:, nt:TILES - 1, :]).then_inc(s["kv_out"], 16)
                    sp.dma_start(d["vb_s"][i].rearrange("a p c -> (a p) c"), v[0:SR, TILES - 1, :]).then_inc(s["kv_out"], 16)
                    sp.wait_ge(s["y_taken"], TILES * (p + 1) + 1)
                    sp.dma_start(d["yb"][i].rearrange("a p c -> (a p) c"), yb[:, :]).then_inc(s["yb_free"], 16)

                with sp.Fori(0, PAIRS - 1) as p:
                    load(p)
                    clear(p)
                    weights(p)
                    outputs(p)
                load(PAIRS - 1)
                clear(PAIRS - 1)
                outputs(PAIRS - 1)
                sp.wait_ge(s["kv_out"], 64 * PAIRS + 16)
                sp.wait_ge(s["cleared"], 16 * PAIRS)
                sp.wait_ge(s["yb_free"], 16 * (PAIRS + 1))

            @block.scalar
            def _(act):
                def pair(p):
                    act.wait_ge(s["y_taken"], TILES * p + 1)
                    act.wait_ge(s["kv_out"], 64 * p + 16)
                    for n in range(JOBS):
                        b, j = n // NJ, n % NJ
                        act.wait_ge(s["pj_ready"], JOBS * p + n + 1)
                        src = sc[n % 2]
                        if b < 3:
                            a = act.activation((qT, kT, vT)[b][:, j * NW:(j + 1) * NW], src[:, 0:NW], ACT.Copy)
                        elif j < NJ - 1:
                            a = act.activation(v[:, NJ * j:NJ * j + NJ, :],
                                               src[:, 0:NJ * P].rearrange("p (t n) -> p t n", n=P), ACT.Copy)
                        else:
                            act.activation(v[0:SR, TILES - 1, :], src[0:SR, 2 * P:3 * P], ACT.Copy)
                            a = act.activation(v[:, NJ * j:NJ * j + 2, :],
                                               src[:, 0:2 * P].rearrange("p (t n) -> p t n", n=P), ACT.Copy)
                        a.then_inc(s["pj_taken"], 1)
                    for i in range(UNITS + 1):
                        if i < UNITS:
                            nk = keys(i // 2)[2]
                            act.wait_ge(s["x_ready"], UNITS * p + i + 3)
                            act.activation(pr[i % 2][:, 0:nk], x[i % 2][:, 0:nk], ACT.Exp, scale=SCALE,
                                           bias=num[:, i % 4, 1:2],
                                           accum_out=num[:, i % 4, 2:3]).then_inc(s["p_ready"], 1)
                        if i >= 1:
                            t = (i - 1) // 2
                            n = keys(t)[1]
                            act.wait_ge(s["pt_ready"], UNITS * p + i)
                            act.wait_ge(s["pv_ready"], UNITS * p + i)
                            dst, src = pt[(i - 1) % 2], pst
                            if t < TILES - 1:
                                a = act.activation(dst[:, 0:n * P], src[:, 0:n * P], ACT.Copy)
                            else:
                                act.activation(dst[0:SR, BAND:W], src[0:SR, BAND:W], ACT.Copy)
                                a = act.activation(dst[:, 0:BAND], src[:, 0:BAND], ACT.Copy)
                            a.then_inc(s["pt_taken"], 1)

                act.wait_ge(s["init"], 1)
                with act.Fori(0, PAIRS) as p:
                    pair(p)

            @block.gpsimd
            def _(pool):
                def split(p, b):
                    pool.wait_ge(s[f"w{b}"], 16 * p + 16)
                    if not isinstance(p, int):
                        pool.wait_ge(s["pj_ready"], JOBS * (p - 1) + NJ * (b + 1))
                    hi, lo = (m[:, :, :] for m in w2[b])
                    pool.tensor_tensor(hi, w[b][:, :, :], c.ones(), ALU.mult).then_inc(s["w_high"], 1)
                    pool.wait_ge(s["w_high"], 3 * p + b + 1)
                    pool.tensor_tensor(lo, w[b][:, :, :], plain(hi), ALU.subtract).then_inc(s["w_split"], 1)

                for b in range(3):
                    split(0, b)
                with pool.Fori(1, PAIRS) as p:
                    for b in range(3):
                        split(p, b)

            @block.tensor
            def _(pe):
                def pair(p):
                    for n in range(JOBS):
                        b, j = n // NJ, n % NJ
                        if j == 0 and b < 3:
                            pe.wait_ge(s["w_split"], 3 * p + b + 1)
                        pe.wait_ge(s["pj_taken"], JOBS * p + n + 1)
                        if n < 2:
                            pe.wait_ge(s["x_ready"], UNITS * p + 2)
                        if b < 3:
                            for k in range(KD):
                                mm = split_matmul(pe, sc[n % 2][:, 0:NW], [m[:, k, :] for m in w2[b]],
                                                  c.h(k, j * NW, (j + 1) * NW), start=(k == 0), stop=(k == KD - 1))
                        else:
                            for t in range(NJ * j, NJ * j + NJ):
                                r = rows_of(t)
                                mm = pe.transpose(sc[n % 2][0:r, (t - NJ * j) * P:(t - NJ * j + 1) * P],
                                                  vT[:, t * P:t * P + r], c.consts[:, C_ID, :])
                        mm.then_inc(s["pj_ready"], 1)
                    pe.wait_ge(s["pj_taken"], JOBS * (p + 1) + 2)
                    pe.wait_ge(s["cache"], 32 * p + 32)

                    def scores(i):
                        t, e = i // 2, i % 2
                        lo, hi = e * DHB, e * DHB + DHB
                        first, n, nk = keys(t)
                        pe.wait_ge(s["x_ready"], UNITS * p + i + 1)
                        lhsT = qT[lo:hi, t * P:(t + 1) * P]
                        if t < TILES - 1:
                            pieces = [(0, min(nk, 512), kT[lo:hi, first * P:first * P + min(nk, 512)])]
                            if nk > 512:
                                pieces.append((512, nk, kT[lo:hi, first * P + 512:first * P + nk]))
                        else:
                            pieces = [(0, BAND, kc[lo:hi, :]), (BAND, NKS, kT[lo:hi, PR:ROWS])]
                        for a, b, rhs in pieces:
                            mm = pe.matmul(sc[i % 2][:, a:b], lhsT, rhs, start=True, stop=True)
                        mm.then_inc(s["sc_ready"], 1)

                    def turn(i):
                        t = i // 2
                        n = keys(t)[1]
                        pe.wait_ge(s["p_ready"], UNITS * p + i + 3)
                        pe.wait_ge(s["pt_taken"], UNITS * p + i + 1)
                        for k in range(n):
                            m = SR if t == TILES - 1 and k == n - 1 else P
                            tr = pe.transpose(pst[0:m, k * P:(k + 1) * P], pr[i % 2][:, k * P:k * P + m],
                                              c.consts[:, C_ID, :])
                        tr.then_inc(s["pt_ready"], 1)

                    def values(i):
                        t, e = i // 2, i % 2
                        first, n, _ = keys(t)
                        pe.wait_ge(s["pt_taken"], UNITS * p + i + 2)
                        if e == 0:
                            pe.wait_ge(s["o_taken"], TILES * p + t + 1)
                        cols = slice(e * DHB, e * DHB + DHB)
                        for k in range(n):
                            m = SR if t == TILES - 1 and k == n - 1 else P
                            if t < TILES - 1:
                                rhs = v[:, first + k, cols]
                            else:
                                rhs = vc[:, k, cols] if k < n - 1 else v[0:SR, TILES - 1, cols]
                            mm = pe.matmul(pso[:, cols], pt[i % 2][0:m, k * P:(k + 1) * P], rhs,
                                           start=(k == 0), stop=(k == n - 1))
                        mm.then_inc(s["pv_ready"], 1)

                    def turn_out(t):
                        pe.wait_ge(s["o_taken"], TILES * p + t + 2)
                        pe.wait_ge(s["y_taken"], TILES * p + t + 1)
                        pe.transpose(psy[:, 0:P], osb[t % 2][:, :], c.consts[:, C_ID, :]).then_inc(s["oT_ready"], 1)

                    for i in range(UNITS + 4):
                        if i < UNITS:
                            scores(i)
                        if 1 <= i <= UNITS:
                            turn(i - 1)
                        if 2 <= i < UNITS + 2:
                            values(i - 2)
                        if i >= 4 and i % 2 == 0:
                            turn_out((i - 4) // 2)

                pe.wait_ge(s["init"], 1)
                with pe.Fori(0, PAIRS) as p:
                    pair(p)

            @block.vector
            def _(dve):
                PER = 6 + 5 * TILES
                dve.memset(zero[:, :], 0.0).then_inc(s["zero"], 1)
                dve.wait_ge(s["tab"], 16)
                inv = 1.0 / SCALE
                end = FIRST + NREL
                for lo, hi, src in ((0, FIRST, tab[:, 0:1].to_broadcast([HB, FIRST])), (FIRST, end, tab[:, :]),
                                    (end, TAB, tab[:, NREL - 1:NREL].to_broadcast([HB, TAB - end]))):
                    dve.tensor_scalar(tab8[:, lo:hi], src, inv, None, ALU.mult).then_inc(s["tab8"], 1)
                dve.memset(qT[:, ROWS:PAD], 0.0).then_inc(s["tab8"], 1)
                for i, (n, k) in enumerate((("pj_taken", 2), ("x_ready", 2), ("p_ready", 2), ("pt_taken", 1),
                                            ("pv_ready", 2), ("o_taken", 1), ("y_taken", 1), ("init", 1))):
                    dve.memset(num[:, 1 + i // 4, i % 4:i % 4 + 1], 0.0).then_inc(s[n], k)

                def pair(p):
                    st = Chain(dve, s["chain"], PER * p)
                    dve.wait_ge(s["bias"], 32 * p + 32)
                    for e in range(2):
                        st.link(dve.tensor_copy(bias[:, e, :], brev[:, e, ::-1]))
                        st.mark(dve.memset(bias[CH:P, e, 0:CH], -1e30))
                        st.mark(dve.memset(bias[0:CH, e, W - CH:W], -1e30))
                    st.wait()

                    def softmax_in(i):
                        t, e = i // 2, i % 2
                        nk, b0 = keys(t)[2], bcol(t)
                        dve.wait_ge(s["p_ready"], UNITS * p + i + 1)
                        dve.wait_ge(s["sc_ready"], UNITS * p + i + 1)
                        st.mark(dve.memset(waits[:, :], 0.0))
                        st.link(dve.tensor_tensor_reduce(x[i % 2][:, 0:nk], sc[i % 2][:, 0:nk],
                                                         bias[:, e, b0:b0 + nk], 1.0, -3.0e38, ALU.add, ALU.max,
                                                         num[:, i % 4, 0:1]))
                        dve.tensor_scalar(num[:, i % 4, 1:2], num[:, i % 4, 0:1], -SCALE, None,
                                          ALU.mult).then_inc(s["x_ready"], 1)

                    def scale_out(t):
                        k = 2 * (t % 2)
                        dve.wait_ge(s["pv_ready"], UNITS * p + 2 * t + 4)
                        st.link(dve.reciprocal(num[:, k:k + 2, 3], num[:, k:k + 2, 2]))
                        dve.tensor_tensor(osb[t % 2][:, :].rearrange("p (e n) -> p e n", e=2),
                                          pso[:, 0:P].rearrange("p (e n) -> p e n", e=2),
                                          num[:, k:k + 2, 3].unsqueeze(2).to_broadcast([P, 2, DHB]),
                                          ALU.mult).then_inc(s["o_taken"], 1)

                    dve.wait_ge(s["yb_free"], 16 * p + 16)
                    for i in range(UNITS + 5):
                        if 4 <= i < UNITS + 4 and i % 2 == 0:
                            scale_out((i - 4) // 2)
                        if i < UNITS:
                            softmax_in(i)
                        if i >= 5 and i % 2 == 1:
                            t = (i - 5) // 2
                            r = rows_of(t)
                            dve.wait_ge(s["oT_ready"], TILES * p + t + 1)
                            dve.tensor_copy(yb[:, t * P:t * P + r], psy[:, 0:r]).then_inc(s["y_taken"], 1)
                    assert st.n == PER, st.n

                with dve.Fori(0, PAIRS) as p:
                    pair(p)


def phase_merge(nc, c):
    d = c.d
    RINGP = 3
    NUP = (HA, PAIRS)
    with ExitStack() as ctx:
        wg = [sb(nc, ctx, f"wg{q}", [P, KD, P]) for q in range(2)]
        wg2 = [[sb(nc, ctx, f"wg{q}_{n}", [P, KD, P], F32R) for n in ("high", "low")] for q in range(2)]
        wu = [sb(nc, ctx, f"wu{q}", [P, NUP[q], P]) for q in range(2)]
        y = [sb(nc, ctx, "yaT", [P, HA, ROWS]), sb(nc, ctx, "ybT", [P, PAIRS, ROWS])]
        sg = [sb(nc, ctx, f"sg{i}", [P, NW]) for i in range(RINGP)]
        m = [sb(nc, ctx, f"mA{j}", [P, NW]) for j in range(NJ)]
        ps = [[ctx.enter_context(nc.psum_tensor(f"pm{i}{q}", [P, 512], F32)) for q in range(2)] for i in range(RINGP)]
        wg_in, wu_in = ([c.sem(f"x_{n}{q}") for q in range(2)] for n in ("wg", "wu"))
        y_in = [[c.sem(f"x_y{q}{j}") for j in range(NJ)] for q in range(2)]
        w_high, w_split, g_ready, u_ready, sg_done, taken, chain, init = (c.sem("x_" + n) for n in (
            "whigh", "wsplit", "g", "u", "sg", "taken", "chain", "init"))
        with nc.Block() as block:
            @block.sync
            def _(sp):
                def gate(n, q):
                    src = d["w_gates"][n, q] if isinstance(n, int) else \
                        d["w_gates"][bass.ds(n, 1), q].rearrange("a p k c -> p (a k) c")
                    sp.dma_start(wg[q][:, :, :], src).then_inc(wg_in[q], 16)

                def up(n, q):
                    w = d[("w_up_a", "w_up_b")[q]]
                    src = w[n] if isinstance(n, int) else w[bass.ds(n, 1)].rearrange("a p k c -> p (a k) c")
                    sp.dma_start(wu[q][:, :, :], src).then_inc(wu_in[q], 16)

                gate(0, 0)
                up(0, 0)
                gate(0, 1)
                up(0, 1)
                for q in range(2):
                    for j in range(NJ):
                        cols = slice(j * NW, (j + 1) * NW)
                        sp.dma_start(y[q][:, :, cols], d[("ya", "yb")[q]].rearrange("h p r -> p h r")[:, :, cols]).then_inc(y_in[q][j], 16)
                with sp.Fori(1, KD) as n:
                    for q in range(2):
                        sp.wait_ge(w_split, 2 * n + q - 1)
                        gate(n, q)
                        sp.wait_ge(u_ready, NJ * (2 * n + q - 1))
                        up(n, q)

            @block.gpsimd
            def _(pool):
                def split(n, q):
                    pool.wait_ge(wg_in[q], 16 * n + 16)
                    if not isinstance(n, int):
                        pool.wait_ge(g_ready, NJ * (2 * n + q - 1))
                    hi, lo = (t[:, :, :] for t in wg2[q])
                    pool.tensor_tensor(hi, wg[q][:, :, :], c.ones(), ALU.mult).then_inc(w_high, 1)
                    pool.wait_ge(w_high, 2 * n + q + 1)
                    pool.tensor_tensor(lo, wg[q][:, :, :], plain(hi), ALU.subtract).then_inc(w_split, 1)

                for q in range(2):
                    split(0, q)
                with pool.Fori(1, KD) as n:
                    for q in range(2):
                        split(n, q)

            @block.tensor
            def _(pe):
                pe.wait_ge(init, 1)
                with pe.Fori(0, KD) as n:
                    for q in range(2):
                        pe.wait_ge(w_split, 2 * n + q + 1)
                        for j in range(NJ):
                            job = NJ * q + j
                            gate, up = ps[job % RINGP]
                            pe.wait_ge(taken, 2 * NJ * n + job + 1)
                            for k in range(KD):
                                mm = split_matmul(pe, gate[:, 0:NW], [t[:, k, :] for t in wg2[q]],
                                                  c.h(k, j * NW, (j + 1) * NW), start=(k == 0), stop=(k == KD - 1))
                            mm.then_inc(g_ready, 1)
                            if j == 0:
                                pe.wait_ge(wu_in[q], 16 * n + 16)
                            pe.wait_ge(y_in[q][j], 16)
                            for k in range(NUP[q]):
                                mm = pe.matmul(up[:, 0:NW], wu[q][:, k, :], y[q][:, k, j * NW:(j + 1) * NW],
                                               start=(k == 0), stop=(k == NUP[q] - 1))
                            mm.then_inc(u_ready, 1)

            @block.scalar
            def _(act):
                act.wait_ge(init, 1)
                with act.Fori(0, KD) as n:
                    for job in range(2 * NJ):
                        act.wait_ge(g_ready, 2 * NJ * n + job + 1)
                        act.wait_ge(taken, 2 * NJ * n + job + 1)
                        act.activation(sg[job % RINGP][:, :], ps[job % RINGP][0][:, 0:NW], ACT.Sigmoid).then_inc(sg_done, 1)

            @block.vector
            def _(dve):
                PER = NJ
                dve.memset(m[0][:, 0:1], 0.0).then_inc(taken, RINGP)
                dve.memset(m[1][:, 0:1], 0.0).then_inc(init, 1)
                with dve.Fori(0, KD) as n:
                    st = Chain(dve, chain, PER * n)
                    for q in range(2):
                        for j in range(NJ):
                            job = NJ * q + j
                            up, g = ps[job % RINGP][1][:, 0:NW], sg[job % RINGP][:, :]
                            dve.wait_ge(u_ready, 2 * NJ * n + job + 1)
                            dve.wait_ge(sg_done, 2 * NJ * n + job + 1)
                            dve.wait_ge(taken, 2 * NJ * n + job + RINGP)
                            if q == 0:
                                dve.tensor_tensor(m[j][:, :], up, g, ALU.mult).then_inc(taken, 1)
                            else:
                                st.link(dve.tensor_tensor(g, up, g, ALU.mult))
                                dve.tensor_tensor(c.mixT[:, bass.ds(n, 1), j * NW:(j + 1) * NW].rearrange("p a r -> p (a r)"),
                                                  m[j][:, :], g, ALU.add).then_inc(taken, 1)
                    assert st.n == PER, st.n


def phase_residual(nc, c):
    d = c.d
    NR = NG + NE
    with ExitStack() as ctx:
        def buf(name, shape):
            return sb(nc, ctx, name, shape)
        wo = buf("wo", [P, KD, D])
        h2T = [buf(f"h2T{i}", [P, KD, P]) for i in range(2)]
        wr = buf("wr", [P, KD, NR])
        br = buf("br", [P, NR])
        gt = buf("gt", [P, 3, 2, D])
        lng, lnb = buf("l1g", [P, D]), buf("l1b", [P, D])
        x0 = [buf(f"xr{i}", [P, D]) for i in range(2)]
        x1 = [buf(f"x1{i}", [P, D]) for i in range(2)]
        h2 = [buf(f"h2{i}", [P, D]) for i in range(2)]
        stats, mv = buf("stats1", [P, 12]), buf("mv1", [P, TILES, 2])
        std, rstd = buf("std1", [P, TILES]), buf("rstd1", [P, TILES])
        eps = buf("eps1", [P, 1])
        psy = [ctx.enter_context(nc.psum_tensor(f"py{i}", [P, 1024], F32)) for i in range(2)]
        pst = ctx.enter_context(nc.psum_tensor("pt_x1", [P, KD, P], F32))
        psr = ctx.enter_context(nc.psum_tensor("p_rt", [P, 512], F32))
        wo_in = [c.sem(f"r_wo{h}") for h in range(2)]
        x_in, x_out, h_out = ([c.sem(f"r_{n}{i}") for i in range(2)] for n in ("xin", "xout", "hout"))
        small, y_ready, var_ready, std_ready, x1_ready, h2_ready, xT, ha, hd, chain, rt, res, init, norm = (
            c.sem("r_" + n) for n in ("small", "y", "var", "std", "x1", "h2", "xT", "ha", "hd", "chain", "rt",
                                      "res", "init", "norm"))
        with nc.Block() as block:
            @block.sync
            def _(sp):
                def x_tile(t):
                    sp.dma_start(x0[t % 2][0:rows_of(t), :], d["x0"][t * P:t * P + rows_of(t), :]).then_inc(x_in[t % 2], 16)

                for h in range(2):
                    sp.dma_start(wo[:, :, h * 512:(h + 1) * 512], d["w_out"][:, :, h * 512:(h + 1) * 512]).then_inc(wo_in[h], 16)
                x_tile(0)
                rows = d["gate_rows"].rearrange("(g s k) c -> g s (k c)", g=4, s=2)
                for g in range(3):
                    for st in range(2):
                        sp.dma_start(gt[:, g, st, :], rows[g, st].partition_broadcast(P)).then_inc(small, 16)
                sp.dma_start(lng[:, :], d["ln1_g"].partition_broadcast(P)).then_inc(small, 16)
                sp.dma_start(lnb[:, :], d["ln1_b"].partition_broadcast(P)).then_inc(small, 16)
                sp.dma_start(wr[:, :, :], d["w_r"]).then_inc(small, 16)
                sp.dma_start(br[:, :], d["b_r"].partition_broadcast(P)).then_inc(small, 16)
                for t in range(TILES + 1):
                    if 1 <= t < TILES:
                        if t >= 2:
                            sp.wait_ge(res, t - 1)
                        x_tile(t)
                    if t >= 1:
                        u = t - 1
                        for ready, dst, src, out in ((x1_ready, d["x1"], x1, x_out), (h2_ready, d["h2"], h2, h_out)):
                            sp.wait_ge(ready, t)
                            sp.dma_start(dst[u * P:u * P + rows_of(u), :], src[u % 2][0:rows_of(u), :]).then_inc(out[u % 2], 16)
                for out in (x_out, h_out):
                    for i in range(2):
                        sp.wait_ge(out[i], 16 * ((TILES + 1 - i) // 2))

            @block.tensor
            def _(pe):
                def turn(t):
                    r = rows_of(t)
                    pe.wait_ge(h2_ready, t + 1)
                    if t >= 1:
                        pe.wait_ge(ha, t)
                        pe.wait_ge(hd, t)
                    for k in range(KD):
                        tr = pe.transpose(pst[:, k, 0:r], h2[t % 2][0:r, k * P:(k + 1) * P], c.consts[0:r, C_ID, 0:r])
                    tr.then_inc(xT, 1)

                def route(t):
                    r = rows_of(t)
                    pe.wait_ge(ha, t + 1)
                    pe.wait_ge(hd, t + 1)
                    pe.wait_ge(small, 16 * 10)
                    for k in range(KD):
                        mm = pe.matmul(psr[0:r, t * NR:(t + 1) * NR], h2T[t % 2][:, k, 0:r], wr[:, k, :],
                                       start=(k == 0), stop=(k == KD - 1))
                    mm.then_inc(rt, 1)

                for t in range(TILES):
                    r = rows_of(t)
                    if t >= 2:
                        pe.wait_ge(res, t - 1)
                    for h in range(2):
                        if t == 0:
                            pe.wait_ge(wo_in[h], 16)
                        for k in range(KD):
                            mm = pe.matmul(psy[t % 2][0:r, h * 512:(h + 1) * 512], c.mixT[:, k, t * P:t * P + r],
                                           wo[:, k, h * 512:(h + 1) * 512], start=(k == 0), stop=(k == KD - 1))
                    mm.then_inc(y_ready, 1)
                    if t >= 2:
                        route(t - 2)
                    if t >= 1:
                        turn(t - 1)
                route(TILES - 2)
                turn(TILES - 1)
                route(TILES - 1)

            @block.scalar
            def _(act):
                act.wait_ge(init, 1)
                for t in range(TILES + 1):
                    if t < TILES:
                        r = rows_of(t)
                        act.wait_ge(var_ready, t + 1)
                        act.activation(std[0:r, t:t + 1], mv[0:r, t, 1:2], ACT.Sqrt, bias=eps[0:r, :]).then_inc(std_ready, 1)
                    if t >= 1:
                        u = t - 1
                        r = rows_of(u)
                        act.wait_ge(xT, u + 1)
                        if u >= 2:
                            act.wait_ge(rt, u - 1)
                        act.activation(h2T[u % 2][:, 0:KD // 2, 0:r], pst[:, 0:KD // 2, 0:r], ACT.Copy).then_inc(ha, 1)

            @block.gpsimd
            def _(pool):
                pool.wait_ge(small, 16 * 10)
                for t in range(TILES):
                    r, s = rows_of(t), 0 if t < TILES - 1 else 1
                    pool.wait_ge(x1_ready, t + 1)
                    if t >= 2:
                        pool.wait_ge(h_out[t % 2], 16 * (t // 2))
                        pool.wait_ge(xT, t - 1)
                    pool.tensor_tensor(h2[t % 2][0:r, :], x1[t % 2][0:r, :], gt[0:r, 1, s, :], ALU.mult).then_inc(norm, 1)
                    pool.wait_ge(norm, t + 1)
                    pool.tensor_tensor(h2[t % 2][0:r, :], h2[t % 2][0:r, :], gt[0:r, 2, s, :], ALU.add).then_inc(h2_ready, 1)

            @block.vector
            def _(dve):
                st = Chain(dve, chain)
                dve.memset(eps[:, :], LN_EPS).then_inc(init, 1)
                st.link(dve.memset(c.lg[:, TILES - 1, :], 0.0))
                dve.wait_ge(small, 16 * 10)
                for t in range(TILES + 1):
                    if t < TILES:
                        r, s = rows_of(t), 0 if t < TILES - 1 else 1
                        xn = x1[t % 2]
                        dve.wait_ge(y_ready, t + 1)
                        if t >= 2:
                            dve.wait_ge(x_out[t % 2], 16 * (t // 2))
                            dve.wait_ge(norm, t - 1)
                        st.link(dve.tensor_tensor(xn[0:r, :], psy[t % 2][0:r, :], gt[0:r, 0, s, :], ALU.mult))
                        dve.wait_ge(x_in[t % 2], 16 * (t // 2 + 1))
                        dve.scalar_tensor_tensor(out=xn[0:r, :], in0=x0[t % 2][0:r, :], scalar=ALPHA, in1=xn[0:r, :],
                                                 op0=ALU.mult, op1=ALU.add).then_inc(res, 1)
                        dve.wait_ge(res, t + 1)
                        for i in range(2):
                            st.mark(dve.bn_stats(stats[0:r, i * 6:i * 6 + 6], xn[0:r, i * 512:(i + 1) * 512]))
                        st.wait()
                        dve.bn_aggr(mv[0:r, t, :], stats[0:r, :]).then_inc(var_ready, 1)
                        dve.wait_ge(std_ready, t + 1)
                        st.link(dve.reciprocal(rstd[0:r, t:t + 1], std[0:r, t:t + 1]))
                        dve.wait_ge(var_ready, t + 1)
                        st.link(dve.tensor_scalar(xn[0:r, :], xn[0:r, :], mv[0:r, t, 0:1], rstd[0:r, t:t + 1],
                                                  ALU.subtract, ALU.mult))
                        st.link(dve.tensor_tensor(xn[0:r, :], xn[0:r, :], lng[0:r, :], ALU.mult))
                        dve.tensor_tensor(xn[0:r, :], xn[0:r, :], lnb[0:r, :], ALU.add).then_inc(x1_ready, 1)
                    if t >= 1:
                        u = t - 1
                        ru = rows_of(u)
                        dve.wait_ge(xT, u + 1)
                        if u >= 2:
                            dve.wait_ge(rt, u - 1)
                        dve.tensor_copy(h2T[u % 2][:, KD // 2:KD, 0:ru], pst[:, KD // 2:KD, 0:ru]).then_inc(hd, 1)
                dve.wait_ge(rt, TILES)
                full = TILES - 1
                st.mark(dve.tensor_tensor(c.lg[:, 0:full, :], psr[:, 0:full * NR].rearrange("p (t n) -> p t n", n=NR),
                                          br[:, :].unsqueeze(1).to_broadcast([P, full, NR]), ALU.add))
                st.link(dve.tensor_tensor(c.lg[0:SR, full, :], psr[0:SR, full * NR:TILES * NR], br[0:SR, :], ALU.add))


def phase_dispatch(nc, c):
    d = c.d
    with ExitStack() as ctx:
        def buf(name, shape):
            return sb(nc, ctx, name, shape)
        z = [buf(f"z{i}", [P, TILES, 4]) for i in range(8)]
        z1 = [buf(f"zz{i}", [P, TILES]) for i in range(8)]
        M = [buf(f"pick{i}", [P, TILES, NE]) for i in range(2)]
        sel, cnt, tot = buf("sel", [P, TILES, NE]), buf("cnt", [P, TILES, NE]), buf("tot", [P, TILES, NE])
        pre = buf("pre", [P, TILES + 1, NE])
        cmp = buf("cmp", [P, NE, TILES])
        nch = buf("nch", [P, NE])
        end = [buf(f"end{i}", [P, NE]) for i in range(2)]
        thr = buf("thr", [P, TCH])
        slot = buf("slot", [P, TILES])
        cmp2 = buf("cmp2", [1, TCH, NE])
        tf = buf("tf", [1, NTAB])
        tg = buf("tg", [1, 4, TCH])
        rid = buf("rid", [P, TILES])
        zero = buf("zero", [TCH, P])
        rows_sb = buf("rows_sb", [TCH, P])
        psc = ctx.enter_context(nc.psum_tensor("psc", [P, 512], F32))
        pso = ctx.enter_context(nc.psum_tensor("ps_rows", [P, 512], F32))
        chain, e_in, e_out, sel_ready, cnt_ready, small, zero_out, slots, scat, rows_in, rows_T, zr = (
            c.sem("d_" + n) for n in ("chain", "ein", "eout", "sel", "cnt", "small", "zero", "slots", "scat",
                                      "rows", "rowsT", "zr"))
        with nc.Block() as block:
            @block.sync
            def _(sp):
                sp.dma_start(rid[:, :], d["row_id"]).then_inc(small, 16)
                sp.wait_ge(zr, 1)
                sp.dma_start(d["slot_rows"].rearrange("(c p) a -> c (p a)", p=P), zero[:, :]).then_inc(zero_out, 16)
                for e in range(RING):
                    sp.dma_start(c.wgu[:, e, :, :], d["w_gu"][e]).then_inc(c.w_in[e], 16)
                    sp.dma_start(c.wdn[:, e, :, :], d["w_dn"][e]).then_inc(c.w_in[e], 16)
                sp.wait_ge(scat, 16 * 2 * TILES)
                sp.dma_start(rows_sb[:, :], d["slot_rows"].rearrange("(c p) a -> c (p a)", p=P)).then_inc(rows_in, 16)

            @block.gpsimd
            def _(pool):
                pool.wait_ge(small, 16)
                pool.wait_ge(zero_out, 16)
                for j in range(2):
                    pool.wait_ge(slots, j + 1)
                    for t in range(TILES):
                        r = rows_of(t)
                        pool.indirect_dma_start(d["slot_rows"], bass.IndirectOffsetOnAxis(ap=c.slots[0:r, j, t:t + 1], axis=0),
                                                rid[0:r, t:t + 1], None).then_inc(scat, 16)

            @block.tensor
            def _(pe):
                pe.wait_ge(sel_ready, 1)
                rhs = flat2(sel[:, :, :])
                pe.matmul(psc[:, 0:TILES * NE], c.consts[:, C_SUM, :], rhs, start=True, stop=True)
                pe.matmul(psc[:, TILES * NE:2 * TILES * NE], c.consts[:, C_ONE, :], rhs, start=True,
                          stop=True).then_inc(cnt_ready, 1)
                pe.wait_ge(rows_in, 16)
                pe.transpose(pso[:, 0:TCH], rows_sb[:, :], c.consts[0:TCH, C_ID, 0:TCH]).then_inc(rows_T, 1)

            @block.scalar
            def _(act):
                act.wait_ge(e_in, 1)
                act.activation(z[1][:, :, :], z[0][:, :, :], ACT.Exp).then_inc(e_out, 1)
                act.wait_ge(e_in, 2)
                act.activation(z1[3][:, :], z1[2][:, :], ACT.Exp).then_inc(e_out, 1)

            @block.vector
            def _(dve):
                st = Chain(dve, chain)
                dve.memset(zero[:, :], 0.0).then_inc(zr, 1)
                lg = c.lg

                def each(col, n=4):
                    return col[:, :].unsqueeze(2).to_broadcast([P, TILES, n])

                def first_max(src, top, pick, seen):
                    st.link(dve.tensor_reduce(top[:, :], src, AX.X, ALU.max))
                    st.link(dve.tensor_tensor(pick[:, :, :], src, each(top), ALU.is_equal))
                    st.link(dve.tensor_copy(seen[:, :], pick[:, :, 0]))
                    for i in range(1, 4):
                        st.link(dve.tensor_tensor(pick[:, :, i], pick[:, :, i], seen[:, :], ALU.is_gt))
                        st.link(dve.tensor_tensor(seen[:, :], seen[:, :], pick[:, :, i], ALU.max))

                grp = lg[:, :, 0:NG]
                first_max(grp, z1[0], z[2], z1[1])
                dve.tensor_tensor(z[0][:, :, :], grp, each(z1[0]), ALU.subtract).then_inc(e_in, 1)
                le = [lg[:, :, NG + 4 * g:NG + 4 * g + 4] for g in range(NG)]
                pick = [z[2][:, :, g].unsqueeze(2).to_broadcast([P, TILES, 4]) for g in range(NG)]
                st.link(dve.tensor_tensor(z[3][:, :, :], le[0], pick[0], ALU.mult))
                for g in range(1, NG):
                    st.link(dve.tensor_tensor(z[4][:, :, :], le[g], pick[g], ALU.mult))
                    st.link(dve.tensor_tensor(z[3][:, :, :], z[3][:, :, :], z[4][:, :, :], ALU.add))
                first_max(z[3][:, :, :], z1[4], z[5], z1[1])
                st.link(dve.scalar_tensor_tensor(out=flat2(z[4][:, :, :]), in0=flat2(z[5][:, :, :]), scalar=-1e30,
                                                 in1=flat2(z[3][:, :, :]), op0=ALU.mult, op1=ALU.add))
                first_max(z[4][:, :, :], z1[5], z[6], z1[1])
                dve.tensor_tensor(z1[2][:, :], z1[5][:, :], z1[4][:, :], ALU.subtract).then_inc(e_in, 1)
                for j in range(2):
                    for g in range(NG):
                        st.mark(dve.tensor_tensor(M[j][:, :, 4 * g:4 * g + 4], z[5 + j][:, :, :], pick[g], ALU.mult))
                st.wait()
                st.link(dve.tensor_tensor(sel[:, :, :], M[0][:, :, :], M[1][:, :, :], ALU.add))
                dve.tensor_tensor(sel[:, :, :], sel[:, :, :],
                                  c.consts[:, C_VAL, 0:TILES].unsqueeze(2).to_broadcast([P, TILES, NE]),
                                  ALU.mult).then_inc(sel_ready, 1)
                st.mark(dve.memset(pre[:, 0, :], 0.0))
                st.mark(dve.tensor_scalar(thr[:, 0:TILES], c.consts[:, C_IOTA, 0:TILES], float(P), None, ALU.mult))
                dve.wait_ge(cnt_ready, 1)
                n = TILES * NE
                st.link(dve.tensor_copy(flat2(tot[:, :, :]), psc[:, n:2 * n]))
                for t in range(TILES):
                    st.link(dve.tensor_tensor(pre[:, t + 1, :], pre[:, t, :], tot[:, t, :], ALU.add))
                st.mark(dve.tensor_tensor(flat2(cnt[:, :, :]), psc[:, 0:n], flat2(pre[:, 0:TILES, :]), ALU.add))
                st.link(dve.tensor_tensor(cmp[:, :, :], pre[:, TILES, :].unsqueeze(2).to_broadcast([P, NE, TILES]),
                                          thr[:, 0:TILES].unsqueeze(1).to_broadcast([P, NE, TILES]), ALU.is_gt))
                st.link(dve.tensor_reduce(nch[:, :], cmp[:, :, :], AX.X, ALU.add))
                src = nch
                for i, k in enumerate((1, 2, 4, 8)):
                    dst = end[i % 2]
                    st.mark(dve.tensor_copy(dst[:, 0:k], src[:, 0:k]))
                    st.link(dve.tensor_tensor(dst[:, k:NE], src[:, k:NE], src[:, 0:NE - k], ALU.add))
                    src = dst
                ends = src
                first = end[0] if ends is end[1] else end[1]
                st.link(dve.tensor_tensor(first[:, :], ends[:, :], nch[:, :], ALU.subtract))
                st.link(dve.tensor_scalar(first[:, :], first[:, :], float(P), None, ALU.mult))
                st.link(dve.tensor_tensor(cnt[:, :, :], cnt[:, :, :], first[:, :].unsqueeze(1).to_broadcast([P, TILES, NE]), ALU.add))
                for j in range(2):
                    st.link(dve.tensor_tensor(M[j][:, :, :], M[j][:, :, :], cnt[:, :, :], ALU.mult))
                    st.link(dve.tensor_reduce(slot[:, :], M[j][:, :, :], AX.X, ALU.add))
                    dve.tensor_copy(c.slots[:, j, :], slot[:, :]).then_inc(slots, 1)
                    dve.wait_ge(slots, j + 1)
                iota = c.consts[0:1, C_IOTA, 0:TCH]
                st.link(dve.tensor_tensor(cmp2[:, :, :], iota.unsqueeze(2).to_broadcast([1, TCH, NE]),
                                          ends[0:1, :].unsqueeze(1).to_broadcast([1, TCH, NE]), ALU.is_ge))
                ex = tf[:, TAB_E:TAB_E + TCH]
                st.link(dve.tensor_reduce(ex, cmp2[:, :, :], AX.X, ALU.add))
                st.link(dve.tensor_scalar(ex, ex, float(NE - 1), None, ALU.min))
                for i in range(1, NE // RING):
                    st.link(dve.tensor_scalar(tg[:, i, :], ex, float(RING * i), -float(RING), ALU.is_ge, ALU.mult))
                src = ex
                for i in range(1, NE // RING):
                    st.link(dve.tensor_tensor(tf[:, TAB_S:TAB_S + TCH], src, tg[:, i, :], ALU.add))
                    src = tf[:, TAB_S:TAB_S + TCH]
                st.mark(dve.tensor_copy(tf[:, TAB_END:TAB_END + NE], ends[0:1, :]))
                st.link(dve.tensor_scalar(tg[:, 0, :], iota, 2.0, None, ALU.mult))
                st.link(dve.tensor_tensor(tg[:, 0, :], ends[0:1, NE - 1:NE].to_broadcast([1, TCH]), tg[:, 0, :], ALU.is_gt))
                st.link(dve.tensor_reduce(tf[:, TAB_N:TAB_N + 1], tg[:, 0, :], AX.X, ALU.add))
                st.mark(dve.tensor_copy(c.table[:, :], tf[:, :]))
                dve.wait_ge(e_out, 2)
                st.mark(dve.tensor_reduce(z1[6][:, :], z[1][:, :, :], AX.X, ALU.add))
                st.link(dve.tensor_scalar(z1[7][:, :], z1[3][:, :], 1.0, None, ALU.add))
                st.link(dve.tensor_tensor(z1[6][:, :], z1[6][:, :], z1[7][:, :], ALU.mult))
                st.link(dve.reciprocal(c.gw[:, 0, :], z1[6][:, :]))
                st.link(dve.tensor_tensor(c.gw[:, 1, :], c.gw[:, 0, :], z1[3][:, :], ALU.mult))
                dve.wait_ge(rows_T, 1)
                st.link(dve.tensor_copy(c.rows[:, :], pso[:, 0:TCH]))


def phase_experts(nc, c):
    d = c.d
    with ExitStack() as ctx:
        def pair(name, shape):
            return [sb(nc, ctx, f"{name}{i}", shape) for i in range(2)]
        xg, xgT, ab, sg = pair("xg", [P, D]), pair("xgT", [P, KD, P]), pair("ab", [P, DE]), pair("sgx", [P, DE])
        aT, ob = pair("aTx", [P, DE // P, P]), pair("ob", [P, D])
        waits = sb(nc, ctx, "wait_cell", [P, 2])
        idx = [ctx.enter_context(nc.sbuf_tensor(f"idx{i}", [P, 1], mybir.dt.int32)) for i in range(2)]
        psT = ctx.enter_context(nc.psum_tensor("psT", [P, KD, P], F32))
        psU = [ctx.enter_context(nc.psum_tensor(f"psU{i}", [P, 512], F32)) for i in range(2)]
        psA = ctx.enter_context(nc.psum_tensor("psA", [P, 512], F32))
        psD = ctx.enter_context(nc.psum_tensor("psD", [P, 1024], F32))
        g_in, o_out = [c.sem(f"e_g{i}") for i in range(2)], [c.sem(f"e_o{i}") for i in range(2)]
        (idx_ready, xT, xTa, xTd, up, sgd, a, aTt, aTs, dn, oa, od, experts_ready, init, pdone) = (
            c.sem("e_" + n) for n in ("idx", "xT", "xTa", "xTd", "up", "sg", "a", "aT", "aTs", "dn", "oa", "od",
                                      "ready", "init", "pool"))

        def turns(eng):
            return eng.value_load(c.table[0:1, TAB_N:TAB_N + 1], min_val=1, max_val=MAXCH // 2)

        def walk(eng, turn, first, turn2, second):
            turn(0, 0, 0)
            first(0, 0)
            turn(1, 1, 0)
            with eng.Fori(0, turns(eng)) as n:
                first(2 * n + 1, 1)
                turn2(2 * n, 0)
                turn(2 * n + 2, 0, n + 1)
                second(2 * n, 0, n)
                first(2 * n + 2, 0)
                turn2(2 * n + 1, 1)
                turn(2 * n + 3, 1, n + 1)
                second(2 * n + 1, 1, n)

        def nothing(*_):
            pass

        with nc.Block() as block:
            @block.sync
            def _(sp):
                def arrived(e, k):
                    sp.wait_ge(c.w_in[e], k)
                    sp.nop().then_inc(experts_ready, 1)

                for e in range(RING - 1):
                    arrived(e, 32)
                with sp.Fori(1, NE // RING) as m:
                    for e in range(RING):
                        last = sp.value_load(c.table[0:1, bass.ds(RING * m + (e - RING + TAB_END), 1)], min_val=0, max_val=MAXCH)
                        sp.wait_ge(dn, last + 2)
                        i = bass.ds(RING * m + e, 1)
                        sp.dma_start(c.wgu[:, e, :, :], d["w_gu"][i].rearrange("a p k c -> p (a k) c")).then_inc(c.w_in[e], 16)
                        sp.dma_start(c.wdn[:, e, :, :], d["w_dn"][i].rearrange("a p k c -> p (a k) c")).then_inc(c.w_in[e], 16)
                        if e == 0:
                            arrived(RING - 1, 32 * m)
                        else:
                            arrived(e - 1, 32 * m + 32)
                arrived(RING - 1, 32 * (NE // RING))

            @block.gpsimd
            def _(pool):
                pool.wait_ge(init, 1)

                def gather(n, b, k):
                    if not isinstance(n, int) or n > 0:
                        pool.wait_ge(pdone, n)
                    pool.wait_ge(idx_ready, n + 1)
                    pool.tensor_tensor(waits[:, 0:1], waits[:, 1:2], waits[:, 1:2], ALU.add).then_inc(pdone, 1)
                    pool.indirect_dma_start(xg[b][:, :], None, d["h2"],
                                            bass.IndirectOffsetOnAxis(ap=idx[b][:, 0:1], axis=0)).then_inc(g_in[b], 16)

                walk(pool, gather, nothing, nothing, nothing)

            @block.tensor
            def _(pe):
                pe.wait_ge(init, 1)

                def turn(n, b, k):
                    pe.wait_ge(g_in[b], 16 * k + 16)
                    pe.wait_ge(xTa, n + 1)
                    pe.wait_ge(xTd, n + 1)
                    for i in range(KD):
                        tr = pe.transpose(psT[:, i, :], xg[b][:, i * P:(i + 1) * P], c.consts[:, C_ID, :])
                    tr.then_inc(xT, 1)

                def first(n, b):
                    e = pe.value_load(c.table[0:1, bass.ds(n + TAB_E, 1)], min_val=0, max_val=NE - 1)
                    place = pe.value_load(c.table[0:1, bass.ds(n + TAB_S, 1)], min_val=0, max_val=RING - 1)
                    pe.wait_ge(experts_ready, e + 1)
                    pe.wait_ge(a, n + 1)
                    pe.wait_ge(xTa, n + 2)
                    pe.wait_ge(xTd, n + 2)
                    for i in range(KD):
                        mm = pe.matmul(psU[b][:, :], xgT[b][:, i, :], c.wgu[:, bass.ds(place, 1), i, :].rearrange("p a c -> p (a c)"),
                                       start=(i == 0), stop=(i == KD - 1))
                    mm.then_inc(up, 1)

                def turn2(n, b):
                    pe.wait_ge(a, n + 3)
                    pe.wait_ge(aTs, n + 1)
                    for i in range(DE // P):
                        tr = pe.transpose(psA[:, i * P:(i + 1) * P], ab[b][:, i * P:(i + 1) * P], c.consts[:, C_ID, :])
                    tr.then_inc(aTt, 1)

                def second(n, b, k):
                    place = pe.value_load(c.table[0:1, bass.ds(n + TAB_S, 1)], min_val=0, max_val=RING - 1)
                    pe.wait_ge(aTs, n + 2)
                    pe.wait_ge(oa, n + 1)
                    pe.wait_ge(od, n + 1)
                    for h in range(2):
                        for i in range(DE // P):
                            mm = pe.matmul(psD[:, h * 512:(h + 1) * 512], aT[b][:, i, :],
                                           c.wdn[:, bass.ds(place, 1), i, h * 512:(h + 1) * 512].rearrange("p a c -> p (a c)"),
                                           start=(i == 0), stop=(i == DE // P - 1))
                    mm.then_inc(dn, 1)

                walk(pe, turn, first, turn2, second)

            @block.scalar
            def _(act):
                for b in range(2):
                    act.dma_start(ob[b][:, 0:KD], d["x1"][0:P, 0:KD]).then_inc(o_out[b], 16)
                act.wait_ge(init, 1)

                def turn(n, b, k):
                    act.wait_ge(xT, n + 3)
                    act.wait_ge(up, n + 1)
                    act.activation(xgT[b][:, 0:KD // 2, :], psT[:, 0:KD // 2, :], ACT.Copy).then_inc(xTa, 1)

                def first(n, b):
                    act.wait_ge(up, n + 3)
                    act.wait_ge(a, n + 1)
                    act.activation(sg[b][:, :], psU[b][:, 0:DE], ACT.Silu).then_inc(sgd, 1)

                def turn2(n, b):
                    act.wait_ge(aTt, n + 3)
                    act.wait_ge(dn, n + 1)
                    act.activation(flat2(aT[b][:, :, :]), psA[:, 0:DE], ACT.Copy).then_inc(aTs, 1)

                def second(n, b, k):
                    act.wait_ge(dn, n + 3)
                    act.wait_ge(o_out[b], 16 * k + 16)
                    act.activation(ob[b][:, 0:512], psD[:, 0:512], ACT.Copy).then_inc(oa, 1)
                    act.wait_ge(oa, n + 2)
                    act.wait_ge(od, n + 2)
                    act.dma_start(d["expert_out"].rearrange("(c p) n -> c p n", p=P)[bass.ds(n, 1)].rearrange("a p n -> (a p) n"),
                                  ob[b][:, :]).then_inc(o_out[b], 16)

                walk(act, turn, first, turn2, second)
                last = act.value_load(c.table[0:1, TAB_N:TAB_N + 1], min_val=1, max_val=MAXCH // 2)
                for b in range(2):
                    act.wait_ge(o_out[b], 16 * last + 16)
                    act.activation(ob[b][0:1, 0:1], ob[b][0:1, 0:1], ACT.Copy)

            @block.vector
            def _(dve):
                for sem, n in ((xT, 2), (xTa, 1), (xTd, 1), (up, 2), (a, 2), (aTt, 2), (aTs, 1), (dn, 2), (oa, 1), (od, 1)):
                    dve.nop().then_inc(sem, n)

                def index(n, b):
                    dve.wait_ge(xT, n + 1)
                    dve.tensor_copy(idx[b][:, :], c.rows[:, bass.ds(n, 1)]).then_inc(idx_ready, 1)

                dve.memset(waits[:, :], 0.0).then_inc(init, 1)
                index(0, 0)
                index(1, 1)

                def turn(n, b, k):
                    dve.wait_ge(xT, n + 3)
                    dve.wait_ge(up, n + 1)
                    dve.tensor_copy(xgT[b][:, KD // 2:KD, :], psT[:, KD // 2:KD, :]).then_inc(xTd, 1)
                    index(n + 2, b)

                def first(n, b):
                    dve.wait_ge(sgd, n + 1)
                    dve.wait_ge(aTt, n + 1)
                    dve.tensor_tensor(ab[b][:, :], psU[b][:, DE:2 * DE], sg[b][:, :], ALU.mult).then_inc(a, 1)

                def second(n, b, k):
                    dve.wait_ge(dn, n + 3)
                    dve.wait_ge(o_out[b], 16 * k + 16)
                    dve.tensor_copy(ob[b][:, 512:1024], psD[:, 512:1024]).then_inc(od, 1)

                walk(dve, turn, first, nothing, second)


def phase_final(nc, c):
    d = c.d
    NX = 4
    with ExitStack() as ctx:
        def buf(name, shape):
            return sb(nc, ctx, name, shape)
        gt = buf("gt2", [P, 2, D])
        lng, lnb = buf("l2g", [P, D]), buf("l2b", [P, D])
        x1 = [buf(f"xf{i}", [P, D]) for i in range(NX)]
        eo = [[buf(f"eo{i}{j}", [P, D]) for j in range(2)] for i in range(NX)]
        stats, mv = buf("stats2", [P, 12]), buf("mv2", [P, TILES, 2])
        std, rstd, eps = buf("std2", [P, TILES]), buf("rstd2", [P, TILES]), buf("eps2", [P, 2])
        x_in, y_out, e_in = ([c.sem(f"f_{n}{i}") for i in range(NX)] for n in ("xin", "yout", "ein"))
        small, e_scaled, var_ready, std_ready, norm, gained, y_ready, chain, init, e_used = (c.sem("f_" + n) for n in (
            "small", "escaled", "var", "std", "norm", "gained", "y", "chain", "init", "eused"))
        with nc.Block() as block:
            @block.sync
            def _(sp):
                def load(t):
                    sp.dma_start(x1[t % NX][0:rows_of(t), :], d["x1"][t * P:t * P + rows_of(t), :]).then_inc(x_in[t % NX], 16)

                load(0)
                rows = d["gate_rows"].rearrange("(g s k) c -> g s (k c)", g=4, s=2)
                for st in range(2):
                    sp.dma_start(gt[:, st, :], rows[3, st].partition_broadcast(P)).then_inc(small, 16)
                sp.dma_start(lng[:, :], d["ln2_g"].partition_broadcast(P)).then_inc(small, 16)
                sp.dma_start(lnb[:, :], d["ln2_b"].partition_broadcast(P)).then_inc(small, 16)
                for t in range(1, NX):
                    load(t)
                for t in range(TILES):
                    sp.wait_ge(y_ready, t + 1)
                    sp.dma_start(d["y"][t * P:t * P + rows_of(t), :], x1[t % NX][0:rows_of(t), :]).then_inc(y_out[t % NX], 16)
                    n = t - 1 + NX
                    if NX <= n < TILES:
                        sp.wait_ge(y_out[n % NX], 16 * (n // NX))
                        load(n)
                for i, q in enumerate(y_out):
                    sp.wait_ge(q, 16 * len(range(i, TILES, NX)))

            @block.gpsimd
            def _(pool):
                def gather(t):
                    r = rows_of(t)
                    if t >= NX:
                        pool.wait_ge(e_used, t - NX + 1)
                    for j in range(2):
                        pool.indirect_dma_start(eo[t % NX][j][0:r, :], None, d["expert_out"],
                                                bass.IndirectOffsetOnAxis(ap=c.slots[0:r, j, t:t + 1], axis=0)).then_inc(e_in[t % NX], 16)

                for t in range(NX):
                    gather(t)
                pool.wait_ge(small, 64)
                for t in range(TILES):
                    r, xn = rows_of(t), x1[t % NX]
                    if t + NX < TILES:
                        gather(t + NX)
                    pool.wait_ge(gained, t + 1)
                    pool.tensor_tensor(xn[0:r, :], xn[0:r, :], lnb[0:r, :], ALU.add).then_inc(y_ready, 1)

            @block.scalar
            def _(act):
                act.wait_ge(init, 2)
                for t in range(-1, TILES):
                    if t + 1 < TILES:
                        u = t + 1
                        r, e1 = rows_of(u), eo[u % NX][0]
                        act.wait_ge(e_in[u % NX], 32 * (u // NX + 1))
                        act.activation(e1[0:r, :], e1[0:r, :], ACT.Identity, bias=eps[0:r, 1:2],
                                       scale=c.gw[0:r, 0, u:u + 1]).then_inc(e_scaled, 1)
                    if t >= 0:
                        r = rows_of(t)
                        act.wait_ge(var_ready, t + 1)
                        act.activation(std[0:r, t:t + 1], mv[0:r, t, 1:2], ACT.Sqrt, bias=eps[0:r, 0:1]).then_inc(std_ready, 1)

            @block.vector
            def _(dve):
                st = Chain(dve, chain)
                dve.memset(eps[:, 0:1], LN_EPS).then_inc(init, 1)
                dve.memset(eps[:, 1:2], 0.0).then_inc(init, 1)
                dve.wait_ge(small, 64)
                for t in range(TILES + 1):
                    if t < TILES:
                        r, s, xn = rows_of(t), 0 if t < TILES - 1 else 1, x1[t % NX]
                        e1, e2 = eo[t % NX]
                        dve.wait_ge(e_in[t % NX], 32 * (t // NX + 1))
                        dve.wait_ge(e_scaled, t + 1)
                        st.link(dve.scalar_tensor_tensor(out=e1[0:r, :], in0=e2[0:r, :], scalar=c.gw[0:r, 1, t:t + 1],
                                                         in1=e1[0:r, :], op0=ALU.mult, op1=ALU.add))
                        st.link(dve.tensor_tensor(e1[0:r, :], e1[0:r, :], gt[0:r, s, :], ALU.mult))
                        dve.wait_ge(x_in[t % NX], 16 * (t // NX + 1))
                        dve.scalar_tensor_tensor(out=xn[0:r, :], in0=xn[0:r, :], scalar=ALPHA, in1=e1[0:r, :],
                                                 op0=ALU.mult, op1=ALU.add).then_inc(e_used, 1)
                        dve.wait_ge(e_used, t + 1)
                        for i in range(2):
                            st.mark(dve.bn_stats(stats[0:r, i * 6:i * 6 + 6], xn[0:r, i * 512:(i + 1) * 512]))
                        st.wait()
                        dve.bn_aggr(mv[0:r, t, :], stats[0:r, :]).then_inc(var_ready, 1)
                    if t >= 1:
                        u = t - 1
                        r, xn = rows_of(u), x1[u % NX]
                        dve.wait_ge(std_ready, u + 1)
                        dve.wait_ge(var_ready, u + 1)
                        st.link(dve.reciprocal(rstd[0:r, u:u + 1], std[0:r, u:u + 1]))
                        dve.tensor_scalar(xn[0:r, :], xn[0:r, :], mv[0:r, u, 0:1], rstd[0:r, u:u + 1],
                                          ALU.subtract, ALU.mult).then_inc(norm, 1)
                        dve.wait_ge(norm, u + 1)
                        dve.tensor_tensor(xn[0:r, :], xn[0:r, :], lng[0:r, :], ALU.mult).then_inc(gained, 1)


def constants():
    r, col = np.arange(P)[:, None], np.arange(P)[None, :]
    same, blk = r // CH == col // CH, r // 16 == col // 16
    k = np.zeros((P, NCONST, P), np.float32)
    k[:, C_ID] = r == col
    k[:, C_CUM] = same & (r <= col)
    k[:, C_ONE] = 1.0
    k[:, C_NEG] = np.where(same & (r <= col), 0.0, -30000.0)
    k[:, C_M16] = blk & (col < r)
    k[:, C_MOFF] = same & ~blk & (col < r)
    k[:, C_CH0] = (r < CH) & (col >= 0)
    k[:, C_CH1] = (r >= CH) & (col >= 0)
    k[:, C_BLK] = same
    k[:, C_VAL, 0:TILES] = 1.0
    k[SR:, C_VAL, TILES - 1] = 0.0
    k[:, C_SUM] = r < col
    k[:, C_IOTA] = col + 0 * r
    return k


def layout(i):
    a = {k: np.asarray(v) for k, v in i.items()}
    w_in = a["w_in"][0]
    kpc = lambda m, *shape: m.reshape((KD, P) + shape)
    o = {}
    o["x"] = np.concatenate([a["x_prompt"][0], a["x_sample"][0]], 0)
    o["cT"] = np.stack([a["c_prompt"][0].reshape(KD, P), a["c_sample"][0].reshape(KD, P)], 2).transpose(1, 0, 2)
    o["consts"] = constants()
    o["w_mod"] = kpc(a["w_mod"][0], 12, 512).transpose(2, 1, 0, 3)
    o["b_mod"] = a["b_mod"][0]
    o["a_dt"] = np.stack([a["a_log"][0], a["dt_bias"][0]])
    o["ln_in_g"], o["ln_in_b"] = a["ln_in_g"], a["ln_in_b"]
    o["w_ba"] = kpc(w_in[:, 4096:4112], 16).transpose(1, 0, 2)
    o["w_gdn"] = kpc(w_in[:, :4096], 4, HA, P).transpose(3, 2, 1, 0, 4)
    o["conv_w"] = a["conv_w"][0].reshape(CW, 3, HA, P).transpose(3, 2, 1, 0)
    o["conv_state"] = a["state_conv_a"][0, 0].reshape(CW - 1, 3, HA, P).transpose(3, 2, 1, 0)
    o["norm_w"] = a["gdn_norm_w"][0].reshape(P, 1)
    o["state"] = a["state_gdn"][0, 0]
    o["rel_bias"] = a["rel_bias"][0]
    o["w_att"] = kpc(w_in[:, 4112:5648], 3, PAIRS, P).transpose(3, 2, 1, 0, 4)
    o["k_cache"] = a["cache_k_b"][0, 0].reshape(BAND, PAIRS, P).transpose(1, 2, 0)
    o["v_cache"] = a["cache_v_b"][0, 0].reshape(BAND // P, P, PAIRS, P).transpose(2, 1, 0, 3)
    o["w_gates"] = kpc(w_in[:, 5648:], 2, KD, P).transpose(3, 2, 1, 0, 4)
    for n in ("w_up_a", "w_up_b"):
        o[n] = a[n][0].reshape(-1, P, KD, P).transpose(2, 1, 0, 3)
    o["w_out"] = kpc(a["w_out"][0], D).transpose(1, 0, 2)
    for n in ("ln1_g", "ln1_b", "ln2_g", "ln2_b"):
        o[n] = a[n][0]
    o["w_r"] = kpc(np.concatenate([a["w_rg"][0], a["w_re"][0]], 1), NG + NE).transpose(1, 0, 2)
    o["b_r"] = np.concatenate([a["b_rg"][0], a["b_re"][0]])
    gu = np.concatenate([a["w_gate_e"][0], a["w_up_e"][0]], 2)
    o["w_gu"] = gu.reshape(NE, KD, P, 2 * DE).transpose(0, 2, 1, 3)
    o["row_id"] = np.arange(PAD, dtype=np.float32).reshape(TILES, P).T
    o["w_dn"] = a["w_down_e"][0].reshape(NE, DE // P, P, D).transpose(0, 2, 1, 3)
    return {k: np.ascontiguousarray(v) for k, v in o.items()}


SCRATCH = {"gate_rows": (8 * KD, P), "x0": (ROWS, D), "ya": (HA, P, ROWS), "yb": (PAIRS, P, ROWS),
           "table": (HB, 768), "toeplitz": (HB, P, KT * P), "x1": (ROWS, D), "h2": (ROWS, D), "slot_rows": (TCH * P, 1),
           "expert_out": (TCH * P, D)}
OUTPUTS = {"gdn_p": (HA, P, P), "gdn_s": (HA, P, P), "tail": (P, HA, 3, 6), "kb_p": (PAIRS, P, BAND),
           "kb_s": (PAIRS, P, SR), "vb_p": (PAIRS, P, BAND // P, P), "vb_s": (PAIRS, SR, P), "y": (ROWS, D)}



def build(nc, d):
    with ExitStack() as ctx:
        c = Core(nc, ctx, d)
        c.consts = sb(nc, ctx, "consts", [P, NCONST, P])
        c.adt = sb(nc, ctx, "adt", [P, 2, HA])
        c.one = sb(nc, ctx, "one", [P, 1])
        c.lg = sb(nc, ctx, "logits", [P, TILES, NG + NE])
        c.gw = sb(nc, ctx, "expert_weights", [P, 2, TILES])
        c.slots = ctx.enter_context(nc.sbuf_tensor("slots", [P, 2, TILES], mybir.dt.int32))
        c.rows = sb(nc, ctx, "slot_row_cols", [P, TCH])
        c.table = ctx.enter_context(nc.sbuf_tensor("table", [1, NTAB], mybir.dt.int32))
        with ExitStack() as mixers:
            c.hT = [sb(nc, mixers, f"hT_{n}", [P, KD, ROWS], F32R) for n in ("high", "low")]
            with ExitStack() as part:
                c.tok = sb(nc, part, "tok", [P, HA, NQ, TILES])
                c.tail = sb(nc, part, "tail", [P, HA, 3, 6])
                c.run(phase_entry)
                c.run(phase_deltanet)
                c.run(phase_attention)
            with ExitStack() as part:
                c.mixT = sb(nc, part, "mixT", [P, KD, ROWS])
                c.run(phase_merge)
                c.run(phase_residual)
        with ExitStack() as part:
            c.wgu = sb(nc, part, "wgu", [P, RING, KD, 2 * DE])
            c.wdn = sb(nc, part, "wdn", [P, RING, DE // P, D])
            c.w_in = [ctx.enter_context(nc.semaphore(f"w_in{i}")) for i in range(RING)]
            c.run(phase_dispatch)
            c.run(phase_experts)
        phase_final(nc, c)


def kernel(**inputs):
    import concourse.bacc as bacc
    from concourse.bass_utils import run_bass_kernel_spmd

    arrays = layout(inputs)
    nc = bacc.Bacc("TRN2", target_bir_lowering=False, num_devices=1)
    d = {n: nc.dram_tensor("in_" + n, a.shape, F32, kind="ExternalInput").ap() for n, a in arrays.items()}
    for n, shape in SCRATCH.items():
        d[n] = nc.dram_tensor("tmp_" + n, shape, F32, kind=SCRATCH_KIND).ap()
    for n, shape in OUTPUTS.items():
        d[n] = nc.dram_tensor("out_" + n, shape, F32, kind="ExternalOutput").ap()
    build(nc, d)
    r = run_bass_kernel_spmd(nc, [{"in_" + n: a for n, a in arrays.items()}], core_ids=[0]).results[0]
    y = r["out_y"]
    tail = r["out_tail"].transpose(3, 2, 1, 0).reshape(2, CW - 1, 3 * HA * P)
    kp = r["out_kb_p"].transpose(2, 0, 1).reshape(1, 1, BAND, HB, DHB)
    ks = r["out_kb_s"].transpose(2, 0, 1).reshape(1, 1, SR, HB, DHB)
    vp = r["out_vb_p"].transpose(2, 1, 0, 3).reshape(1, 1, BAND, HB, DHB)
    vs = r["out_vb_s"].transpose(1, 0, 2).reshape(1, 1, SR, HB, DHB)
    return (y[None, :PR], y[None, PR:], tail[None, None, 0], tail[None, None, 1],
            r["out_gdn_p"][None, None], r["out_gdn_s"][None, None], kp, ks, vp, vs)


SCRATCH_KIND = "Internal"
```
